# Optimizing a Trainium2 kernel written in Bass

```python
import math
import jax, jax.numpy as jnp
from jax import lax
import numpy as np

D_MODEL = 1024
BATCH = 1
SEQ = 512
DEPTH = 2

GRID_W = 64
NA_HEADS = 8
NA_HEAD_DIM = 64
NA_WIN_ROWS = 8
NA_WIN_COLS = 16
NA_W = NA_HEADS * NA_HEAD_DIM
RET_HEADS = 4
RET_QK_DIM = 128
RET_V_DIM = 256
RET_CHUNK = 128
RET_QK_W = RET_HEADS * RET_QK_DIM
RET_V_W = RET_HEADS * RET_V_DIM
ROPE_BASE = 10000.0
IN_SIZES = (NA_W, NA_W, NA_W, RET_QK_W, RET_QK_W, RET_V_W, RET_V_W, D_MODEL, D_MODEL)
IN_SPLITS = tuple(int(s) for s in np.cumsum(IN_SIZES)[:-1])
D_IN = int(sum(IN_SIZES))
D_FF = 2816
CONV_W = 3
PLE_DIM = 256
LN_EPS = 1e-5
GN_EPS = 1e-6
DEEPNORM_ALPHA = (2.0 * DEPTH) ** 0.25
DEEPNORM_BETA = (8.0 * DEPTH) ** -0.25


def layer_norm(x, g, b):
    xf = x.astype(jnp.float32)
    mu = jnp.mean(xf, axis=-1, keepdims=True)
    var = jnp.mean(jnp.square(xf - mu), axis=-1, keepdims=True)
    y = (xf - mu) * lax.rsqrt(var + LN_EPS) * g.astype(jnp.float32) + b.astype(jnp.float32)
    return y.astype(x.dtype)

def rotary(x, pos):
    half = x.shape[-1] // 2
    inv = ROPE_BASE ** (-jnp.arange(half, dtype=jnp.float32) / half)
    ang = pos[:, None] * inv[None, :]
    cos, sin = jnp.cos(ang), jnp.sin(ang)
    x1, x2 = x[..., :half].astype(jnp.float32), x[..., half:].astype(jnp.float32)
    return jnp.concatenate([x1 * cos - x2 * sin, x2 * cos + x1 * sin], axis=-1).astype(x.dtype)

def neighbourhood_attention(q, k, v, rpb):
    B, T, H, dh = q.shape
    rows = T // GRID_W
    wr = min(NA_WIN_ROWS, rows)
    scale = dh ** -0.5
    q_g = q.reshape(B, rows, GRID_W, H, dh).transpose(1, 0, 3, 2, 4)
    k_g = k.reshape(B, rows, GRID_W, H, dh).transpose(0, 3, 1, 2, 4)
    v_g = v.reshape(B, rows, GRID_W, H, dh).transpose(0, 3, 1, 2, 4)
    cols = np.arange(GRID_W)
    col_start = np.clip(cols - NA_WIN_COLS // 2, 0, GRID_W - NA_WIN_COLS)
    col_idx = col_start[:, None] + np.arange(NA_WIN_COLS)[None, :]
    col_off = col_idx - cols[:, None] + (NA_WIN_COLS - 1)

    def row_step(args):
        r, q_row = args
        rs = jnp.clip(r - wr // 2, 0, rows - wr)
        k_rows = lax.dynamic_slice_in_dim(k_g, rs, wr, axis=2)
        v_rows = lax.dynamic_slice_in_dim(v_g, rs, wr, axis=2)
        k_win = jnp.take(k_rows, col_idx, axis=3)
        v_win = jnp.take(v_rows, col_idx, axis=3)
        s = jnp.einsum('bhcd,bhrckd->bhcrk', q_row, k_win).astype(jnp.float32) * scale
        row_off = rs + jnp.arange(wr) - r + (NA_WIN_ROWS - 1)
        bias = jnp.take(rpb[:, row_off], col_off, axis=2)
        s = s + bias.transpose(0, 2, 1, 3)[None].astype(jnp.float32)
        pr = jax.nn.softmax(s.reshape(B, H, GRID_W, wr * NA_WIN_COLS), axis=-1)
        pr = pr.reshape(B, H, GRID_W, wr, NA_WIN_COLS).astype(v.dtype)
        return jnp.einsum('bhcrk,bhrckd->bhcd', pr, v_win)

    out = lax.map(row_step, (jnp.arange(rows), q_g))
    return out.transpose(1, 0, 3, 2, 4).reshape(B, T, H * dh)

def retention_dir(q, k, v, gamma, include_diag):
    B, H, T, dk = q.shape
    dv = v.shape[-1]
    C = RET_CHUNK
    n = T // C
    qc = q.reshape(B, H, n, C, dk)
    kc = k.reshape(B, H, n, C, dk)
    vc = v.reshape(B, H, n, C, dv)
    log_g = jnp.log(gamma)
    i = np.arange(C)
    diff = i[:, None] - i[None, :]
    mask = (diff >= 0) if include_diag else (diff > 0)
    dpos = np.maximum(diff, 0).astype(np.float32)
    decay_in = jnp.where(mask[None], jnp.exp(log_g[:, None, None] * dpos[None]), 0.0)
    s = jnp.einsum('bhnid,bhnjd->bhnij', qc, kc) * decay_in[None, :, None]
    inner = jnp.einsum('bhnij,bhnje->bhnie', s, vc)
    zeta = jnp.exp(log_g[:, None] * (C - 1 - i).astype(np.float32))
    xi = jnp.exp(log_g[:, None] * (i + 1).astype(np.float32))
    chunk_decay = jnp.exp(log_g * C)
    kv = jnp.einsum('bhnjd,bhnje->nbhde', kc * zeta[None, :, None, :, None], vc)

    def body(S, kv_c):
        return S * chunk_decay[None, :, None, None] + kv_c, S

    S0 = jnp.zeros((B, H, dk, dv), kv.dtype)
    _, S_prev = lax.scan(body, S0, kv)
    cross = jnp.einsum('bhnid,nbhde->bhnie', qc, S_prev) * xi[None, :, None, :, None]
    return (inner + cross).reshape(B, H, T, dv)

def bidirectional_retention(q, k, v, g, decay_f, decay_b):
    B, T, H, dk = q.shape
    pos = jnp.arange(T, dtype=jnp.float32)
    qh = rotary(q.transpose(0, 2, 1, 3), pos)
    kh = rotary(k.transpose(0, 2, 1, 3), pos) * (dk ** -0.5)
    vh = v.reshape(B, T, H, RET_V_DIM).transpose(0, 2, 1, 3)
    gam_f = jax.nn.sigmoid(decay_f.astype(jnp.float32))
    gam_b = jax.nn.sigmoid(decay_b.astype(jnp.float32))
    fwd = retention_dir(qh, kh, vh, gam_f, True)
    bwd = jnp.flip(retention_dir(jnp.flip(qh, 2), jnp.flip(kh, 2), jnp.flip(vh, 2), gam_b, False), 2)
    o = (fwd + bwd).astype(jnp.float32)
    mu = jnp.mean(o, axis=-1, keepdims=True)
    var = jnp.mean(jnp.square(o - mu), axis=-1, keepdims=True)
    o = ((o - mu) * lax.rsqrt(var + GN_EPS)).astype(v.dtype)
    o = o.transpose(0, 2, 1, 3).reshape(B, T, H * RET_V_DIM)
    return jax.nn.silu(g) * o

def conv_glu_ffn(x, w_up, conv_w, conv_b, w_down):
    h = x @ w_up
    hp = jnp.pad(h, ((0, 0), (1, 1), (0, 0)))
    h = hp[:, :-2] * conv_w[0] + hp[:, 1:-1] * conv_w[1] + hp[:, 2:] * conv_w[2] + conv_b
    a, b = jnp.split(h, 2, axis=-1)
    return (jax.nn.gelu(a) * b) @ w_down

def first_inputs(seed: int = 0) -> dict:
    key = jax.random.key(seed)
    ks = jax.random.split(key, 20)
    f32 = jnp.float32
    nrm = lambda k, shape: jax.random.normal(k, shape, f32)
    beta = DEEPNORM_BETA
    col_scale = np.ones((D_IN,), np.float32)
    col_scale[2 * NA_W:3 * NA_W] = beta
    v0 = 3 * NA_W + 2 * RET_QK_W
    col_scale[v0:v0 + RET_V_W] = beta
    gam = 1.0 - 2.0 ** (-5.0 - np.arange(RET_HEADS))
    base_logit = jnp.asarray(np.log(gam / (1.0 - gam)), f32)
    return {
        "x": nrm(ks[0], (BATCH, SEQ, D_MODEL)),
        "p": nrm(ks[1], (DEPTH, BATCH, SEQ, PLE_DIM)),
        "w_in": nrm(ks[2], (DEPTH, D_MODEL, D_IN)) * (D_MODEL ** -0.5) * jnp.asarray(col_scale),
        "na_rpb": 0.02 * nrm(ks[3], (DEPTH, NA_HEADS, 2 * NA_WIN_ROWS - 1, 2 * NA_WIN_COLS - 1)),
        "ret_decay_f": base_logit + 0.01 * nrm(ks[4], (DEPTH, RET_HEADS)),
        "ret_decay_b": base_logit + 0.01 * nrm(ks[5], (DEPTH, RET_HEADS)),
        "w_branch_a": nrm(ks[6], (DEPTH, NA_W, D_MODEL)) * (NA_W ** -0.5) * beta,
        "w_branch_b": nrm(ks[7], (DEPTH, RET_V_W, D_MODEL)) * (RET_V_W ** -0.5) * beta,
        "w_out": nrm(ks[8], (DEPTH, D_MODEL, D_MODEL)) * (D_MODEL ** -0.5) * beta,
        "ln1_g": 1.0 + 0.02 * nrm(ks[9], (DEPTH, D_MODEL)),
        "ln1_b": 0.02 * nrm(ks[10], (DEPTH, D_MODEL)),
        "w_up": nrm(ks[11], (DEPTH, D_MODEL, 2 * D_FF)) * (D_MODEL ** -0.5) * beta,
        "conv_w": nrm(ks[12], (DEPTH, CONV_W, 2 * D_FF)) * (CONV_W ** -0.5),
        "conv_b": 0.02 * nrm(ks[13], (DEPTH, 2 * D_FF)),
        "w_down": nrm(ks[14], (DEPTH, D_FF, D_MODEL)) * (D_FF ** -0.5) * beta,
        "w_ple_gate": nrm(ks[15], (DEPTH, D_MODEL, D_MODEL)) * (D_MODEL ** -0.5),
        "w_ple_proj": nrm(ks[16], (DEPTH, PLE_DIM, D_MODEL)) * (PLE_DIM ** -0.5) * beta,
        "ln2_g": 1.0 + 0.02 * nrm(ks[17], (DEPTH, D_MODEL)),
        "ln2_b": 0.02 * nrm(ks[18], (DEPTH, D_MODEL)),
    }

def first_block(x, p, w_in, na_rpb, ret_decay_f, ret_decay_b, w_branch_a, w_branch_b, w_out,
              ln1_g, ln1_b, w_up, conv_w, conv_b, w_down, w_ple_gate, w_ple_proj, ln2_g, ln2_b):
    B, T, _ = x.shape
    for i in range(DEPTH):
        proj = x @ w_in[i]
        q_na, k_na, v_na, q_r, k_r, v_r, g_r, gate_a, gate_b = jnp.split(proj, IN_SPLITS, axis=-1)
        ya = neighbourhood_attention(q_na.reshape(B, T, NA_HEADS, NA_HEAD_DIM),
                                     k_na.reshape(B, T, NA_HEADS, NA_HEAD_DIM),
                                     v_na.reshape(B, T, NA_HEADS, NA_HEAD_DIM), na_rpb[i])
        yb = bidirectional_retention(q_r.reshape(B, T, RET_HEADS, RET_QK_DIM),
                                     k_r.reshape(B, T, RET_HEADS, RET_QK_DIM),
                                     v_r, g_r, ret_decay_f[i], ret_decay_b[i])
        merged = jax.nn.sigmoid(gate_a) * (ya @ w_branch_a[i]) + jax.nn.sigmoid(gate_b) * (yb @ w_branch_b[i])
        y = merged @ w_out[i]
        x = layer_norm(DEEPNORM_ALPHA * x + y, ln1_g[i], ln1_b[i])
        ffn = conv_glu_ffn(x, w_up[i], conv_w[i], conv_b[i], w_down[i])
        ple = jax.nn.sigmoid(x @ w_ple_gate[i]) * (p[i] @ w_ple_proj[i])
        x = layer_norm(DEEPNORM_ALPHA * x + ffn + ple, ln2_g[i], ln2_b[i])
    return x


DEPTH_2 = 1

D_MIX = D_MODEL
D_POOL = D_MIX // 2
D_SSM = D_MIX - D_POOL
POOL_WINDOWS = (2, 4, 8, 16)
N_POOL_GROUPS = len(POOL_WINDOWS)
POOL_GROUP = D_POOL // N_POOL_GROUPS
SSM_GROUP = 16
N_SSM_GROUPS = D_SSM // SSM_GROUP
SSM_STATE = 64
D_FF_2 = -(-8 * D_MODEL // (3 * 256)) * 256
RMS_EPS = 1e-6
DT_MIN = 1e-3
DT_MAX = 1e-1


def rmsnorm(x, g):
    xf = x.astype(jnp.float32)
    y = xf * lax.rsqrt(jnp.mean(xf * xf, axis=-1, keepdims=True) + RMS_EPS)
    return y.astype(x.dtype) * g

def pool_mixer(u, w_pool, scale):
    b, l, _ = u.shape
    ug = u.astype(jnp.float32).reshape(b, l, N_POOL_GROUPS, POOL_GROUP)
    cs = jnp.cumsum(ug, axis=1)
    n_pos = jnp.arange(1, l + 1, dtype=jnp.float32)
    diffs = []
    for gi, w in enumerate(POOL_WINDOWS):
        c = cs[:, :, gi]
        lagged = jnp.pad(c, ((0, 0), (w, 0), (0, 0)))[:, :l]
        mean = (c - lagged) / jnp.minimum(n_pos, float(w))[None, :, None]
        diffs.append(mean - ug[:, :, gi])
    d = jnp.stack(diffs, axis=2)
    y = jnp.einsum('blgc,gcd->blgd', d, w_pool.astype(jnp.float32)).reshape(b, l, D_POOL)
    return (y * scale.astype(jnp.float32)).astype(u.dtype)

def _complex_affine_combine(e1, e2):
    a1r, a1i, b1r, b1i = e1
    a2r, a2i, b2r, b2i = e2
    ar = a2r * a1r - a2i * a1i
    ai = a2r * a1i + a2i * a1r
    br = a2r * b1r - a2i * b1i + b2r
    bi = a2r * b1i + a2i * b1r + b2i
    return ar, ai, br, bi

def ssm_mixer(u, lam_re, lam_im, log_dt, b_re, b_im, c_re, c_im, d_skip, w_glu, b_glu):
    f32 = jnp.float32
    bsz, l, _ = u.shape
    ug = u.astype(f32).reshape(bsz, l, N_SSM_GROUPS, SSM_GROUP)
    lr, li = lam_re.astype(f32), lam_im.astype(f32)
    dt = jnp.exp(log_dt.astype(f32))[:, None]
    mag = jnp.exp(lr * dt)
    abar_r = mag * jnp.cos(li * dt)
    abar_i = mag * jnp.sin(li * dt)
    den = lr * lr + li * li
    nr, ni = abar_r - 1.0, abar_i
    coef_r = (nr * lr + ni * li) / den
    coef_i = (ni * lr - nr * li) / den
    br, bi = b_re.astype(f32), b_im.astype(f32)
    bbar_r = coef_r[..., None] * br - coef_i[..., None] * bi
    bbar_i = coef_r[..., None] * bi + coef_i[..., None] * br
    bu_r = jnp.einsum('blgh,gph->blgp', ug, bbar_r)
    bu_i = jnp.einsum('blgh,gph->blgp', ug, bbar_i)
    a_r = jnp.broadcast_to(abar_r, (1, l, N_SSM_GROUPS, SSM_STATE))
    a_i = jnp.broadcast_to(abar_i, (1, l, N_SSM_GROUPS, SSM_STATE))
    _, _, s_r, s_i = lax.associative_scan(_complex_affine_combine, (a_r, a_i, bu_r, bu_i), axis=1)
    y = (jnp.einsum('blgp,ghp->blgh', s_r, c_re.astype(f32))
         - jnp.einsum('blgp,ghp->blgh', s_i, c_im.astype(f32))
         + d_skip.astype(f32) * ug).reshape(bsz, l, D_SSM)
    y = jax.nn.gelu(y)
    y = y * jax.nn.sigmoid(y @ w_glu.astype(f32) + b_glu.astype(f32))
    return y.astype(u.dtype)

def swiglu(h, w_gate, w_up, w_down):
    return (jax.nn.silu(h @ w_gate) * (h @ w_up)) @ w_down

def second_inputs(seed: int = 0) -> dict:
    key = jax.random.key(seed)
    ks = jax.random.split(key, 24)
    f32 = jnp.float32
    nrm = lambda k, s, sc: jax.random.normal(k, s, f32) * sc
    res_scale = (2 * DEPTH_2) ** -0.5
    n_idx = jnp.arange(SSM_STATE, dtype=f32)
    lam_re = -0.5 + nrm(ks[5], (DEPTH_2, N_SSM_GROUPS, SSM_STATE), 0.01)
    lam_im = math.pi * n_idx[None, None, :] + nrm(ks[6], (DEPTH_2, N_SSM_GROUPS, SSM_STATE), 0.01)
    log_dt = jax.random.uniform(ks[7], (DEPTH_2, N_SSM_GROUPS), f32, math.log(DT_MIN), math.log(DT_MAX))
    return {
        "x": nrm(ks[0], (BATCH, SEQ, D_MODEL), 1.0),
        "norm_mix": 1.0 + nrm(ks[1], (DEPTH_2, D_MODEL), 0.02),
        "w_in": nrm(ks[2], (DEPTH_2, D_MODEL, D_MIX), D_MODEL ** -0.5),
        "w_pool": nrm(ks[3], (DEPTH_2, N_POOL_GROUPS, POOL_GROUP, POOL_GROUP), POOL_GROUP ** -0.5),
        "pool_scale": 1.0 + nrm(ks[4], (DEPTH_2, D_POOL), 0.02),
        "lam_re": lam_re,
        "lam_im": lam_im,
        "log_dt": log_dt,
        "b_re": nrm(ks[8], (DEPTH_2, N_SSM_GROUPS, SSM_STATE, SSM_GROUP), (2 * SSM_GROUP) ** -0.5),
        "b_im": nrm(ks[9], (DEPTH_2, N_SSM_GROUPS, SSM_STATE, SSM_GROUP), (2 * SSM_GROUP) ** -0.5),
        "c_re": nrm(ks[10], (DEPTH_2, N_SSM_GROUPS, SSM_GROUP, SSM_STATE), (2 * SSM_STATE) ** -0.5),
        "c_im": nrm(ks[11], (DEPTH_2, N_SSM_GROUPS, SSM_GROUP, SSM_STATE), (2 * SSM_STATE) ** -0.5),
        "d_skip": nrm(ks[12], (DEPTH_2, N_SSM_GROUPS, SSM_GROUP), 1.0),
        "w_glu": nrm(ks[13], (DEPTH_2, D_SSM, D_SSM), D_SSM ** -0.5),
        "b_glu": nrm(ks[14], (DEPTH_2, D_SSM), 0.01),
        "w_out": nrm(ks[15], (DEPTH_2, D_MIX, D_MODEL), D_MIX ** -0.5 * res_scale),
        "norm_ffn": 1.0 + nrm(ks[16], (DEPTH_2, D_MODEL), 0.02),
        "w_gate": nrm(ks[17], (DEPTH_2, D_MODEL, D_FF_2), D_MODEL ** -0.5),
        "w_up": nrm(ks[18], (DEPTH_2, D_MODEL, D_FF_2), D_MODEL ** -0.5),
        "w_down": nrm(ks[19], (DEPTH_2, D_FF_2, D_MODEL), D_FF_2 ** -0.5 * res_scale),
        "norm_final": 1.0 + nrm(ks[20], (D_MODEL,), 0.02),
    }

def second_block(x, norm_mix, w_in, w_pool, pool_scale, lam_re, lam_im, log_dt, b_re, b_im,
              c_re, c_im, d_skip, w_glu, b_glu, w_out, norm_ffn, w_gate, w_up, w_down,
              norm_final):
    h = x
    for i in range(DEPTH_2):
        u = rmsnorm(h, norm_mix[i]) @ w_in[i]
        u_pool, u_ssm = u[..., :D_POOL], u[..., D_POOL:]
        y_pool = pool_mixer(u_pool, w_pool[i], pool_scale[i])
        y_ssm = ssm_mixer(u_ssm, lam_re[i], lam_im[i], log_dt[i], b_re[i], b_im[i],
                          c_re[i], c_im[i], d_skip[i], w_glu[i], b_glu[i])
        h = h + jnp.concatenate([y_pool, y_ssm], axis=-1) @ w_out[i]
        h = h + swiglu(rmsnorm(h, norm_ffn[i]), w_gate[i], w_up[i], w_down[i])
    return rmsnorm(h, norm_final)


def setup_inputs(seed=0):
    out = dict(first_inputs(seed))
    for name, value in second_inputs(seed + 1).items():
        if name != "x":
            out[name + "_2"] = value
    return out


def reference(
    x, p, w_in, na_rpb, ret_decay_f, ret_decay_b, w_branch_a, w_branch_b, w_out, ln1_g, ln1_b,
    w_up, conv_w, conv_b, w_down, w_ple_gate, w_ple_proj, ln2_g, ln2_b, norm_mix_2, w_in_2,
    w_pool_2, pool_scale_2, lam_re_2, lam_im_2, log_dt_2, b_re_2, b_im_2, c_re_2, c_im_2,
    d_skip_2, w_glu_2, b_glu_2, w_out_2, norm_ffn_2, w_gate_2, w_up_2, w_down_2, norm_final_2,
):
    x = first_block(
        x, p, w_in, na_rpb, ret_decay_f, ret_decay_b, w_branch_a, w_branch_b, w_out, ln1_g,
        ln1_b, w_up, conv_w, conv_b, w_down, w_ple_gate, w_ple_proj, ln2_g, ln2_b,
    )
    return second_block(
        x, norm_mix_2, w_in_2, w_pool_2, pool_scale_2, lam_re_2, lam_im_2, log_dt_2, b_re_2,
        b_im_2, c_re_2, c_im_2, d_skip_2, w_glu_2, b_glu_2, w_out_2, norm_ffn_2, w_gate_2,
        w_up_2, w_down_2, norm_final_2,
    )


_drawn_inputs = setup_inputs


def setup_inputs(seed=0):
    import zlib

    import numpy as np

    out = dict(_drawn_inputs(seed))
    spreads = {}
    factors = {'na_rpb': 48.0,
     'ret_decay_b': 21.408,
     'w_branch_a': 5.518,
     'conv_b': 8.0,
     'norm_mix_2': 6.115,
     'pool_scale_2': 6.814,
     'lam_re_2': 64.0,
     'lam_im_2': 42.6,
     'log_dt_2': 43.52,
     'b_re_2': 60.344,
     'b_im_2': 60.392,
     'c_re_2': 59.288,
     'c_im_2': 59.08,
     'b_glu_2': 200.0,
     'norm_ffn_2': 16.581,
     'norm_final_2': 22.443,
     'ret_decay_f': 23.848,
     'ln1_b': 8.0,
     'ln2_b': 8.0}
    for name, (base, spread) in spreads.items():
        noise = np.random.default_rng([zlib.crc32(name.encode()), seed]).standard_normal(out[name].shape)
        drawn = base * np.exp(spread * noise) if base else spread * noise
        out[name] = __import__('jax').numpy.asarray(drawn.astype(out[name].dtype))
    for name, factor in factors.items():
        out[name] = (out[name] * factor).astype(out[name].dtype)
    return out
```

```python
import concourse.bass as bass
from concourse import mybir
from contextlib import ExitStack

F32 = mybir.dt.float32
F32R = mybir.dt.float32r
ALU = mybir.AluOpType
ACT = mybir.ActivationFunctionType

P = 128
T = 512
D = 1024
KT = D // P
DEPTH = 2
GRID_W, ROWS, WIN_ROWS, WIN_COLS = 64, 8, 8, 16
NA_HEADS, NA_DH = 8, 64
CB = GRID_W // 16
RET_H, RET_DK, RET_DV = 4, 128, 256
FF = 2816
FT = FF // P
PLE_T = 2
ALPHA = (2.0 * DEPTH) ** 0.25
LN_EPS, GN_EPS, RMS_EPS = 1e-5, 1e-6, 1e-6
RING = 4
UT = 8

ATT_U, BR_U, OUT_U, PLE_U, UP_U, DOWN_U = 4 * 12, 2 * 8, 8, 10, 2 * FT, FT
ATT0 = 0
BR0 = ATT0 + ATT_U
OUT0 = BR0 + BR_U
PLE0 = OUT0 + OUT_U
UP0 = PLE0 + PLE_U
DOWN0 = UP0 + UP_U
LAYER_U = DOWN0 + DOWN_U
ATT_R0 = 0
BR_R0 = ATT_R0 + 48
OUT_R0 = BR_R0 + 20
PLE_R0 = OUT_R0 + 8
UP_R0 = PLE_R0 + 16
DOWN_R0 = UP_R0 + 44
LAYER_R = DOWN_R0 + 8
BR_M0 = 0
PLE_M0 = BR_M0 + 4
DOWN_M0 = PLE_M0 + 6
LAYER_M = DOWN_M0 + 6
MIX = DEPTH
MIN_U0, GLU_U0, MOUT_U0, GU_U0 = 0, 8, 10, 18
MDOWN_U0 = GU_U0 + UP_U
MIX_U = MDOWN_U0 + DOWN_U
MIN_R0, GLU_R0, MOUT_R0, GU_R0 = 0, 8, 12, 20
MDOWN_R0 = GU_R0 + UP_U
GLU_M0, MDOWN_M0 = 0, 2
N_UNITS = DEPTH * LAYER_U + MIX_U
MIX_LOADS = 5
V_READ = 4 * 6
WINDOWS = (2, 4, 8, 16)
SP_T = 4
SG, SCH, SN = 32, 16, 64
ST = SG * SN // P
BT = 8
NB = T // BT
LAM = SP_T * SN + ST
NORM_C, POOLS_C, SKIP_C, BGLU_C, HALF_C, QUART_C, INV_C = 0, 24, 28, 32, 36, 38, 42
MPAR = INV_C + SP_T * 16
TWO_PI = 6.283185307179586
TWO_PI_HI = 6.28125
TWO_PI_MID = 0.0019350051879882812
TWO_PI_LO = TWO_PI - TWO_PI_HI - TWO_PI_MID
ROUND = 1.5 * 2.0 ** 23
SIN_MAX = 3.1415925


def build(nc, a, out):
    ctx = ExitStack()
    with ctx:
        at = [nc.sbuf_base]

        def place(name, shape, dt=F32, offset=None):
            size = 4
            for s in shape[1:]:
                size *= s
            if offset is None:
                offset, at[0] = at[0], at[0] + (size + 31) // 32 * 32
            return nc.alloc_sbuf_tensor_at(name, shape, dt, offset=offset)

        def sem(name):
            return ctx.enter_context(nc.semaphore(name))

        at[0] = (at[0] + 31) // 32 * 32
        stage = [place(f"stage{i}", [P, UT, P]) for i in range(RING)]
        w_hi = [place(f"w_hi{i}", [P, UT, P], F32R) for i in range(RING)]
        w_lo = [place(f"w_lo{i}", [P, UT, P], F32R) for i in range(RING)]
        xh = place("xh", [P, KT, T], F32R)
        xl = place("xl", [P, KT, T], F32R)
        z_at = at[0]
        z = place("z", [P, KT, T])
        ident = place("ident", [P, P])
        swap = place("swap", [P, P])
        mean_w = place("mean_w", [P, P])
        ln_eps = place("ln_eps", [P, 1])
        gn_eps = place("gn_eps", [P, 1])
        lnp = place("lnp", [P, DEPTH, 4, KT])
        convp = place("convp", [P, DEPTH, 4, 2 * FT])
        decay = place("decay", [P, 2, DEPTH * RET_H])
        decay_a = place("decay_a", [P, 2 * DEPTH * RET_H])
        decay_b = place("decay_b", [P, 2 * DEPTH * RET_H])
        at[0] = (at[0] + 31) // 32 * 32
        c_at = at[0]
        rope = place("rope", [P, 2, T])
        delta = place("delta", [P, 7 * P])
        masks = place("masks", [P, 3, 3 * P])
        conv_a = [place(f"conv_a{i}", [P, T], offset=c_at + 2048 * i) for i in range(2)]
        conv_b = [place(f"conv_b{i}", [P, T], offset=c_at + 4096 + 2048 * i) for i in range(2)]
        a_at = at[0]
        gates = place("gates", [P, 16, T])
        merged_p = place("merged_p", [P, 16, T], F32R, offset=a_at)
        yb = place("yb", [P, KT, T])
        yb_lo = place("yb_lo", [P, KT, T], F32R, offset=a_at + 32768)
        ya = place("ya", [P, 4, T])
        ya_lo = place("ya_lo", [P, 4, T], F32R, offset=a_at + 49152)
        tmp_at = at[0]
        yb_hi = place("yb_hi", [P, KT, T], F32R)
        ya_hi = place("ya_hi", [P, 4, T], F32R)
        p_at = at[0]
        p_raw = place("p_raw", [P, PLE_T, T])
        p_hi = place("p_hi", [P, PLE_T, T], F32R, offset=a_at)
        p_lo = place("p_lo", [P, PLE_T, T], F32R, offset=a_at + 4096)
        s_t = place("s_t", [P, 8, 3 * P], offset=z_at)
        pr = place("pr", [P, 4, T], offset=z_at)
        bias = place("bias", [P, 2, 3 * P], offset=z_at + 12288)
        na_q = place("na_q", [P, T], offset=tmp_at)
        na_k = place("na_k", [P, T], offset=tmp_at + 2048)
        na_v = place("na_v", [P, CB, P], offset=tmp_at + 4096)
        r_q = place("r_q", [P, T], offset=tmp_at + 6144)
        r_k = place("r_k", [P, T], offset=tmp_at + 8192)
        r_tmp = place("r_tmp", [P, T], offset=tmp_at + 10240)
        r_v = place("r_v", [P, 4, RET_DV], offset=tmp_at + 12288)
        sg = place("sg", [P, 2, T], offset=tmp_at + 16384)
        pt = place("pt", [P, 2, 3 * P], offset=tmp_at + 20480)
        o_n = place("o_n", [P, 4, RET_DV], offset=tmp_at + 23552)
        d_tmp = place("d_tmp", [P, 7 * P], offset=tmp_at + 23552)
        d_tab = place("d_tab", [P, 7 * P])
        m_tmp = [place(f"m_tmp{i}", [P, T], offset=z_at + 2048 * i) for i in range(2)]
        sq = [place(f"sq{i}", [P, T], offset=a_at + 8192 + 2048 * i) for i in range(4)]
        rstd = place("rstd", [P, T], offset=a_at + 16384)
        p_sig = [place(f"p_sig{i}", [P, T], offset=a_at + 18432 + 2048 * i) for i in range(4)]
        g_hi = place("g_hi", [P, FT, T], F32R, offset=a_at)
        g_lo = place("g_lo", [P, FT, T], F32R, offset=a_at + FT * T * 4)
        at[0] = max(at[0], a_at + 2 * FT * T * 4)
        lam = place("lam", [P, 3, LAM], offset=c_at)
        lam_re, lam_im, dt = lam[:, 0, :], lam[:, 1, :], lam[:, 2, :]
        angle = place("angle", [P, LAM], offset=c_at + 3 * LAM * 4)
        turns = place("turns", [P, LAM], offset=c_at + 4 * LAM * 4)
        mag = place("mag", [P, LAM], offset=c_at + 5 * LAM * 4)
        sine = place("sine", [P, LAM], offset=c_at + 6 * LAM * 4)
        phase = place("phase", [P, 2, ST, NB], offset=c_at)
        abar_r = place("abar_r", [P, LAM], offset=c_at + 8192)
        abar_i = place("abar_i", [P, LAM], offset=c_at + 8192 + LAM * 4)
        st = place("st", [P, 12, ST], offset=c_at + 8192 + 2 * LAM * 4)
        mpar = place("mpar", [P, MPAR], offset=c_at + 8192 + 2 * LAM * 4 + 48 * ST)
        rms_eps = place("rms_eps", [P, 1], offset=c_at + 12288 - 32)
        u_all = place("u_all", [P, KT, T], offset=c_at + 12288)
        mix_lo = place("mix_lo", [P, KT, T], F32R, offset=c_at + 12288)
        w_b = place("w_b", [P, BT, 2, SP_T, SN], offset=c_at + 28672)
        k_conv = place("k_conv", [P, SP_T, BT, P], offset=c_at + 28672)
        yg = place("yg", [P, SP_T, T], offset=c_at + 28672)
        yg_hi = place("yg_hi", [P, SP_T, T], F32R, offset=c_at + 36864)
        c_pow = place("c_pow", [P, ST, 2, BT + 1, 2 * SCH], offset=c_at + 45056)
        yg_lo = place("yg_lo", [P, SP_T, T], F32R, offset=c_at + 45056)
        glu_sig = [place(f"glu_sig{i}", [P, T], offset=c_at + 53248 + 2048 * i) for i in range(2)]
        mix_hi = place("mix_hi", [P, KT, T], F32R, offset=c_at + 61440)
        b_st = place("b_st", [P, 2, ST, 2 * SCH], offset=c_at + 81920)
        x_zone = c_at + 86016
        w_pool = place("w_pool", [P, SP_T, P], offset=x_zone)
        t_w = place("t_w", [P, SP_T, SN], offset=x_zone + 2048)
        t_c = [place(f"t_c{i}", [P, ST, 2 * SCH], offset=x_zone + 3072 + 2048 * i) for i in range(2)]
        run = [place(f"run{i}", [P, T], offset=x_zone + 7168 + 2048 * i) for i in range(2)]
        c_st = place("c_st", [P, 2, ST, 2 * SCH], offset=x_zone + 11264)
        xn = p_sig
        xn_2 = [place(f"xn_2{i}", [P, T], offset=c_at + 28672 + 2048 * i) for i in range(4)]
        sq_2 = [place(f"sq_2{i}", [P, T], offset=c_at + 2048 * i) for i in range(4)]
        rstd_2 = place("rstd_2", [P, T], offset=x_zone + 8192)
        silu = [place(f"silu{i}", [P, T], offset=c_at + 2048 * i) for i in range(2)]
        hidden = [place(f"hidden{i}", [P, T], offset=c_at + 4096 + 2048 * i) for i in range(2)]
        xh_at = z_at - 2 * KT * T * 4
        w_b2 = place("w_b2", [P, BT, 2, SP_T, 2, SN], offset=xh_at)
        s_r = place("s_r", [P, ST, NB], offset=xh_at)
        s_i = place("s_i", [P, ST, NB], offset=xh_at + 4096)
        before_r = place("before_r", [P, ST, NB + 1], offset=xh_at + 8192)
        before_i = place("before_i", [P, ST, NB + 1], offset=xh_at + 12384)
        t_s = [place(f"t_s{i}", [P, ST // 2, NB], offset=xh_at + 16640 + 2048 * i) for i in range(2)]
        out_t = place("out_t", [P, KT, T], offset=xh_at)
        rstd_3 = place("rstd_3", [P, T], offset=xh_at + KT * T * 4)
        small = place("small", [P, 64])
        row_max, row_nmax, row_sum, row_inv = (small[:, 8 * i:8 * i + 8] for i in range(4))
        gn_std, gn_inv = small[:, 32:36], small[:, 36:40]
        lg_now = small[:, 40:42]
        gn_st = place("gn_st", [P, 4, 6])
        gn_mv = place("gn_mv", [P, 4, 2])
        assert at[0] <= nc.sbuf_usable_end, (at[0], nc.sbuf_usable_end)

        bank = [ctx.enter_context(nc.psum_tensor(f"bank{i}", [P, T], F32)) for i in range(8)]
        U_BANK, S_BANK, T_BANK, Y_BANK, O_BANK = bank[0:2], bank[2:4], bank[4:6], bank[6], bank[7]

        landed = [sem(f"unit_landed{i}") for i in range(RING)]
        hi_done = sem("unit_hi_done")
        lo_done = sem("unit_lo_done")
        unit_used = sem("unit_used")
        mid_done = sem("mid_unit_result_done")
        bank_free = [sem(f"unit_bank_free{i}") for i in range(2)]
        params_in = sem("params_in")
        x_in = sem("x_in")
        consts_set = sem("consts_set")
        x_hi, x_lo = sem("x_hi"), sem("x_lo")
        decay_step = sem("decay_step")
        tables_in = sem("tables_in")
        bias_in = sem("bias_in")
        vt_done, v_ready = sem("v_turned"), sem("v_ready")
        dterm_copy = sem("decay_rates_copied")
        dterm, dtab_ready = sem("decay_terms"), sem("decay_table_ready")
        score_done = sem("score_done")
        s_free = [sem(f"score_bank_free{i}") for i in range(2)]
        masked, nmax_ready = sem("scores_masked"), sem("neg_max_ready")
        exp_done, inv_ready, p_ready = sem("exp_done"), sem("row_inverse"), sem("probs_ready")
        pt_done, pt_ready, pv_done = sem("probs_turned"), sem("probs_t_ready"), sem("pv_done")
        ya_ready = sem("ya_ready")
        rope_cos, rope_ready = sem("rope_cos"), sem("rope_ready")
        o_done, gn_stat, gn_aggr = sem("ret_out_done"), sem("gn_stats"), sem("gn_aggr")
        std_ready, ginv_ready, o_norm = sem("gn_std"), sem("gn_inv"), sem("ret_out_normed")
        ot_done, ot_read = sem("ret_out_turned"), sem("yb_ready")
        sig_ready = sem("silu_sigmoid")
        br_hi, br_lo = sem("branch_in_hi"), sem("branch_in_lo")
        merged, merged_hi, merged_lo = sem("merged"), sem("merged_hi"), sem("merged_lo")
        z_ready, mean_done, centred = sem("z_ready"), sem("mean_done"), sem("centred")
        squared, sq_used = sem("squared"), sem("square_used")
        lstd, lrstd, normed = sem("ln_std"), sem("ln_rstd"), sem("ln_normed")
        x_ready = sem("x_ready")
        p_in, p_hi_s, p_lo_s = sem("p_in"), sem("p_hi_done"), sem("p_lo_done")
        ple_term, zpre = sem("ple_term"), sem("z_pre_ready")
        conv_mid, conv_left = sem("conv_centre"), sem("conv_left")
        gelu_done, glu_done = sem("gelu_done"), sem("glu_done")
        g_hi_s, g_lo_s = sem("g_hi_done"), sem("g_lo_done")
        out_done = sem("out_done")
        mix_in = sem("mixer_params_in")
        dt_ready, growth, mag_ready = sem("ssm_dt"), sem("ssm_growth"), sem("ssm_mag")
        angle_ready, sines_ready, lam_ready = sem("ssm_angle"), sem("ssm_sines"), sem("ssm_lambda")
        prep, c_ready, zeroed = sem("ssm_prep_step"), sem("ssm_c_powers"), sem("ssm_zeroed")
        wb_step, wb_ready, wb_apart = sem("ssm_b_step"), sem("ssm_b_powers"), sem("ssm_b_apart")
        lam_in = sem("eigenvalues_in")
        kernel_done, kernel_ready = sem("ssm_kernel_done"), sem("ssm_kernel_ready")
        pool_step, pooled, pool_done, y_pool = (sem("pool_step"), sem("pooled"), sem("pool_product"), sem("y_pool"))
        v_done, turn_step, state_ready = sem("ssm_block_inputs"), sem("ssm_turn_step"), sem("ssm_state")
        y_done, y_skip, y_gelu = sem("ssm_y_done"), sem("ssm_y_skip"), sem("ssm_y_gelu")
        yg_hi_s, yg_lo_s, glu_sig_s, y_ssm = sem("yg_hi"), sem("yg_lo"), sem("glu_sigmoid"), sem("y_ssm")
        mix_hi_s, mix_lo_s = sem("mix_hi"), sem("mix_lo")
        gu_hi, gu_lo = sem("hidden_hi"), sem("hidden_lo")
        rms_set = sem("rms_eps_set")
        pe_passed, dve_passed = sem("pe_passed"), sem("dve_passed")

        block = ctx.enter_context(nc.Block())

        def stand(eng, passed):
            eng.sem_inc(passed, 1)

        def block_view(ap):
            return ap.rearrange("p (r b c) -> p b r c", r=ROWS, b=CB)

        def kblocks(j):
            return range(1 if j == 0 else 0, 2 if j == CB - 1 else 3)

        def mask_of(j):
            return 0 if j == 0 else 2 if j == CB - 1 else 1

        def free_before(L, r, i=0):
            return L * (LAYER_R // 2) + i + r // 2 + 1

        def after_result(L, r, i=0):
            return bank_free[r % 2], free_before(L, r, i) + 1

        @block.sync
        def _(sp):
            def load(s, u):
                src = a["w"][u] if isinstance(u, int) else a["w"][bass.ds(u, 1)].rearrange("s p n -> p (s n)")
                sp.dma_start(stage[s][:, :, :].rearrange("p t n -> p (t n)"), src).then_inc(landed[s], 16)

            for s in range(RING):
                load(s, s)
            with sp.Fori(1, N_UNITS // RING) as n:
                for s in range(RING):
                    sp.wait_ge(lo_done, n * RING + (s - RING + 1))
                    load(s, n * RING + s)
            for h in range(2):
                sp.wait_ge(normed, (MIX * 2 + 2) * KT + (4 * h + 4))
                sp.dma_start(out[:, 4 * h:4 * h + 4, :], out_t[:, 4 * h:4 * h + 4, :]).then_inc(out_done, 16)
            sp.wait_ge(out_done, 32)

        @block.gpsimd
        def _(pool):
            def low_part(n, s):
                pool.wait_ge(hi_done, n * RING + (s + 1))
                pool.tensor_tensor(w_lo[s][:, :, :], stage[s][:, :, :], w_hi[s][:, :, :].bitcast(F32),
                                   ALU.subtract).then_inc(lo_done, 1)

            mixer_round = DEPTH * LAYER_U // RING
            with pool.Fori(0, mixer_round + 1) as n:
                for s in range(RING):
                    low_part(n, s)
            pool.wait_ge(mix_in, 16 * MIX_LOADS)
            pool.wait_ge(lam_ready, 2)
            ar, ai = (x[:, 0:SP_T * SN].rearrange("p (q n) -> p q n", q=SP_T) for x in (abar_r, abar_i))
            for k in range(BT):
                if k < BT - 1:
                    now, new = BT - 1 - k, BT - 2 - k
                    br, bi, nr, ni = (w_b[:, j, c, :, :] for j in (now, new) for c in (0, 1))
                    if k:
                        pool.wait_ge(wb_ready, 2 * k)
                    pool.tensor_tensor(nr, br, ar, ALU.mult).then_inc(wb_step, 1)
                    pool.tensor_tensor(t_w[:, :, :], bi, ai, ALU.mult).then_inc(wb_step, 1)
                    pool.wait_ge(wb_step, 4 * k + 2)
                    pool.tensor_tensor(nr, nr, t_w[:, :, :], ALU.subtract).then_inc(wb_ready, 1)
                    pool.tensor_tensor(ni, br, ai, ALU.mult).then_inc(wb_step, 1)
                    pool.wait_ge(wb_ready, 2 * k + 1)
                    pool.tensor_tensor(t_w[:, :, :], bi, ar, ALU.mult).then_inc(wb_step, 1)
                    pool.wait_ge(wb_step, 4 * k + 4)
                    pool.tensor_tensor(ni, ni, t_w[:, :, :], ALU.add).then_inc(wb_ready, 1)
                low_part(mixer_round + 1 + k // RING, k % RING)
            with pool.Fori(mixer_round + 3, N_UNITS // RING) as n:
                for s in range(RING):
                    low_part(n, s)

        @block.tensor
        def _(pe):
            def passes(dst, lhs, rhs, start, stop, swapped=False):
                for n, (i, j) in enumerate(((0, 0), (0, 1), (1, 0))):
                    mm = pe.matmul(dst, lhs[i], rhs[j], start=start and n == 0, stop=stop and n == 2)
                return mm

            def take_unit(L, u, i=0):
                pe.wait_ge(lo_done, L * LAYER_U + i + u + 1)

            def take_bank(L, r, i=0):
                pe.wait_ge(bank_free[r % 2], free_before(L, r, i))
                return U_BANK[r % 2]

            def wt(u, k):
                s = u % RING
                return w_hi[s][:, k, :], w_lo[s][:, k, :]

            def feature_unit(L, u, r, rhs, ui=0, ri=0):
                take_unit(L, u, ui)
                dst = take_bank(L, r, ri)
                for k in range(KT):
                    mm = passes(dst[:, :], wt(u, k), rhs(k), k == 0, k == KT - 1)
                mm.then_inc(unit_used, 1)

            def x_parts(k):
                return xh[:, k, :], xl[:, k, :]

            def token_unit(L, u, r, ui=0, ri=0):
                take_unit(L, u, ui)
                dst = take_bank(L, r, ri)
                for b in range(4):
                    for k in range(KT):
                        mm = passes(dst[:, b * P:(b + 1) * P], (xh[:, k, b * P:(b + 1) * P], xl[:, k, b * P:(b + 1) * P]),
                                    wt(u, k), k == 0, k == KT - 1)
                mm.then_inc(unit_used, 1)

            def attention(L, t):
                it = L * 4 + t
                ui, ri = t * 12, t * 6

                def take_score(n):
                    pe.wait_ge(s_free[n % 2], it * 7 + (n // 2 + 1))
                    return S_BANK[n % 2]

                def scores(hh):
                    for r in range(2):
                        pe.wait_ge(*after_result(L, r, ri))
                    r0 = hh * NA_DH
                    q, k = na_q[r0:r0 + NA_DH, :], na_k[r0:r0 + NA_DH, :]
                    for j in range(CB):
                        dst = take_score(4 * hh + j)
                        for b in kblocks(j):
                            mm = pe.matmul(dst[:, b * P:(b + 1) * P], q[:, j * P:(j + 1) * P], k[:, (j - 1 + b) * P:(j + b) * P],
                                           start=True, stop=True)
                        mm.then_inc(score_done, 1)

                def rotate(n, src, ready):
                    pe.wait_ge(*after_result(L, ready, ri))
                    dst = take_score(n)
                    pe.matmul(dst[:, :], swap[:, :], src[:, :], start=True, stop=True).then_inc(score_done, 1)

                def turn_v():
                    pe.wait_ge(*after_result(L, 2, ri))
                    pe.wait_ge(o_norm, it * 4 + 4)
                    for b in range(CB):
                        mm = pe.transpose(O_BANK[:, b * P:(b + 1) * P], r_tmp[:, b * P:(b + 1) * P], ident[:, :])
                    mm.then_inc(vt_done, 1)

                def turn_probs(i):
                    j = i % CB
                    if i < 2:
                        pe.wait_ge(ot_read, it * 2 + (i + 1))
                    else:
                        pe.wait_ge(pt_ready, it * 8 + (i - 1))
                    pe.wait_ge(p_ready, it * 8 + (i + 1))
                    for b in kblocks(j):
                        mm = pe.transpose(T_BANK[i % 2][:, b * P:(b + 1) * P], s_t[:, i, b * P:(b + 1) * P], ident[:, :])
                    mm.then_inc(pt_done, 1)

                def pv(i):
                    hh, j = i // CB, i % CB
                    if i == 0:
                        pe.wait_ge(o_norm, it * 4 + 4)
                        pe.wait_ge(v_ready, it + 1)
                    pe.wait_ge(pt_ready, it * 8 + (i + 1))
                    r0 = hh * NA_DH
                    dst = Y_BANK[r0:r0 + NA_DH, j * P:(j + 1) * P]
                    bs = kblocks(j)
                    for b in bs:
                        mm = pe.matmul(dst, na_v[:, j - 1 + b, r0:r0 + NA_DH], pt[:, i % 2, b * P:(b + 1) * P],
                                       start=b == bs[0], stop=b == bs[-1])
                    mm.then_inc(pv_done, 1)

                feature_unit(L, 0, 0, x_parts, ui, ri)
                feature_unit(L, 1, 1, x_parts, ui, ri)
                feature_unit(L, 2, 2, x_parts, ui, ri)
                scores(0)
                turn_v()
                feature_unit(L, 3, 3, x_parts, ui, ri)
                scores(1)
                rotate(8, r_q, 3)
                turn_probs(0)
                turn_probs(1)
                feature_unit(L, 4, 4, x_parts, ui, ri)
                pv(0)
                pv(1)
                turn_probs(2)
                turn_probs(3)
                rotate(9, r_k, 4)
                token_unit(L, 5, 5, ui, ri)
                pv(2)
                pv(3)
                turn_probs(4)
                turn_probs(5)
                token_unit(L, 6, 6, ui, ri)
                pv(4)
                pv(5)
                turn_probs(6)
                turn_probs(7)
                pe.wait_ge(rope_ready, it * 2 + 2)
                for m in range(4):
                    dst = take_score(10 + m)
                    pe.matmul(dst[:, :], r_k[:, m * P:(m + 1) * P], r_q[:, :], start=True, stop=True).then_inc(score_done, 1)
                feature_unit(L, 7, 7, x_parts, ui, ri)
                pv(6)
                pv(7)
                feature_unit(L, 8, 8, x_parts, ui, ri)
                for b in range(2):
                    pe.wait_ge(s_free[b], it * 7 + 8)
                for r in (5, 6):
                    pe.wait_ge(*after_result(L, r, ri))
                for n in range(4):
                    dst = (O_BANK if n < 2 else Y_BANK)[:, (n % 2) * RET_DV:(n % 2 + 1) * RET_DV]
                    if n == 2:
                        pe.wait_ge(ya_ready, it + 1)
                    for m in range(4):
                        mm = pe.matmul(dst, pr[:, m, n * P:(n + 1) * P], r_v[:, m, :], start=m == 0, stop=m == 3)
                    mm.then_inc(o_done, 1)
                feature_unit(L, 9, 9, x_parts, ui, ri)
                feature_unit(L, 10, 10, x_parts, ui, ri)
                for f in range(2):
                    pe.wait_ge(pt_ready, it * 8 + (7 + f))
                    pe.wait_ge(o_norm, it * 4 + 8)
                    for n in range(4):
                        mm = pe.transpose(T_BANK[f][:, n * P:(n + 1) * P], o_n[:, n, f * P:(f + 1) * P], ident[:, :])
                    mm.then_inc(ot_done, 1)
                feature_unit(L, 11, 11, x_parts, ui, ri)

            def branches(L, i):
                ui, ri = i * 8, i * 5
                it = L * 2 + i
                for g in range(2):
                    feature_unit(L, BR0 + g, BR_R0 + g, x_parts, ui, ri)
                pe.wait_ge(br_lo, L * 3 + 1)
                for m in range(4):
                    u = BR0 + 2 + m // 2
                    if m % 2 == 0:
                        take_unit(L, u, ui)
                    dst = take_bank(L, BR_R0 + 2 + m, ri)
                    for k in range(4):
                        mm = passes(dst[:, :], wt(u, 4 * (m % 2) + k), (ya_hi[:, k, :], ya_lo[:, k, :]), k == 0, k == 3)
                    mm.then_inc(unit_used if m % 2 else mid_done, 1)
                pe.wait_ge(br_lo, L * 3 + 3)
                for m in range(4):
                    feature_unit(L, BR0 + 4 + m, BR_R0 + 6 + m, lambda k: (yb_hi[:, k, :], yb_lo[:, k, :]), ui, ri)

            def mean_term(k, ready):
                pe.wait_ge(*ready(k))
                mm = pe.matmul(S_BANK[0][:, :], mean_w[:, :], z[:, k, :], start=k == 0, stop=k == KT - 1)
                if k == KT - 1:
                    mm.then_inc(mean_done, 1)

            def square_term(n, k, squares):
                pe.wait_ge(squared, n * KT + (k + 1))
                pe.matmul(S_BANK[1][:, :], mean_w[:, :], squares[k % 4][:, :], start=k == 0, stop=k == KT - 1)\
                    .then_inc(sq_used, 1)

            def variance(n):
                for k in range(KT):
                    square_term(n, k, sq)

            def out_proj(L):
                pe.wait_ge(merged_lo, L * 8 + 8)
                ready = lambda k: (z_ready, L * KT + (k + 1))
                for k in range(KT):
                    feature_unit(L, OUT0 + k, OUT_R0 + k, lambda q: (merged_p[:, q, :], merged_p[:, 8 + q, :]))
                    if k > 0:
                        mean_term(k - 1, ready)
                mean_term(KT - 1, ready)
                variance(L * 2)

            def new_x(n):
                pe.wait_ge(x_lo, n * KT + KT)

            def ple(L):
                pe.wait_ge(p_lo_s, L + 1)
                for h in range(2):
                    u0, r0 = PLE0 + 5 * h, PLE_R0 + 8 * h
                    for m in range(4):
                        feature_unit(L, u0 + m, r0 + m, x_parts)
                    take_unit(L, u0 + 4)
                    for m in range(4):
                        dst = take_bank(L, r0 + 4 + m)
                        for k in range(PLE_T):
                            mm = passes(dst[:, :], wt(u0 + 4, PLE_T * m + k), (p_hi[:, k, :], p_lo[:, k, :]), k == 0, k == PLE_T - 1)
                        mm.then_inc(unit_used if m == 3 else mid_done, 1)

            def down(L, u0, r0, after):
                for m in range(KT):
                    dst = take_bank(L, r0 + m)
                    for k in range(FT):
                        i = m * FT + k
                        if i % UT == 0:
                            take_unit(L, u0 + i // UT)
                        mm = passes(dst[:, :], wt(u0 + i // UT, i % UT), (g_hi[:, k, :], g_lo[:, k, :]), k == 0, k == FT - 1)
                        if i % UT == UT - 1:
                            mm.then_inc(unit_used, 1)
                        elif k == FT - 1:
                            mm.then_inc(mid_done, 1)
                    after(m)

            def down_layer(L):
                pe.wait_ge(g_lo_s, L * FT + FT)
                ready = lambda k: (bank_free[k % 2], free_before(L, DOWN_R0 + k) + 1)
                down(L, DOWN0, DOWN_R0, lambda m: mean_term(m - 1, ready) if m else None)
                mean_term(KT - 1, ready)
                variance(L * 2 + 1)

            def mixer():
                n0 = MIX * 2
                variance(n0)
                new_x(n0 + 1)
                for m in range(KT):
                    feature_unit(MIX, MIN_U0 + m, MIN_R0 + m, x_parts)
                V = (*S_BANK, *T_BANK)
                for r in (SP_T - 2, SP_T - 1):
                    pe.wait_ge(*after_result(MIX, MIN_R0 + r))
                for j in range(BT):
                    pe.wait_ge(wb_apart, 2 * j + 2)
                    for m in range(ST):
                        q, r0 = m // 4, m % 4 * 2 * SCH
                        for c in range(2):
                            mm = pe.matmul(V[m % 4][:, (c * SP_T + q) * NB:(c * SP_T + q + 1) * NB],
                                           w_b2[r0:r0 + 2 * SCH, j, c, q, :, :].rearrange("p h n -> p (h n)"),
                                           u_all[r0:r0 + 2 * SCH, 4 + q, :].rearrange("p (b j) -> p b j", j=BT)[:, :, j],
                                           start=j == 0 and q == 0 and c == 0, stop=j == BT - 1 and q == SP_T - 1 and c == 1)
                        if j == BT - 1 and q == SP_T - 1:
                            mm.then_inc(v_done, 1)
                K_BANK = (Y_BANK, O_BANK)
                pe.wait_ge(c_ready, 2 * BT)
                for m in range(ST):
                    q, r0 = m // 4, m % 4 * 2 * SCH
                    for c in range(2):
                        mm = pe.matmul(K_BANK[q // 2][r0:r0 + 2 * SCH, q % 2 * 256:q % 2 * 256 + 256], b_st[:, c, m, :],
                                       c_pow[:, m, c, 0:BT, :].rearrange("p k n -> p (k n)"), start=c == 0, stop=c == 1)
                    if m % 8 == 7:
                        mm.then_inc(kernel_done, 1)
                for g in range(SP_T):
                    if g >= 2:
                        pe.wait_ge(y_pool, g - 1)
                    pe.wait_ge(pooled, 2 * g + 2)
                    pe.matmul(U_BANK[g % 2][:, :], w_pool[:, g, :], u_all[:, g, :], start=True, stop=True).then_inc(pool_done, 1)
                Y = (Y_BANK, O_BANK, S_BANK[0], S_BANK[1])
                by_place = lambda bank: bank.rearrange("p (b j) -> p b j", j=BT)
                for q in range(SP_T):
                    if q == 0:
                        pe.wait_ge(kernel_ready, 8)
                    if q == 2:
                        pe.wait_ge(turn_step, V_READ)
                    for k in range(BT):
                        pe.matmul(by_place(Y[q][:, :])[:, :, k:BT], k_conv[:, q, k, :],
                                  by_place(u_all[:, 4 + q, :])[:, :, 0:BT - k], start=k == 0, stop=False)
                pe.wait_ge(zeroed, 2)
                pe.wait_ge(c_ready, 2 * BT + 2)
                for q in range(SP_T):
                    pe.wait_ge(state_ready, 2 * (q // 2) + 2)
                    for m in range(4 * q, 4 * q + 4):
                        r0 = m % 4 * 2 * SCH
                        for j in range(BT):
                            for c, s in ((0, before_r), (1, before_i)):
                                mm = pe.matmul(by_place(Y[q][r0:r0 + 2 * SCH, :])[:, :, j], c_pow[:, m, c, j + 1, :],
                                               s[:, m, 0:NB], start=False, stop=j == BT - 1 and c == 1)
                    mm.then_inc(y_done, 1)
                pe.wait_ge(yg_lo_s, SP_T)
                pe.wait_ge(y_pool, SP_T)
                for m in range(SP_T):
                    u = GLU_U0 + m // 2
                    if m % 2 == 0:
                        take_unit(MIX, u)
                    dst = take_bank(MIX, GLU_R0 + m)
                    for k in range(SP_T):
                        mm = passes(dst[:, :], wt(u, 4 * (m % 2) + k), (yg_hi[:, k, :], yg_lo[:, k, :]), k == 0, k == SP_T - 1)
                    mm.then_inc(unit_used if m % 2 else mid_done, 1)
                pe.wait_ge(mix_lo_s, KT)
                for m in range(KT):
                    feature_unit(MIX, MOUT_U0 + m, MOUT_R0 + m, lambda k: (mix_hi[:, k, :], mix_lo[:, k, :]))
                    if m:
                        square_term(n0 + 1, m - 1, sq_2)
                square_term(n0 + 1, KT - 1, sq_2)
                new_x(n0 + 2)
                with pe.Fori(0, FT // 2) as j:
                    for m in range(4):
                        feature_unit(MIX, GU_U0 + m, GU_R0 + m, x_parts, j * 4, j * 2)
                pe.wait_ge(gu_lo, FT)
                down(MIX, MDOWN_U0, MDOWN_R0, lambda m: square_term(n0 + 2, m - 1, sq_2) if m else None)
                square_term(n0 + 2, KT - 1, sq_2)

            pe.sem_inc(unit_used, 1)
            pe.wait_ge(params_in, 16 * 5)
            pe.wait_ge(consts_set, 3)
            with pe.Fori(0, DEPTH) as L:
                new_x(L * 2)
                stand(pe, pe_passed)
                with pe.Fori(0, 4) as t:
                    attention(L, t)
                with pe.Fori(0, 2) as i:
                    branches(L, i)
                out_proj(L)
                new_x(L * 2 + 1)
                ple(L)
                with pe.Fori(0, FT // 2) as j:
                    for m in range(4):
                        feature_unit(L, UP0 + m, UP_R0 + m, x_parts, j * 4, j * 2)
                down_layer(L)
            mixer()

        @block.scalar
        def _(act):
            def round_ahead(L, u, i=0):
                n = u + 3
                s = n % RING
                act.wait_ge(landed[s], (L * (LAYER_U // RING) + n // RING + 1) * 16 + i * (16 // RING))
                act.wait_ge(unit_used, L * LAYER_U + i + (u + 1))
                act.activation(w_hi[s][:, :, :], stage[s][:, :, :], ACT.Copy).then_inc(hi_done, 1)

            def unit_result(L, u, i=0):
                act.wait_ge(unit_used, L * LAYER_U + i + (u + 2))

            def attention(L, t):
                it = L * 4 + t
                ui = t * 12

                def copy_out(u, dst, scale=1.0):
                    unit_result(L, u, ui)
                    act.activation(dst, U_BANK[u % 2][:, :], ACT.Copy, scale=scale).then_inc(bank_free[u % 2], 1)

                def copy_blocks(u, dst, scale=1.0):
                    unit_result(L, u, ui)
                    act.activation(dst.rearrange("p (b r c) -> p b r c", b=CB, r=ROWS), block_view(U_BANK[u % 2][:, :]),
                                   ACT.Copy, scale=scale).then_inc(bank_free[u % 2], 1)

                def exps(hh):
                    act.wait_ge(nmax_ready, it * 2 + (hh + 1))
                    for j in range(CB):
                        i = 4 * hh + j
                        bs = kblocks(j)
                        s = s_t[:, i, bs[0] * P:(bs[-1] + 1) * P]
                        act.activation(s, s, ACT.Exp, bias=row_nmax[:, i:i + 1], accum_out=row_sum[:, i:i + 1])\
                            .then_inc(exp_done, 1)

                def probs_t(i):
                    bs = kblocks(i % CB)
                    act.wait_ge(pt_done, it * 8 + (i + 1))
                    if i >= 2:
                        act.wait_ge(pv_done, it * 8 + (i - 1))
                    act.activation(pt[:, i % 2, bs[0] * P:(bs[-1] + 1) * P],
                                   T_BANK[i % 2][:, bs[0] * P:(bs[-1] + 1) * P], ACT.Copy).then_inc(pt_ready, 1)

                act.wait_ge(unit_used, L * LAYER_U + t * 12 + 1)
                act.dma_start(bias[:, :, :].rearrange("p h n -> p (h n)"),
                              a["bias"][bass.ds(it, 1)].rearrange("s p n -> p (s n)")).then_inc(bias_in, 16)
                round_ahead(L, 0, ui)
                copy_blocks(0, na_q[:, :], NA_DH ** -0.5)
                round_ahead(L, 1, ui)
                copy_blocks(1, na_k[:, :])
                round_ahead(L, 2, ui)
                copy_blocks(2, r_tmp[:, :])
                act.wait_ge(dterm, it * 3 + 3)
                act.activation(d_tab[:, :], d_tab[:, :], ACT.Exp).then_inc(dtab_ready, 1)
                act.wait_ge(vt_done, it + 1)
                act.activation(na_v[:, :, :].rearrange("p b n -> p (b n)"), O_BANK[:, :], ACT.Copy).then_inc(v_ready, 1)
                exps(0)
                round_ahead(L, 3, ui)
                copy_out(3, r_q[:, :])
                probs_t(0)
                probs_t(1)
                exps(1)
                round_ahead(L, 4, ui)
                copy_out(4, r_k[:, :])
                probs_t(2)
                probs_t(3)
                round_ahead(L, 5, ui)
                unit_result(L, 5, ui)
                act.activation(r_v[:, :, 0:P], U_BANK[1][:, :].rearrange("p (n c) -> p n c", n=4), ACT.Copy)\
                    .then_inc(bank_free[1], 1)
                probs_t(4)
                probs_t(5)
                round_ahead(L, 6, ui)
                unit_result(L, 6, ui)
                act.activation(r_v[:, :, P:2 * P], U_BANK[0][:, :].rearrange("p (n c) -> p n c", n=4), ACT.Copy)\
                    .then_inc(bank_free[0], 1)
                probs_t(6)
                probs_t(7)
                for f in range(2):
                    round_ahead(L, 7 + f, ui)
                    unit_result(L, 7 + f, ui)
                    act.activation(sg[:, f, :], U_BANK[(7 + f) % 2][:, :], ACT.Sigmoid).then_inc(sig_ready, 1)
                    if f == 0:
                        act.wait_ge(pv_done, it * 8 + 8)
                        act.activation(ya[:, bass.ds(t, 1), :].rearrange("p s (r b c) -> p (s r) b c", r=ROWS, b=CB),
                                       Y_BANK[:, :].rearrange("p (b r c) -> p r b c", b=CB, r=ROWS), ACT.Copy)\
                            .then_inc(ya_ready, 1)
                round_ahead(L, 9, ui)
                act.wait_ge(gn_aggr, it * 4 + 4)
                act.activation(gn_std, gn_mv[:, :, 1], ACT.Sqrt, bias=gn_eps[:, :]).then_inc(std_ready, 1)
                for g in range(3):
                    if g:
                        round_ahead(L, 9 + g, ui)
                    unit_result(L, 9 + g, ui)
                    act.activation(gates[:, bass.ds(t * 3 + g, 1), :].rearrange("p s n -> p (s n)"),
                                   U_BANK[(9 + g) % 2][:, :], ACT.Sigmoid).then_inc(bank_free[(9 + g) % 2], 1)

            def branches(L, i):
                ui = i * 8
                it = L * 2 + i
                for g in range(2):
                    round_ahead(L, BR0 + g, ui)
                    unit_result(L, BR0 + g, ui)
                    act.activation(gates[:, bass.ds(i * 2 + (12 + g), 1), :].rearrange("p s n -> p (s n)"),
                                   U_BANK[g][:, :], ACT.Sigmoid).then_inc(bank_free[g], 1)
                for u in range(2, 4):
                    round_ahead(L, BR0 + u, ui)
                for m in range(4):
                    round_ahead(L, BR0 + 4 + m, ui)
                    act.wait_ge(merged, it * 4 + (m + 1))
                    act.activation(merged_p[:, bass.ds(i * 4 + m, 1), :].rearrange("p s n -> p (s n)"),
                                   m_tmp[m % 2][:, :], ACT.Copy).then_inc(merged_hi, 1)

            def split_branch_inputs(L):
                act.wait_ge(ya_ready, L * 4 + 4)
                act.wait_ge(ot_read, L * 8 + 10)
                act.activation(ya_hi[:, :, :], ya[:, :, :], ACT.Copy).then_inc(br_hi, 1)
                for h in range(2):
                    act.activation(yb_hi[:, 4 * h:4 * h + 4, :], yb[:, 4 * h:4 * h + 4, :], ACT.Copy).then_inc(br_hi, 1)

            def norm(L, which):
                n = L * 2 + which
                for k in range(KT):
                    act.wait_ge(centred, n * KT + (k + 1))
                    if k >= 4:
                        act.wait_ge(sq_used, n * KT + (k - 3))
                    act.activation(sq[k % 4][:, :], z[:, k, :], ACT.Square).then_inc(squared, 1)
                act.wait_ge(sq_used, n * KT + KT)
                act.activation(rstd[:, :], S_BANK[1][:, :], ACT.Sqrt, bias=ln_eps[:, :]).then_inc(lstd, 1)
                for k in range(KT):
                    act.wait_ge(normed, n * KT + (k + 1))
                    act.activation(z[:, k, :], z[:, k, :], ACT.Identity,
                                   scale=lnp[:, bass.ds(L, 1), 2 * which, k], bias=lnp[:, bass.ds(L, 1), 2 * which + 1, k])\
                        .then_inc(x_ready, 1)
                    act.wait_ge(x_ready, n * KT + (k + 1))
                    act.activation(xh[:, k, :], z[:, k, :], ACT.Copy).then_inc(x_hi, 1)

            def ple(L):
                act.wait_ge(p_in, L * 16 + 16)
                act.activation(p_hi[:, :, :], p_raw[:, :, :], ACT.Copy).then_inc(p_hi_s, 1)
                for h in range(2):
                    u0, r0 = PLE0 + 5 * h, PLE_R0 + 8 * h
                    for m in range(4):
                        round_ahead(L, u0 + m)
                        unit_result(L, u0 + m)
                        if h:
                            act.wait_ge(zpre, L * 8 + (m + 1))
                        act.activation(p_sig[m][:, :], U_BANK[m % 2][:, :], ACT.Sigmoid).then_inc(bank_free[m % 2], 1)
                    round_ahead(L, u0 + 4)

            def up(L, j):
                it = L * FT + j * 2
                for c in range(2):
                    for half, buf in ((0, conv_a), (1, conv_b)):
                        u = UP0 + 2 * c + half
                        round_ahead(L, u, j * 4)
                        unit_result(L, u, j * 4)
                        ch = bass.ds(j * 2 + (half * FT + c), 1)
                        act.activation(buf[c][:, :], U_BANK[half][:, :], ACT.Identity,
                                       scale=convp[:, bass.ds(L, 1), 1, ch].rearrange("p l c -> p (l c)"),
                                       bias=convp[:, bass.ds(L, 1), 3, ch].rearrange("p l c -> p (l c)")).then_inc(conv_mid, 1)
                    act.wait_ge(bank_free[0], free_before(L, UP_R0 + 2 * c, j * 2) + 1)
                    act.activation(conv_a[c][:, :], conv_a[c][:, :], ACT.Gelu_apprx_tanh).then_inc(gelu_done, 1)
                    act.wait_ge(glu_done, it + (c + 1))
                    act.activation(g_hi[:, bass.ds(j * 2 + c, 1), :].rearrange("p s n -> p (s n)"), conv_b[c][:, :],
                                   ACT.Copy).then_inc(g_hi_s, 1)

            def rms_split(n, tiles):
                for k in range(KT):
                    act.wait_ge(normed, n * KT + (k + 1))
                    act.activation(xh[:, k, :], tiles[k % 4][:, :], ACT.Copy).then_inc(x_hi, 1)

            def root(n, dst):
                act.wait_ge(sq_used, n * KT + KT)
                act.wait_ge(rms_set, 1)
                act.activation(dst[:, :], S_BANK[1][:, :], ACT.Sqrt, bias=rms_eps[:, :]).then_inc(lstd, 1)

            def square(n, k, squares, ready):
                act.wait_ge(*ready)
                if k >= 4:
                    act.wait_ge(sq_used, n * KT + (k - 3))
                act.activation(squares[k % 4][:, :], z[:, k, :], ACT.Square).then_inc(squared, 1)

            def mixer():
                n0 = MIX * 2
                ahead = lambda u: round_ahead(MIX, u) if u + 3 < MIX_U else None
                after = lambda r: (bank_free[r % 2], free_before(MIX, r) + 1)
                act.wait_ge(x_lo, n0 * KT + KT)
                act.dma_start(lam[:, :, :], a["lam"]).then_inc(lam_in, 16)
                for dst, name in ((mpar, "mpar"), (w_pool, "w_pool"), (b_st, "b_st"), (c_st, "c_st")):
                    act.dma_start(dst[:], a[name]).then_inc(mix_in, 16)
                act.dma_start(w_b[:, BT - 1, :, :, :], a["w_b"]).then_inc(mix_in, 16)
                for k in range(KT):
                    square(n0, k, sq, (x_ready, (n0 - 1) * KT + (k + 1)))
                root(n0, rstd)
                rms_split(n0, xn)
                act.wait_ge(lam_in, 16)
                act.activation(dt, dt, ACT.Exp).then_inc(dt_ready, 1)
                act.wait_ge(growth, 1)
                act.activation(mag[:, :], mag[:, :], ACT.Exp).then_inc(mag_ready, 1)
                act.wait_ge(angle_ready, 1)
                act.activation(sine[:, :], angle[:, :], ACT.Sin).then_inc(sines_ready, 1)
                act.activation(turns[:, :], angle[:, :], ACT.Sin, scale=0.5).then_inc(sines_ready, 1)
                for m in range(KT):
                    ahead(MIN_U0 + m)
                    unit_result(MIX, MIN_U0 + m)
                    act.activation(u_all[:, (m + SP_T) % KT, :], U_BANK[m % 2][:, :], ACT.Copy).then_inc(bank_free[m % 2], 1)
                act.wait_ge(unit_used, MIX * LAYER_U + (MIN_U0 + KT) + 1)
                for j in range(BT):
                    for h in range(2):
                        act.wait_ge(wb_ready, 2 * (BT - 1))
                        act.activation(w_b2[:, j, :, :, h, :].rearrange("p c q n -> p (c q) n"),
                                       w_b[:, j, :, :, :].rearrange("p c q n -> p (c q) n"), ACT.Copy,
                                       scale=mpar[:, HALF_C + h:HALF_C + h + 1]).then_inc(wb_apart, 1)
                act.wait_ge(v_done, 4)
                for f in range(2):
                    act.wait_ge(kernel_done, f + 1)
                    for h in range(4):
                        bank_f = (Y_BANK, O_BANK)[f]
                        act.activation(k_conv[:, 2 * f:2 * f + 2, :, h * 2 * SCH:(h + 1) * 2 * SCH].rearrange("p q k n -> p (q k) n"),
                                       bank_f[:, :].rearrange("p (a n) -> p a n", n=2 * SCH), ACT.Copy,
                                       scale=mpar[:, QUART_C + h:QUART_C + h + 1]).then_inc(kernel_ready, 1)
                for g in range(SP_T):
                    act.wait_ge(pool_done, g + 1)
                    act.activation(u_all[:, g, :], U_BANK[g % 2][:, :], ACT.Copy,
                                   scale=mpar[:, POOLS_C + g:POOLS_C + g + 1]).then_inc(y_pool, 1)
                for q in range(SP_T):
                    act.wait_ge(y_skip, q + 1)
                    act.activation(yg[:, q, :], yg[:, q, :], ACT.Gelu_apprx_tanh).then_inc(y_gelu, 1)
                    act.wait_ge(y_gelu, q + 1)
                    act.activation(yg_hi[:, q, :], yg[:, q, :], ACT.Copy).then_inc(yg_hi_s, 1)
                for g in range(SP_T):
                    act.wait_ge(y_pool, g + 1)
                    act.activation(mix_hi[:, g, :], u_all[:, g, :], ACT.Copy).then_inc(mix_hi_s, 1)
                for m in range(SP_T):
                    if m % 2 == 0:
                        ahead(GLU_U0 + m // 2)
                        act.wait_ge(mid_done, MIX * LAYER_M + (GLU_M0 + m // 2 + 1))
                    else:
                        unit_result(MIX, GLU_U0 + m // 2)
                    if m >= 2:
                        act.wait_ge(y_ssm, m - 1)
                    act.activation(glu_sig[m % 2][:, :], U_BANK[m % 2][:, :], ACT.Sigmoid,
                                   bias=mpar[:, BGLU_C + m:BGLU_C + m + 1]).then_inc(bank_free[m % 2], 1)
                for m in range(SP_T):
                    act.wait_ge(y_ssm, m + 1)
                    act.activation(mix_hi[:, SP_T + m, :], u_all[:, SP_T + m, :], ACT.Copy).then_inc(mix_hi_s, 1)
                for m in range(KT):
                    ahead(MOUT_U0 + m)
                    square(n0 + 1, m, sq_2, after(MOUT_R0 + m))
                root(n0 + 1, rstd_2)
                rms_split(n0 + 1, xn_2)
                with act.Fori(0, FT // 2) as j:
                    for c in range(2):
                        u = GU_U0 + 2 * c
                        round_ahead(MIX, u, j * 4)
                        unit_result(MIX, u, j * 4)
                        act.activation(silu[c][:, :], U_BANK[0][:, :], ACT.Silu).then_inc(bank_free[0], 1)
                        round_ahead(MIX, u + 1, j * 4)
                        act.wait_ge(bank_free[1], free_before(MIX, GU_R0 + 2 * c + 1, j * 2) + 1)
                        act.activation(g_hi[:, bass.ds(j * 2 + c, 1), :].rearrange("p s n -> p (s n)"), hidden[c][:, :],
                                       ACT.Copy).then_inc(gu_hi, 1)
                sq_m = 0
                for u in range(DOWN_U):
                    ahead(MDOWN_U0 + u)
                    while sq_m < KT and ((sq_m + 1) * FT - 1) // UT < u:
                        square(n0 + 2, sq_m, sq_2, after(MDOWN_R0 + sq_m))
                        sq_m += 1
                for m in range(sq_m, KT):
                    square(n0 + 2, m, sq_2, after(MDOWN_R0 + m))
                root(n0 + 2, rstd_3)

            act.sem_inc(bank_free[0], 1)
            act.sem_inc(bank_free[1], 1)
            for dst, src in ((z[:, :, :], "x"),):
                act.dma_start(dst, a[src]).then_inc(x_in, 16)
            for dst, src in ((ident, "ident"), (swap, "swap"), (lnp, "lnp"), (convp, "convp"), (decay, "decay")):
                act.dma_start(dst[:], a[src]).then_inc(params_in, 16)
            for n in range(3):
                act.wait_ge(landed[n], 16)
                act.activation(w_hi[n][:, :, :], stage[n][:, :, :], ACT.Copy).then_inc(hi_done, 1)
            act.wait_ge(x_in, 16)
            for k in range(KT):
                act.activation(xh[:, k, :], z[:, k, :], ACT.Copy).then_inc(x_hi, 1)
            act.wait_ge(params_in, 16 * 5)
            flat = decay[:, :, :].rearrange("p d n -> p (d n)")
            act.activation(decay_a[:, :], flat, ACT.Abs).then_inc(decay_step, 1)
            act.wait_ge(decay_step, 1)
            act.activation(decay_a[:, :], decay_a[:, :], ACT.Exp, scale=-1.0).then_inc(decay_step, 1)
            act.wait_ge(decay_step, 2)
            act.activation(decay_a[:, :], decay_a[:, :], ACT.Ln, bias=1.0).then_inc(decay_step, 1)
            with act.Fori(0, DEPTH) as L:
                act.wait_ge(x_lo, (L * 2 + 1) * KT)
                act.dma_start(rope[:, :, :], a["rope"]).then_inc(tables_in, 16)
                act.dma_start(delta[:, :], a["delta"]).then_inc(tables_in, 16)
                act.dma_start(masks[:, :, :], a["masks"]).then_inc(tables_in, 16)
                with act.Fori(0, 4) as t:
                    attention(L, t)
                split_branch_inputs(L)
                act.dma_start(p_raw[:, :, :], a["p"][bass.ds(L, 1)].rearrange("s p k n -> p (s k) n")).then_inc(p_in, 16)
                with act.Fori(0, 2) as i:
                    branches(L, i)
                for k in range(KT):
                    round_ahead(L, OUT0 + k)
                norm(L, 0)
                ple(L)
                with act.Fori(0, FT // 2) as j:
                    up(L, j)
                for k in range(DOWN_U):
                    round_ahead(L, DOWN0 + k)
                norm(L, 1)
            mixer()

        @block.vector
        def _(dve):
            def unit_result(L, u, i=0):
                dve.wait_ge(unit_used, L * LAYER_U + i + (u + 2))

            def attention(L, t):
                it = L * 4 + t
                ui, ri = t * 12, t * 6

                def after_score(n):
                    return s_free[n % 2], it * 7 + (n // 2 + 2)

                dve.tensor_copy(lg_now, decay[:, :, bass.ds(it, 1)].rearrange("p d s -> p (d s)")).then_inc(dterm_copy, 1)
                dve.wait_ge(dterm_copy, it + 1)
                dve.tensor_scalar(d_tmp[:, :], delta[:, :], 0.0, lg_now[:, 1:2], ALU.min, ALU.mult).then_inc(dterm, 1)
                dve.tensor_scalar(d_tab[:, :], delta[:, :], 0.0, lg_now[:, 0:1], ALU.max, ALU.mult).then_inc(dterm, 1)
                dve.wait_ge(dterm, it * 3 + 2)
                dve.tensor_tensor(d_tab[:, :], d_tab[:, :], d_tmp[:, :], ALU.subtract).then_inc(dterm, 1)

                def mask_scores(hh):
                    dve.wait_ge(bias_in, it * 16 + 16)
                    for j in range(CB):
                        i = 4 * hh + j
                        bs = kblocks(j)
                        cols = slice(bs[0] * P, (bs[-1] + 1) * P)
                        dve.wait_ge(score_done, it * 14 + (i + 1))
                        dve.tensor_tensor(s_t[:, i, cols], S_BANK[i % 2][:, cols], bias[:, hh, cols], ALU.add)\
                            .then_inc(s_free[i % 2], 1)
                        dve.wait_ge(*after_score(i))
                        stand(dve, dve_passed)
                        dve.tensor_tensor_reduce(s_t[:, i, cols], s_t[:, i, cols], masks[:, mask_of(j), cols], 1.0, -3.0e38,
                                                 ALU.add, ALU.max, row_max[:, i:i + 1]).then_inc(masked, 1)
                    dve.wait_ge(masked, it * 8 + (4 * hh + 4))
                    dve.tensor_scalar(row_nmax[:, 4 * hh:4 * hh + 4], row_max[:, 4 * hh:4 * hh + 4], -1.0, None, ALU.mult)\
                        .then_inc(nmax_ready, 1)

                def normalise(hh):
                    dve.wait_ge(exp_done, it * 8 + (4 * hh + 4))
                    dve.reciprocal(row_inv[:, 4 * hh:4 * hh + 4], row_sum[:, 4 * hh:4 * hh + 4]).then_inc(inv_ready, 1)
                    dve.wait_ge(inv_ready, it * 2 + (hh + 1))
                    for j in range(CB):
                        i = 4 * hh + j
                        bs = kblocks(j)
                        s = s_t[:, i, bs[0] * P:(bs[-1] + 1) * P]
                        dve.tensor_scalar(s, s, row_inv[:, i:i + 1], None, ALU.mult).then_inc(p_ready, 1)

                def rotate(n, x):
                    k = n - 8
                    dve.wait_ge(score_done, it * 14 + (n + 1))
                    dve.tensor_tensor(r_tmp[:, :], S_BANK[n % 2][:, :], rope[:, 1, :], ALU.mult).then_inc(s_free[n % 2], 1)
                    dve.tensor_tensor(x[:, :], x[:, :], rope[:, 0, :], ALU.mult).then_inc(rope_cos, 1)
                    dve.wait_ge(*after_score(n))
                    dve.wait_ge(rope_cos, it * 2 + (k + 1))
                    dve.tensor_tensor(x[:, :], x[:, :], r_tmp[:, :], ALU.add).then_inc(rope_ready, 1)

                mask_scores(0)
                normalise(0)
                mask_scores(1)
                rotate(8, r_q)
                normalise(1)
                rotate(9, r_k)
                dve.wait_ge(rope_ready, it * 2 + 2)
                dve.wait_ge(dtab_ready, it + 1)
                for m in range(4):
                    dve.wait_ge(score_done, it * 14 + (11 + m))
                    dve.scalar_tensor_tensor(out=pr[:, m, :], in0=S_BANK[m % 2][:, :], scalar=RET_DK ** -0.5,
                                             in1=d_tab[:, (3 - m) * P:(7 - m) * P], op0=ALU.mult, op1=ALU.mult)\
                        .then_inc(s_free[m % 2], 1)
                for f in range(2):
                    dve.wait_ge(sig_ready, it * 2 + (f + 1))
                    dve.tensor_tensor(sg[:, f, :], U_BANK[(7 + f) % 2][:, :], sg[:, f, :], ALU.mult)\
                        .then_inc(bank_free[(7 + f) % 2], 1)

                def o_tile(n):
                    return (O_BANK if n < 2 else Y_BANK)[:, (n % 2) * RET_DV:(n % 2 + 1) * RET_DV]

                for n in range(4):
                    dve.wait_ge(o_done, it * 4 + (2 * (n // 2) + 2))
                    dve.bn_stats(gn_st[:, n, :], o_tile(n)).then_inc(gn_stat, 1)
                dve.wait_ge(gn_stat, it * 4 + 4)
                stand(dve, dve_passed)
                for n in range(4):
                    dve.bn_aggr(gn_mv[:, n, :], gn_st[:, n, :]).then_inc(gn_aggr, 1)
                dve.wait_ge(std_ready, it + 1)
                dve.reciprocal(gn_inv, gn_std).then_inc(ginv_ready, 1)
                dve.wait_ge(ginv_ready, it + 1)
                for n in range(4):
                    dve.tensor_scalar(o_n[:, n, :], o_tile(n), gn_mv[:, n, 0:1], gn_inv[:, n:n + 1], ALU.subtract, ALU.mult)\
                        .then_inc(o_norm, 1)
                for f in range(2):
                    dve.wait_ge(ot_done, it * 2 + (f + 1))
                    dve.tensor_tensor(yb[:, bass.ds(t * 2 + f, 1), :].rearrange("p s n -> p (s n)"), T_BANK[f][:, :],
                                      sg[:, f, :], ALU.mult).then_inc(ot_read, 1)

            def split_branch_inputs(L):
                dve.wait_ge(br_hi, L * 3 + 1)
                dve.tensor_tensor(ya_lo[:, :, :], ya[:, :, :], ya_hi[:, :, :].bitcast(F32), ALU.subtract).then_inc(br_lo, 1)
                for h in range(2):
                    dve.wait_ge(br_hi, L * 3 + (2 + h))
                    q = slice(4 * h, 4 * h + 4)
                    dve.tensor_tensor(yb_lo[:, q, :], yb[:, q, :], yb_hi[:, q, :].bitcast(F32), ALU.subtract).then_inc(br_lo, 1)

            def branches(L, i):
                ui, ri = i * 8, i * 5
                it = L * 2 + i
                g_a = lambda m: gates[:, bass.ds(i * 4 + m, 1), :].rearrange("p s n -> p (s n)")
                g_b = lambda m: gates[:, bass.ds(i * 4 + (8 + m), 1), :].rearrange("p s n -> p (s n)")
                for m in range(4):
                    r = BR_R0 + 2 + m
                    if m % 2:
                        unit_result(L, BR0 + 2 + m // 2, ui)
                    else:
                        dve.wait_ge(mid_done, L * LAYER_M + i * 2 + (BR_M0 + m // 2 + 1))
                    dve.tensor_tensor(g_a(m), U_BANK[r % 2][:, :], g_a(m), ALU.mult).then_inc(bank_free[r % 2], 1)
                for m in range(4):
                    r = BR_R0 + 6 + m
                    unit_result(L, BR0 + 4 + m, ui)
                    dve.tensor_tensor(g_b(m), U_BANK[r % 2][:, :], g_b(m), ALU.mult).then_inc(bank_free[r % 2], 1)
                    dve.wait_ge(bank_free[r % 2], free_before(L, r, ri) + 1)
                    dve.tensor_tensor(m_tmp[m % 2][:, :], g_a(m), g_b(m), ALU.add).then_inc(merged, 1)
                    dve.wait_ge(merged_hi, it * 4 + (m + 1))
                    dve.tensor_tensor(merged_p[:, bass.ds(i * 4 + (8 + m), 1), :].rearrange("p s n -> p (s n)"), m_tmp[m % 2][:, :],
                                      merged_p[:, bass.ds(i * 4 + m, 1), :].rearrange("p s n -> p (s n)").bitcast(F32),
                                      ALU.subtract).then_inc(merged_lo, 1)

            def residual_out(L):
                for k in range(KT):
                    unit_result(L, OUT0 + k)
                    dve.scalar_tensor_tensor(out=z[:, k, :], in0=xh[:, k, :].bitcast(F32), scalar=ALPHA,
                                             in1=U_BANK[k % 2][:, :], op0=ALU.mult, op1=ALU.add).then_inc(bank_free[k % 2], 1)
                    dve.wait_ge(bank_free[k % 2], free_before(L, OUT_R0 + k) + 1)
                    dve.scalar_tensor_tensor(out=z[:, k, :], in0=xl[:, k, :].bitcast(F32), scalar=ALPHA,
                                             in1=z[:, k, :], op0=ALU.mult, op1=ALU.add).then_inc(z_ready, 1)

            def norm(L, which):
                n = L * 2 + which
                dve.wait_ge(mean_done, n + 1)
                for k in range(KT):
                    dve.tensor_tensor(z[:, k, :], z[:, k, :], S_BANK[0][:, :], ALU.subtract).then_inc(centred, 1)
                dve.wait_ge(lstd, n + 1)
                dve.reciprocal(rstd[:, :], rstd[:, :]).then_inc(lrstd, 1)
                dve.wait_ge(lrstd, n + 1)
                for k in range(KT):
                    dve.tensor_tensor(z[:, k, :], z[:, k, :], rstd[:, :], ALU.mult).then_inc(normed, 1)
                for k in range(KT):
                    dve.wait_ge(x_hi, n * KT + (KT + k + 1))
                    dve.tensor_tensor(xl[:, k, :], z[:, k, :], xh[:, k, :].bitcast(F32), ALU.subtract).then_inc(x_lo, 1)

            def ple(L):
                dve.wait_ge(p_hi_s, L + 1)
                dve.tensor_tensor(p_lo[:, :, :], p_raw[:, :, :], p_hi[:, :, :].bitcast(F32), ALU.subtract).then_inc(p_lo_s, 1)
                for h in range(2):
                    for m in range(4):
                        r = PLE_R0 + 8 * h + 4 + m
                        if m == 3:
                            unit_result(L, PLE0 + 5 * h + 4)
                        else:
                            dve.wait_ge(mid_done, L * LAYER_M + (PLE_M0 + 3 * h + m + 1))
                        dve.tensor_tensor(p_sig[m][:, :], U_BANK[r % 2][:, :], p_sig[m][:, :], ALU.mult)\
                            .then_inc(bank_free[r % 2], 1)
                        dve.wait_ge(bank_free[r % 2], free_before(L, r) + 1)
                        dve.scalar_tensor_tensor(out=z[:, 4 * h + m, :], in0=z[:, 4 * h + m, :], scalar=ALPHA, in1=p_sig[m][:, :],
                                                 op0=ALU.mult, op1=ALU.add).then_inc(zpre, 1)

            def up(L, j):
                it = L * FT + j * 2
                for c in range(2):
                    for half, buf in ((0, conv_a), (1, conv_b)):
                        n = 2 * c + half
                        ch = bass.ds(j * 2 + (half * FT + c), 1)
                        tap = lambda w: convp[:, bass.ds(L, 1), w, ch].rearrange("p l c -> p (l c)")
                        ps, y = U_BANK[half], buf[c]
                        dve.wait_ge(conv_mid, it * 2 + (n + 1))
                        dve.scalar_tensor_tensor(out=y[:, 1:T], in0=ps[:, 0:T - 1], scalar=tap(0), in1=y[:, 1:T],
                                                 op0=ALU.mult, op1=ALU.add).then_inc(conv_left, 1)
                        dve.wait_ge(conv_left, it * 2 + (n + 1))
                        dve.scalar_tensor_tensor(out=y[:, 0:T - 1], in0=ps[:, 1:T], scalar=tap(2), in1=y[:, 0:T - 1],
                                                 op0=ALU.mult, op1=ALU.add).then_inc(bank_free[half], 1)
                    dve.wait_ge(gelu_done, it + (c + 1))
                    dve.wait_ge(bank_free[1], free_before(L, UP_R0 + 2 * c + 1, j * 2) + 1)
                    dve.tensor_tensor(conv_b[c][:, :], conv_a[c][:, :], conv_b[c][:, :], ALU.mult).then_inc(glu_done, 1)
                    dve.wait_ge(g_hi_s, it + (c + 1))
                    g = bass.ds(j * 2 + c, 1)
                    dve.tensor_tensor(g_lo[:, g, :].rearrange("p s n -> p (s n)"), conv_b[c][:, :],
                                      g_hi[:, g, :].rearrange("p s n -> p (s n)").bitcast(F32), ALU.subtract).then_inc(g_lo_s, 1)

            def residual_down(L):
                done = 0
                for m in range(KT):
                    last = (m + 1) * FT - 1
                    if last % UT == UT - 1:
                        unit_result(L, DOWN0 + last // UT)
                    else:
                        done += 1
                        dve.wait_ge(mid_done, L * LAYER_M + (DOWN_M0 + done))
                    dve.tensor_tensor(z[:, m, :], z[:, m, :], U_BANK[m % 2][:, :], ALU.add).then_inc(bank_free[m % 2], 1)

            def rms(n, which, rs, tiles):
                dve.wait_ge(lstd, n + 1)
                dve.reciprocal(rs[:, :], rs[:, :]).then_inc(lrstd, 1)
                dve.wait_ge(lrstd, n + 1)

                def low(k):
                    dve.wait_ge(x_hi, (n + 1) * KT + (k + 1))
                    dve.tensor_tensor(xl[:, k, :], tiles[k % 4][:, :], xh[:, k, :].bitcast(F32), ALU.subtract).then_inc(x_lo, 1)

                for k in range(KT):
                    g = mpar[:, NORM_C + which * KT + k:NORM_C + which * KT + k + 1]
                    dst = out_t[:, k, :] if tiles is None else tiles[k % 4][:, :]
                    if tiles is not None and k >= 4:
                        dve.wait_ge(x_lo, (n + 1) * KT + (k - 3))
                    dve.scalar_tensor_tensor(out=dst, in0=z[:, k, :], scalar=g, in1=rs[:, :],
                                             op0=ALU.mult, op1=ALU.mult).then_inc(normed, 1)
                    if tiles is not None and k >= 2:
                        low(k - 2)
                if tiles is not None:
                    low(KT - 2)
                    low(KT - 1)

            def eigenvalues():
                tt, stt, ts = dve.tensor_tensor, dve.scalar_tensor_tensor, dve.tensor_scalar
                dve.wait_ge(dt_ready, 1)
                tt(mag[:, :], lam_re, dt, ALU.mult).then_inc(growth, 1)
                tt(angle[:, :], lam_im, dt, ALU.mult).then_inc(prep, 1)
                dve.wait_ge(prep, 1)
                ts(turns[:, :], angle[:, :], 1.0 / TWO_PI, ROUND, ALU.mult, ALU.add).then_inc(prep, 1)
                dve.wait_ge(prep, 2)
                ts(turns[:, :], turns[:, :], ROUND, None, ALU.subtract).then_inc(prep, 1)
                for n, part in enumerate((TWO_PI_HI, TWO_PI_MID, TWO_PI_LO)):
                    dve.wait_ge(prep, 3 + n)
                    stt(out=angle[:, :], in0=turns[:, :], scalar=-part, in1=angle[:, :], op0=ALU.mult, op1=ALU.add)\
                        .then_inc(prep, 1)
                dve.wait_ge(prep, 6)
                ts(angle[:, :], angle[:, :], SIN_MAX, -SIN_MAX, ALU.min, ALU.max).then_inc(angle_ready, 1)
                dve.wait_ge(sines_ready, 2)
                stt(out=turns[:, :], in0=turns[:, :], scalar=-2.0, in1=turns[:, :], op0=ALU.mult, op1=ALU.mult)\
                    .then_inc(prep, 1)
                dve.wait_ge(prep, 7)
                dve.wait_ge(mag_ready, 1)
                stt(out=abar_r[:, :], in0=turns[:, :], scalar=1.0, in1=mag[:, :], op0=ALU.add, op1=ALU.mult).then_inc(lam_ready, 1)
                tt(abar_i[:, :], sine[:, :], mag[:, :], ALU.mult).then_inc(lam_ready, 1)
                dve.wait_ge(lam_ready, 2)

            def coefficients():
                tt, stt = dve.tensor_tensor, dve.scalar_tensor_tensor
                by_state = slice(SP_T * SN, LAM)
                re, im, mg, cm1, sn = (x[:, by_state] for x in (lam_re, lam_im, mag, turns, sine))
                den, t, nr, cr, ci, t2 = (st[:, i, :] for i in range(6))
                ni = abar_i[:, by_state]
                tt(den, re, re, ALU.mult).then_inc(prep, 1)
                tt(t, im, im, ALU.mult).then_inc(prep, 1)
                tt(nr, mg, cm1, ALU.mult).then_inc(prep, 1)
                dve.wait_ge(prep, 10)
                tt(den, den, t, ALU.add).then_inc(prep, 1)
                stt(out=nr, in0=mg, scalar=-1.0, in1=nr, op0=ALU.add, op1=ALU.add).then_inc(prep, 1)
                dve.wait_ge(prep, 12)
                dve.reciprocal(den, den).then_inc(prep, 1)
                tt(cr, nr, re, ALU.mult).then_inc(prep, 1)
                tt(t, ni, im, ALU.mult).then_inc(prep, 1)
                tt(ci, ni, re, ALU.mult).then_inc(prep, 1)
                tt(t2, nr, im, ALU.mult).then_inc(prep, 1)
                dve.wait_ge(prep, 17)
                tt(cr, cr, t, ALU.add).then_inc(prep, 1)
                tt(ci, ci, t2, ALU.subtract).then_inc(prep, 1)
                dve.wait_ge(prep, 19)
                tt(cr, cr, den, ALU.mult).then_inc(prep, 1)
                tt(ci, ci, den, ALU.mult).then_inc(prep, 1)
                dve.wait_ge(prep, 21)
                wide = lambda x: x.unsqueeze(2).to_broadcast([P, ST, 2 * SCH])
                c_r, c_i = c_st[:, 0, :, :], c_st[:, 1, :, :]
                dve.wait_ge(mix_in, 16 * MIX_LOADS)
                tt(c_pow[:, :, 0, 0, :], c_r, wide(cr), ALU.mult).then_inc(prep, 1)
                tt(t_c[0][:, :, :], c_i, wide(ci), ALU.mult).then_inc(prep, 1)
                tt(c_pow[:, :, 1, 0, :], c_r, wide(ci), ALU.mult).then_inc(prep, 1)
                tt(t_c[1][:, :, :], c_i, wide(cr), ALU.mult).then_inc(prep, 1)
                dve.wait_ge(prep, 25)
                tt(c_pow[:, :, 0, 0, :], c_pow[:, :, 0, 0, :], t_c[0][:, :, :], ALU.subtract).then_inc(c_ready, 1)
                stt(out=c_pow[:, :, 1, 0, :], in0=c_pow[:, :, 1, 0, :], scalar=-1.0, in1=t_c[1][:, :, :],
                    op0=ALU.mult, op1=ALU.subtract).then_inc(c_ready, 1)
                ar, ai = wide(abar_r[:, by_state]), wide(abar_i[:, by_state])
                for k in range(BT):
                    r, n, r2, n2 = (c_pow[:, :, c, i, :] for i in (k, k + 1) for c in (0, 1))
                    dve.wait_ge(c_ready, 2 * k + 2)
                    tt(r2, r, ar, ALU.mult).then_inc(prep, 1)
                    tt(t_c[0][:, :, :], n, ai, ALU.mult).then_inc(prep, 1)
                    tt(n2, n, ar, ALU.mult).then_inc(prep, 1)
                    tt(t_c[1][:, :, :], r, ai, ALU.mult).then_inc(prep, 1)
                    dve.wait_ge(prep, 25 + 4 * k + 4)
                    tt(r2, r2, t_c[0][:, :, :], ALU.add).then_inc(c_ready, 1)
                    tt(n2, n2, t_c[1][:, :, :], ALU.subtract).then_inc(c_ready, 1)

            def phases(p0):
                tt, stt = dve.tensor_tensor, dve.scalar_tensor_tensor
                by_state = slice(SP_T * SN, LAM)
                pc, ps, mg, t, u = (st[:, 6 + i, :] for i in range(5))
                dve.tensor_scalar(pc, turns[:, by_state], 1.0, None, ALU.add).then_inc(prep, 1)
                dve.tensor_copy(ps, sine[:, by_state]).then_inc(prep, 1)
                dve.tensor_copy(mg, mag[:, by_state]).then_inc(prep, 1)
                dve.wait_ge(prep, p0 + 3)
                dve.memset(phase[:, 0, :, 0:1], 1.0).then_inc(prep, 1)
                dve.memset(phase[:, 1, :, 0:1], 0.0).then_inc(prep, 1)
                p0 += 5
                levels = NB.bit_length() - 1
                for k in range(3 + levels):
                    if k >= 3:
                        n = 1 << (k - 3)
                        dve.wait_ge(prep, p0)
                        wc, ws = (x.unsqueeze(2).to_broadcast([P, ST, n]) for x in (pc, ps))
                        c0, s0, c1, s1 = (phase[:, c, :, i:i + n] for i in (0, n) for c in (0, 1))
                        t0, t1 = (x[:, :, 0:n] for x in t_c)
                        tt(c1, c0, wc, ALU.mult).then_inc(prep, 1)
                        tt(t0, s0, ws, ALU.mult).then_inc(prep, 1)
                        tt(s1, s0, wc, ALU.mult).then_inc(prep, 1)
                        tt(t1, c0, ws, ALU.mult).then_inc(prep, 1)
                        dve.wait_ge(prep, p0 + 4)
                        tt(c1, c1, t0, ALU.subtract).then_inc(prep, 1)
                        tt(s1, s1, t1, ALU.add).then_inc(prep, 1)
                        p0 += 6
                    dve.wait_ge(prep, p0)
                    tt(t, ps, ps, ALU.mult).then_inc(prep, 1)
                    tt(u, pc, pc, ALU.mult).then_inc(prep, 1)
                    stt(out=ps, in0=pc, scalar=2.0, in1=ps, op0=ALU.mult, op1=ALU.mult).then_inc(prep, 1)
                    dve.wait_ge(prep, p0 + 3)
                    tt(pc, u, t, ALU.subtract).then_inc(prep, 1)
                    p0 += 4
                    if k < 3:
                        tt(mg, mg, mg, ALU.mult).then_inc(prep, 1)
                        p0 += 1
                dve.wait_ge(prep, p0)

            def pooling():
                tt, stt = dve.tensor_tensor, dve.scalar_tensor_tensor
                steps = 0
                for g, w in enumerate(WINDOWS):
                    r = MIN_R0 + SP_T + g
                    dve.wait_ge(bank_free[r % 2], free_before(MIX, r) + 1)
                    if g:
                        dve.wait_ge(pooled, 2 * g)
                    u = u_all[:, g, :]
                    src, n, i = u, 1, 0
                    while n < w:
                        dst = run[i][:, :]
                        tt(dst[:, n:T], src[:, n:T], src[:, 0:T - n], ALU.add).then_inc(pool_step, 1)
                        dve.tensor_copy(dst[:, 0:n], src[:, 0:n]).then_inc(pool_step, 1)
                        steps += 2
                        dve.wait_ge(pool_step, steps)
                        src, n, i = dst, 2 * n, 1 - i
                    start = run[i]
                    tt(start[:, 0:16], src[:, 0:16], mpar[:, INV_C + 16 * g:INV_C + 16 * g + 16], ALU.mult).then_inc(pool_step, 1)
                    steps += 1
                    dve.wait_ge(pool_step, steps)
                    tt(u[:, 0:16], start[:, 0:16], u[:, 0:16], ALU.subtract).then_inc(pooled, 1)
                    stt(out=u[:, 16:T], in0=src[:, 16:T], scalar=1.0 / w, in1=u[:, 16:T], op0=ALU.mult, op1=ALU.subtract)\
                        .then_inc(pooled, 1)

            def states():
                tt = dve.tensor_tensor
                V = (*S_BANK, *T_BANK)
                half = ST // 2
                dve.wait_ge(v_done, 4)
                dve.memset(before_r[:, :, 0:1], 0.0).then_inc(zeroed, 1)
                dve.memset(before_i[:, :, 0:1], 0.0).then_inc(zeroed, 1)
                for k in range(4):
                    v = V[k][:, :].rearrange("p (c q b) -> p c q b", c=2, b=NB)
                    vr, vi = v[:, 0, :, :], v[:, 1, :, :]
                    c, s, sr, si = (x[:, k:ST:4, :] for x in (phase[:, 0, :, :], phase[:, 1, :, :], s_r, s_i))
                    t0, t1 = (x[:, k % 2 * 4:k % 2 * 4 + 4, :] for x in t_s)
                    if k >= 2:
                        dve.wait_ge(turn_step, 6 * (k - 1))
                    tt(sr, vr, c, ALU.mult).then_inc(turn_step, 1)
                    tt(t0, vi, s, ALU.mult).then_inc(turn_step, 1)
                    tt(si, vi, c, ALU.mult).then_inc(turn_step, 1)
                    tt(t1, vr, s, ALU.mult).then_inc(turn_step, 1)
                    dve.wait_ge(turn_step, 6 * k + 4)
                    tt(sr, sr, t0, ALU.add).then_inc(turn_step, 1)
                    tt(si, si, t1, ALU.subtract).then_inc(turn_step, 1)
                mg = st[:, 8, :]
                dve.wait_ge(turn_step, V_READ)
                for h in range(2):
                    for m in range(h * half, (h + 1) * half):
                        for x in (s_r, s_i):
                            dve.tensor_tensor_scan(x[:, m, :], mg[:, m:m + 1].to_broadcast([P, NB]), x[:, m, :], 0.0,
                                                   ALU.mult, ALU.add).then_inc(turn_step, 1)
                    ms = slice(h * half, (h + 1) * half)
                    c, s = phase[:, 0, ms, :], phase[:, 1, ms, :]
                    sr, si = s_r[:, ms, :], s_i[:, ms, :]
                    t0, t1 = t_s[0][:, :, :], t_s[1][:, :, :]
                    dr, di = before_r[:, ms, 1:NB + 1], before_i[:, ms, 1:NB + 1]
                    t_n = V_READ + (2 * half + 4) * h
                    dve.wait_ge(turn_step, t_n + 2 * half)
                    if h:
                        dve.wait_ge(state_ready, 2)
                    tt(dr, sr, c, ALU.mult).then_inc(turn_step, 1)
                    tt(t0, si, s, ALU.mult).then_inc(turn_step, 1)
                    tt(di, si, c, ALU.mult).then_inc(turn_step, 1)
                    tt(t1, sr, s, ALU.mult).then_inc(turn_step, 1)
                    dve.wait_ge(turn_step, t_n + 2 * half + 4)
                    tt(dr, dr, t0, ALU.subtract).then_inc(state_ready, 1)
                    tt(di, di, t1, ALU.add).then_inc(state_ready, 1)

            def mixer():
                n0 = MIX * 2
                dve.wait_ge(lam_in, 16)
                dve.memset(rms_eps[:, :], RMS_EPS).then_inc(rms_set, 1)
                dve.wait_ge(mix_in, 16 * MIX_LOADS)
                rms(n0, 0, rstd, xn)
                eigenvalues()
                coefficients()
                phases(25 + 4 * BT)
                pooling()
                states()
                Y = (Y_BANK, O_BANK, S_BANK[0], S_BANK[1])
                for q in range(SP_T):
                    dve.wait_ge(y_done, q + 1)
                    dve.scalar_tensor_tensor(out=yg[:, q, :], in0=u_all[:, SP_T + q, :], scalar=mpar[:, SKIP_C + q:SKIP_C + q + 1],
                                             in1=Y[q][:, :], op0=ALU.mult, op1=ALU.add).then_inc(y_skip, 1)
                for q in range(SP_T):
                    dve.wait_ge(yg_hi_s, q + 1)
                    dve.tensor_tensor(yg_lo[:, q, :], yg[:, q, :], yg_hi[:, q, :].bitcast(F32), ALU.subtract).then_inc(yg_lo_s, 1)

                def mix_low(m):
                    dve.wait_ge(mix_hi_s, m + 1)
                    dve.tensor_tensor(mix_lo[:, m, :], u_all[:, m, :], mix_hi[:, m, :].bitcast(F32), ALU.subtract)\
                        .then_inc(mix_lo_s, 1)

                for m in range(SP_T):
                    mix_low(m)
                for m in range(SP_T):
                    dve.wait_ge(bank_free[m % 2], free_before(MIX, GLU_R0 + m) + 1)
                    dve.tensor_tensor(u_all[:, SP_T + m, :], yg[:, m, :], glu_sig[m % 2][:, :], ALU.mult).then_inc(y_ssm, 1)
                for m in range(SP_T, KT):
                    mix_low(m)
                for m in range(KT):
                    unit_result(MIX, MOUT_U0 + m)
                    dve.tensor_tensor(z[:, m, :], z[:, m, :], U_BANK[m % 2][:, :], ALU.add).then_inc(bank_free[m % 2], 1)
                rms(n0 + 1, 1, rstd_2, xn_2)
                with dve.Fori(0, FT // 2) as j:
                    for c in range(2):
                        unit_result(MIX, GU_U0 + 2 * c + 1, j * 4)
                        dve.wait_ge(bank_free[0], free_before(MIX, GU_R0 + 2 * c, j * 2) + 1)
                        dve.tensor_tensor(hidden[c][:, :], U_BANK[1][:, :], silu[c][:, :], ALU.mult).then_inc(bank_free[1], 1)
                        dve.wait_ge(gu_hi, j * 2 + (c + 1))
                        g = bass.ds(j * 2 + c, 1)
                        dve.tensor_tensor(g_lo[:, g, :].rearrange("p s n -> p (s n)"), hidden[c][:, :],
                                          g_hi[:, g, :].rearrange("p s n -> p (s n)").bitcast(F32), ALU.subtract).then_inc(gu_lo, 1)
                done = 0
                for m in range(KT):
                    last = (m + 1) * FT - 1
                    if last % UT == UT - 1:
                        unit_result(MIX, MDOWN_U0 + last // UT)
                    else:
                        done += 1
                        dve.wait_ge(mid_done, MIX * LAYER_M + (MDOWN_M0 + done))
                    dve.tensor_tensor(z[:, m, :], z[:, m, :], U_BANK[m % 2][:, :], ALU.add).then_inc(bank_free[m % 2], 1)
                rms(n0 + 2, 2, rstd_3, None)

            for b in range(2):
                dve.sem_inc(s_free[b], 1)
            dve.sem_inc(ot_read, 2)
            dve.sem_inc(o_norm, 4)
            dve.memset(mean_w[:, :], 1.0 / D).then_inc(consts_set, 1)
            dve.memset(ln_eps[:, :], LN_EPS).then_inc(consts_set, 1)
            dve.memset(gn_eps[:, :], GN_EPS).then_inc(consts_set, 1)
            for k in range(KT):
                dve.wait_ge(x_hi, k + 1)
                dve.tensor_tensor(xl[:, k, :], z[:, k, :], xh[:, k, :].bitcast(F32), ALU.subtract).then_inc(x_lo, 1)
            dve.wait_ge(decay_step, 3)
            flat = decay[:, :, :].rearrange("p d n -> p (d n)")
            dve.tensor_scalar(decay_b[:, :], flat, 0.0, None, ALU.min).then_inc(decay_step, 1)
            dve.wait_ge(decay_step, 4)
            dve.tensor_tensor(flat, decay_b[:, :], decay_a[:, :], ALU.subtract).then_inc(decay_step, 1)
            dve.wait_ge(decay_step, 5)
            with dve.Fori(0, DEPTH) as L:
                dve.wait_ge(tables_in, L * 48 + 48)
                stand(dve, dve_passed)
                with dve.Fori(0, 4) as t:
                    attention(L, t)
                split_branch_inputs(L)
                with dve.Fori(0, 2) as i:
                    branches(L, i)
                residual_out(L)
                norm(L, 0)
                ple(L)
                with dve.Fori(0, FT // 2) as j:
                    up(L, j)
                residual_down(L)
                norm(L, 1)
            mixer()


def weight_tiles(w):
    import numpy as np
    k, m = w.shape
    return np.ascontiguousarray(w.reshape(k // P, P, m // P, P).transpose(0, 2, 1, 3))


def layer_stream(inp, i):
    w_in, w_a, w_b, w_o, w_up, w_dn, w_pg, w_pp = (
        weight_tiles(inp[n][i]) for n in
        ("w_in", "w_branch_a", "w_branch_b", "w_out", "w_up", "w_down", "w_ple_gate", "w_ple_proj"))
    col = lambda w, m: [w[k, m] for k in range(w.shape[0])]
    q_na, k_na, v_na, q_r, k_r, v_r, g_r, gate = 0, 4, 8, 12, 16, 20, 28, 36
    out = []
    for t in range(4):
        for m in (q_na + t, k_na + t, v_na + t, q_r + t, k_r + t, v_r + 2 * t, v_r + 2 * t + 1,
                  g_r + 2 * t, g_r + 2 * t + 1, gate + 3 * t, gate + 3 * t + 1, gate + 3 * t + 2):
            out += col(w_in, m)
    for h in range(2):
        for g in range(2):
            out += col(w_in, gate + 12 + 2 * h + g)
        for w in (w_a, w_b):
            for m in range(4):
                out += col(w, 4 * h + m)
    for m in range(KT):
        out += col(w_o, m)
    for h in range(2):
        for w in (w_pg, w_pp):
            for m in range(4):
                out += col(w, 4 * h + m)
    for j in range(FT):
        out += col(w_up, j) + col(w_up, FT + j)
    for m in range(KT):
        out += col(w_dn, m)
    return out


def mixer_stream(inp):
    w_in, w_glu, w_o, w_g, w_up, w_dn = (
        weight_tiles(inp[n + "_2"][0]) for n in ("w_in", "w_glu", "w_out", "w_gate", "w_up", "w_down"))
    col = lambda w, m: [w[k, m] for k in range(w.shape[0])]
    out = []
    for m in range(KT):
        out += col(w_in, (m + SP_T) % KT)
    for m in range(SP_T):
        out += col(w_glu, m)
    for m in range(KT):
        out += col(w_o, m)
    for j in range(FT):
        out += col(w_g, j) + col(w_up, j)
    for m in range(KT):
        out += col(w_dn, m)
    return out


def unit_array(tiles):
    import numpy as np
    w = np.stack(tiles)
    return np.ascontiguousarray(w.reshape(-1, UT, P, P).transpose(0, 2, 1, 3)).reshape(-1, P, UT * P)


def feature_major(v):
    import numpy as np
    return np.ascontiguousarray(np.moveaxis(v.reshape(*v.shape[:-1], -1, P), -1, 0))


def layout(inp):
    import numpy as np
    f32 = np.float32
    a = {}
    tiles = []
    for i in range(DEPTH):
        tiles += layer_stream(inp, i)
    tiles += mixer_stream(inp)
    a["w"] = unit_array(tiles)
    a["x"] = np.ascontiguousarray(inp["x"][0].T.reshape(KT, P, T).transpose(1, 0, 2))
    a["p"] = np.ascontiguousarray(inp["p"][:, 0].transpose(0, 2, 1).reshape(DEPTH, PLE_T, P, T).transpose(0, 2, 1, 3))
    a["lnp"] = feature_major(np.stack([inp["ln1_g"], inp["ln1_b"], inp["ln2_g"], inp["ln2_b"]], 1))
    a["convp"] = feature_major(np.concatenate([inp["conv_w"], inp["conv_b"][:, None]], 1))
    rates = np.stack([inp["ret_decay_f"].reshape(-1), inp["ret_decay_b"].reshape(-1)])
    a["decay"] = np.ascontiguousarray(np.broadcast_to(rates[None], (P, 2, DEPTH * RET_H)))
    rows, cols = np.arange(ROWS), np.arange(16)
    dr = rows[None, :] - rows[:, None] + WIN_ROWS - 1
    dc = 16 * np.arange(3)[None, :, None] - 16 + cols[None, None, :] - cols[:, None, None] + WIN_COLS - 1
    table = np.pad(inp["na_rpb"], ((0, 0), (0, 0), (0, 0), (16, 16)))
    spread = table[:, :, dr[:, None, None, :, None], dc[None, :, :, None, :] + 16]
    a["bias"] = np.ascontiguousarray(spread.reshape(DEPTH, 4, 2, P, 3 * P).transpose(0, 1, 3, 2, 4)).reshape(DEPTH * 4, P, 6 * P)
    a["ident"] = np.eye(P, dtype=f32)
    half = RET_DK // 2
    sw = np.zeros((P, P), f32)
    sw[np.arange(half) + half, np.arange(half)] = 1.0
    sw[np.arange(half), np.arange(half) + half] = 1.0
    a["swap"] = sw
    inv = f32(10000.0) ** (-np.arange(half, dtype=f32) / f32(half))
    ang = np.arange(T, dtype=f32)[None, :] * inv[:, None]
    c, s = np.cos(ang), np.sin(ang)
    a["rope"] = np.ascontiguousarray(np.stack([np.concatenate([c, c]), np.concatenate([-s, s])], 1).astype(f32))
    a["delta"] = (np.arange(7 * P)[None, :] - 3 * P - np.arange(P)[:, None]).astype(f32)
    masks = np.zeros((P, 3, 3, ROWS, 16), f32)
    for m, j in enumerate((0, 1, CB - 1)):
        q = 16 * j + cols
        first = np.clip(q - WIN_COLS // 2, 0, GRID_W - WIN_COLS)
        key = 16 * (j - 1) + 16 * np.arange(3)[:, None] + cols[None, :]
        ok = (key[None] >= first[:, None, None]) & (key[None] < first[:, None, None] + WIN_COLS)
        neg = np.where(ok, 0.0, -1e30).astype(f32)
        masks[:, m] = np.tile(neg, (ROWS, 1, 1))[:, :, None, :]
    a["masks"] = masks.reshape(P, 3, 3 * P)
    two = SG // ST
    by_channel = lambda v: np.repeat(v.reshape(SP_T, P // SCH, SN), SCH, 1).transpose(1, 0, 2).reshape(P, SP_T * SN)
    by_state = lambda v: v.reshape(ST, two * SN).T
    re, im = inp["lam_re_2"][0], inp["lam_im_2"][0]
    log_dt = np.repeat(inp["log_dt_2"][0][:, None], SN, 1)
    a["lam"] = np.stack([np.concatenate([by_channel(v), by_state(v)], 1) for v in (re, im, log_dt)], 1)
    b_cs = np.stack([inp["b_re_2"][0], inp["b_im_2"][0]])
    a["w_b"] = b_cs.reshape(2, SP_T, P // SCH, SN, SCH).transpose(2, 4, 0, 1, 3).reshape(P, 2, SP_T, SN)
    apart = np.zeros((two, SN, 2, ST, two, SCH), f32)
    for h in range(two):
        apart[h, :, :, :, h] = b_cs.reshape(2, ST, two, SN, SCH)[:, :, h].transpose(2, 0, 1, 3)
    a["b_st"] = apart.reshape(P, 2, ST, two * SCH)
    c_cs = np.stack([inp["c_re_2"][0], inp["c_im_2"][0]])
    apart = np.zeros((two, SN, 2, ST, two, SCH), f32)
    for h in range(two):
        apart[h, :, :, :, h] = c_cs.reshape(2, ST, two, SCH, SN)[:, :, h].transpose(3, 0, 1, 2)
    a["c_st"] = apart.reshape(P, 2, ST, two * SCH)
    a["w_pool"] = inp["w_pool_2"][0].transpose(1, 0, 2)
    part = np.arange(P)[:, None]
    counts = [np.broadcast_to((f32(1.0) / np.minimum(np.arange(1, 17), w).astype(f32))[None], (P, 16)) for w in WINDOWS]
    cols = [feature_major(v) for v in (inp["norm_mix_2"][0], inp["norm_ffn_2"][0], inp["norm_final_2"], inp["pool_scale_2"][0],
                                       inp["d_skip_2"][0].reshape(-1), inp["b_glu_2"][0])]
    a["mpar"] = np.concatenate(cols + [(part // SCH % 2 == np.arange(2)).astype(f32),
                                       (part // (2 * SCH) == np.arange(4)).astype(f32)] + counts, 1)
    return {n: np.ascontiguousarray(v) for n, v in a.items()}


def kernel(**inputs):
    import numpy as np
    import concourse.bacc as bacc
    from concourse.bass_utils import run_bass_kernel_spmd

    arrays = layout({n: np.asarray(v) for n, v in inputs.items()})
    nc = bacc.Bacc("TRN2", target_bir_lowering=False, num_devices=1)
    dram = {n: nc.dram_tensor(f"in_{n}", v.shape, F32, kind="ExternalInput").ap() for n, v in arrays.items()}
    out = nc.dram_tensor("out_x", (P, KT, T), F32, kind="ExternalOutput").ap()
    build(nc, dram, out)
    r = run_bass_kernel_spmd(nc, [{f"in_{n}": v for n, v in arrays.items()}], core_ids=[0])
    got = r.results[0]["out_x"]
    return np.ascontiguousarray(got.transpose(1, 0, 2).reshape(D, T).T).reshape(1, T, D)
```

```python
import concourse.bass as bass
from concourse import mybir
from contextlib import ExitStack

F32 = mybir.dt.float32
F32R = mybir.dt.float32r
ALU = mybir.AluOpType
ACT = mybir.ActivationFunctionType

P = 128
T = 512
D = 1024
KT = D // P
DEPTH = 2
GRID_W, ROWS, WIN_ROWS, WIN_COLS = 64, 8, 8, 16
NA_HEADS, NA_DH = 8, 64
CB = GRID_W // 16
RET_H, RET_DK, RET_DV = 4, 128, 256
FF = 2816
FT = FF // P
PLE_T = 2
ALPHA = (2.0 * DEPTH) ** 0.25
LN_EPS, GN_EPS, RMS_EPS = 1e-5, 1e-6, 1e-6
RING = 4
UT = 8

ATT_U, BR_U, OUT_U, PLE_U, UP_U, DOWN_U = 4 * 12, 2 * 8, 8, 10, 2 * FT, FT
ATT0 = 0
BR0 = ATT0 + ATT_U
OUT0 = BR0 + BR_U
PLE0 = OUT0 + OUT_U
UP0 = PLE0 + PLE_U
DOWN0 = UP0 + UP_U
LAYER_U = DOWN0 + DOWN_U
ATT_R0 = 0
BR_R0 = ATT_R0 + 48
OUT_R0 = BR_R0 + 20
PLE_R0 = OUT_R0 + 8
UP_R0 = PLE_R0 + 16
DOWN_R0 = UP_R0 + 44
LAYER_R = DOWN_R0 + 8
BR_M0 = 0
PLE_M0 = BR_M0 + 4
DOWN_M0 = PLE_M0 + 6
LAYER_M = DOWN_M0 + 6
MIX = DEPTH
MIN_U0, GLU_U0, MOUT_U0, GU_U0 = 0, 8, 10, 18
MDOWN_U0 = GU_U0 + UP_U
MIX_U = MDOWN_U0 + DOWN_U
MIN_R0, GLU_R0, MOUT_R0, GU_R0 = 0, 8, 12, 20
MDOWN_R0 = GU_R0 + UP_U
GLU_M0, MDOWN_M0 = 0, 2
N_UNITS = DEPTH * LAYER_U + MIX_U
MIX_LOADS = 4
WINDOWS = (2, 4, 8, 16)
SP_T = 4
SG, SCH, SN = 32, 16, 64
ST = SG * SN // P
BT = 2
NB = T // BT
LAM = SP_T * SN + ST
NORM_C, POOLS_C, SKIP_C, BGLU_C, HALF_C, QUART_C, INV_C = 0, 24, 28, 32, 36, 38, 42
MPAR = INV_C + SP_T * 16
LEVELS = NB.bit_length() - 1
QUARTER = 1.5707963267948966
QUARTER_HI = 1.5703125
QUARTER_MID = 0.00048375129699707031
QUARTER_LO = QUARTER - QUARTER_HI - QUARTER_MID
LN2 = 0.6931471805599453
LN2_HI = 0.693359375
LN2_LO = LN2 - LN2_HI
ROUND = 1.5 * 2.0 ** 23
EXP_MAX, EXP_MIN = 88.0, -87.0
EXP_C = [1 / 5040, 1 / 720, 1 / 120, 1 / 24, 1 / 6, 1 / 2, 1.0]
SIN_C = [1 / 362880, -1 / 5040, 1 / 120, -1 / 6]
COS_C = [-1 / 3628800, 1 / 40320, -1 / 720, 1 / 24, -1 / 2]


def build(nc, a, out):
    ctx = ExitStack()
    with ctx:
        at = [nc.sbuf_base]

        def place(name, shape, dt=F32, offset=None):
            size = 4
            for s in shape[1:]:
                size *= s
            if offset is None:
                offset, at[0] = at[0], at[0] + (size + 31) // 32 * 32
            return nc.alloc_sbuf_tensor_at(name, shape, dt, offset=offset)

        def sem(name):
            return ctx.enter_context(nc.semaphore(name))

        at[0] = (at[0] + 31) // 32 * 32
        stage = [place(f"stage{i}", [P, UT, P]) for i in range(RING)]
        w_hi = [place(f"w_hi{i}", [P, UT, P], F32R) for i in range(RING)]
        w_lo = [place(f"w_lo{i}", [P, UT, P], F32R) for i in range(RING)]
        xh = place("xh", [P, KT, T], F32R)
        xl = place("xl", [P, KT, T], F32R)
        z_at = at[0]
        z = place("z", [P, KT, T])
        ident = place("ident", [P, P])
        swap = place("swap", [P, P])
        mean_w = place("mean_w", [P, P])
        ln_eps = place("ln_eps", [P, 1])
        warm = place("warm", [P, 1])
        gn_eps = place("gn_eps", [P, 1])
        lnp = place("lnp", [P, DEPTH, 4, KT])
        convp = place("convp", [P, DEPTH, 4, 2 * FT])
        decay = place("decay", [P, 2, DEPTH * RET_H])
        decay_a = place("decay_a", [P, 2 * DEPTH * RET_H])
        decay_b = place("decay_b", [P, 2 * DEPTH * RET_H])
        at[0] = (at[0] + 31) // 32 * 32
        c_at = at[0]
        rope = place("rope", [P, 2, T])
        delta = place("delta", [P, 7 * P])
        masks = place("masks", [P, 3, 3 * P])
        conv_a = [place(f"conv_a{i}", [P, T], offset=c_at + 2048 * i) for i in range(2)]
        conv_b = [place(f"conv_b{i}", [P, T], offset=c_at + 4096 + 2048 * i) for i in range(2)]
        a_at = at[0]
        gates = place("gates", [P, 16, T])
        merged_p = place("merged_p", [P, 16, T], F32R, offset=a_at)
        yb = place("yb", [P, KT, T])
        yb_lo = place("yb_lo", [P, KT, T], F32R, offset=a_at + 32768)
        ya = place("ya", [P, 4, T])
        ya_lo = place("ya_lo", [P, 4, T], F32R, offset=a_at + 49152)
        tmp_at = at[0]
        yb_hi = place("yb_hi", [P, KT, T], F32R)
        ya_hi = place("ya_hi", [P, 4, T], F32R)
        p_at = at[0]
        p_raw = place("p_raw", [P, PLE_T, T])
        p_hi = place("p_hi", [P, PLE_T, T], F32R, offset=a_at)
        p_lo = place("p_lo", [P, PLE_T, T], F32R, offset=a_at + 4096)
        s_t = place("s_t", [P, 8, 3 * P], offset=z_at)
        pr = place("pr", [P, 4, T], offset=z_at)
        bias = place("bias", [P, 2, 3 * P], offset=z_at + 12288)
        na_q = place("na_q", [P, T], offset=tmp_at)
        na_k = place("na_k", [P, T], offset=tmp_at + 2048)
        na_v = place("na_v", [P, CB, P], offset=tmp_at + 4096)
        r_q = place("r_q", [P, T], offset=tmp_at + 6144)
        r_k = place("r_k", [P, T], offset=tmp_at + 8192)
        r_tmp = place("r_tmp", [P, T], offset=tmp_at + 10240)
        r_v = place("r_v", [P, 4, RET_DV], offset=tmp_at + 12288)
        sg = place("sg", [P, 2, T], offset=tmp_at + 16384)
        pt = place("pt", [P, 2, 3 * P], offset=tmp_at + 20480)
        o_n = place("o_n", [P, 4, RET_DV], offset=tmp_at + 23552)
        d_tmp = place("d_tmp", [P, 7 * P], offset=tmp_at + 23552)
        d_tab = place("d_tab", [P, 7 * P])
        m_tmp = [place(f"m_tmp{i}", [P, T], offset=z_at + 2048 * i) for i in range(2)]
        sq = [place(f"sq{i}", [P, T], offset=a_at + 8192 + 2048 * i) for i in range(4)]
        rstd = place("rstd", [P, T], offset=a_at + 16384)
        p_sig = [place(f"p_sig{i}", [P, T], offset=a_at + 18432 + 2048 * i) for i in range(4)]
        g_hi = place("g_hi", [P, FT, T], F32R, offset=a_at)
        g_lo = place("g_lo", [P, FT, T], F32R, offset=a_at + FT * T * 4)
        at[0] = max(at[0], a_at + 2 * FT * T * 4)
        abar = place("abar", [P, 2, SP_T, SN])
        st = place("st", [P, 10, ST])
        powers = place("powers", [P, LEVELS, 2, ST])
        mpar = place("mpar", [P, MPAR])
        rms_eps = place("rms_eps", [P, 1])
        dt = place("dt", [P, 4, SP_T + ST])
        assert at[0] <= nc.sbuf_usable_end, (at[0], nc.sbuf_usable_end)
        eig = [place(f"eig{i}", [P, LAM], offset=a_at + 16384 + LAM * 4 * i) for i in range(8)]
        lam = place("lam", [P, 2, LAM], offset=a_at + 16384 + LAM * 32)
        int_at = a_at + 16384 + LAM * 40
        eig_tmp = place("eig_tmp", [P, LAM], offset=a_at + 16384 + LAM * 48)
        exp2 = place("exp2", [P, LAM], mybir.dt.int32, offset=int_at)
        exp2_dt = place("exp2_dt", [P, SP_T + ST], mybir.dt.int32, offset=int_at + LAM * 4)
        phase = place("phase", [P, 2, ST, NB], offset=c_at)
        u_all = place("u_all", [P, KT, T], offset=c_at + 32768)
        mix_lo = place("mix_lo", [P, KT, T], F32R, offset=c_at + 32768)
        w_b = place("w_b", [P, BT, 2, SP_T, SN], offset=c_at + 49152)
        t_p = place("t_p", [P, 4, NB], offset=c_at + 49152)
        w_b2 = place("w_b2", [P, BT, 2, SP_T, 2, SN], offset=c_at + 53248)
        phase_tp = place("phase_tp", [P, ST, NB // 2], offset=c_at + 53248)
        c_pow = place("c_pow", [P, ST, 2, BT + 1, 2 * SCH], offset=c_at + 61440)
        phase_td = place("phase_td", [P, ST, NB // 2], offset=c_at + 61440)
        k_conv = place("k_conv", [P, SP_T, BT, P], offset=c_at + 73728)
        b_st = place("b_st", [P, 2, ST, 2 * SCH], offset=c_at + 77824)
        c_st = place("c_st", [P, 2, ST, 2 * SCH], offset=c_at + 81920)
        t_c = [place(f"t_c{i}", [P, ST, 2 * SCH], offset=c_at + 86016 + 2048 * i) for i in range(2)]
        run = [place(f"run{i}", [P, T], offset=c_at + 90112 + 2048 * i) for i in range(2)]
        w_pool = place("w_pool", [P, SP_T, P], offset=c_at + 94208)
        t_s = place("t_s", [P, 4, NB], offset=c_at + 96256)
        yg = place("yg", [P, SP_T, T], offset=c_at)
        yg_hi = place("yg_hi", [P, SP_T, T], F32R, offset=c_at + 8192)
        yg_lo = place("yg_lo", [P, SP_T, T], F32R, offset=c_at + 16384)
        glu_sig = [place(f"glu_sig{i}", [P, T], offset=c_at + 24576 + 2048 * i) for i in range(2)]
        mix_hi = place("mix_hi", [P, KT, T], F32R, offset=c_at + 49152)
        sq_1 = [place(f"sq_1{i}", [P, T], offset=c_at + 32768 + 2048 * i) for i in range(4)]
        xn_1 = [place(f"xn_1{i}", [P, T], offset=c_at + 40960 + 2048 * i) for i in range(4)]
        rstd_1 = place("rstd_1", [P, T], offset=c_at + 96256)
        sq_2 = [place(f"sq_2{i}", [P, T], offset=c_at + 65536 + 2048 * i) for i in range(4)]
        xn_2 = [place(f"xn_2{i}", [P, T], offset=c_at + 2048 * i) for i in range(4)]
        rstd_2 = place("rstd_2", [P, T], offset=c_at + 98304)
        xh_at = z_at - 2 * KT * T * 4
        sq_3 = [place(f"sq_3{i}", [P, T], offset=c_at + 2048 * i) for i in range(4)]
        out_t = place("out_t", [P, KT, T], offset=xh_at)
        rstd_3 = place("rstd_3", [P, T], offset=xh_at + KT * T * 4)
        states = [place("states0", [P, 2, 4, NB], offset=c_at + 81920)]
        states += [place(f"states{q}", [P, 2, 4, NB], offset=xh_at + 8192 * (q - 1)) for q in range(1, SP_T)]
        silu = [place(f"silu{i}", [P, T], offset=c_at + 2048 * i) for i in range(2)]
        hidden = [place(f"hidden{i}", [P, T], offset=c_at + 4096 + 2048 * i) for i in range(2)]
        small = place("small", [P, 64])
        row_max, row_nmax, row_sum, row_inv = (small[:, 8 * i:8 * i + 8] for i in range(4))
        gn_std, gn_inv = small[:, 32:36], small[:, 36:40]
        lg_now = small[:, 40:42]
        gn_st = place("gn_st", [P, 4, 6])
        gn_mv = place("gn_mv", [P, 4, 2])
        assert at[0] <= nc.sbuf_usable_end, (at[0], nc.sbuf_usable_end)

        psum = ctx.enter_context(nc.psum_tensor("psum", [P, 8, T], F32))
        bank = [psum[:, i, :] for i in range(8)]
        U_BANK, S_BANK, T_BANK, Y_BANK, O_BANK = bank[0:2], bank[2:4], bank[4:6], bank[6], bank[7]
        V_BANKS = psum[:, 2:6, :]

        landed = [sem(f"unit_landed{i}") for i in range(RING)]
        hi_done = sem("unit_hi_done")
        lo_done = sem("unit_lo_done")
        unit_used = sem("unit_used")
        mid_done = sem("mid_unit_result_done")
        bank_free = [sem(f"unit_bank_free{i}") for i in range(2)]
        params_in = sem("params_in")
        x_in = [sem(f"x_in{i}") for i in range(4)]
        consts_set = sem("consts_set")
        x_hi, x_lo = sem("x_hi"), sem("x_lo")
        decay_step = sem("decay_step")
        tables_in = sem("tables_in")
        bias_in = sem("bias_in")
        vt_done, v_ready = sem("v_turned"), sem("v_ready")
        dterm_copy = sem("decay_rates_copied")
        dterm, dtab_ready = sem("decay_terms"), sem("decay_table_ready")
        score_done = sem("score_done")
        s_free = [sem(f"score_bank_free{i}") for i in range(2)]
        masked, nmax_ready = sem("scores_masked"), sem("neg_max_ready")
        exp_done, inv_ready, p_ready = sem("exp_done"), sem("row_inverse"), sem("probs_ready")
        pt_done, pt_ready, pv_done = sem("probs_turned"), sem("probs_t_ready"), sem("pv_done")
        ya_ready = sem("ya_ready")
        rope_cos, rope_ready = sem("rope_cos"), sem("rope_ready")
        o_done, gn_stat, gn_aggr = sem("ret_out_done"), sem("gn_stats"), sem("gn_aggr")
        std_ready, ginv_ready, o_norm = sem("gn_std"), sem("gn_inv"), sem("ret_out_normed")
        ot_done, ot_read = sem("ret_out_turned"), sem("yb_ready")
        sig_ready = sem("silu_sigmoid")
        br_hi, br_lo = sem("branch_in_hi"), sem("branch_in_lo")
        merged, merged_hi, merged_lo = sem("merged"), sem("merged_hi"), sem("merged_lo")
        z_ready, mean_done, centred = sem("z_ready"), sem("mean_done"), sem("centred")
        squared, sq_used = sem("squared"), sem("square_used")
        lstd, lrstd, normed = sem("ln_std"), sem("ln_rstd"), sem("ln_normed")
        x_ready = sem("x_ready")
        p_in, p_hi_s, p_lo_s = sem("p_in"), sem("p_hi_done"), sem("p_lo_done")
        ple_term, zpre = sem("ple_term"), sem("z_pre_ready")
        conv_mid, conv_left = sem("conv_centre"), sem("conv_left")
        gelu_done, glu_done = sem("gelu_done"), sem("glu_done")
        g_hi_s, g_lo_s = sem("g_hi_done"), sem("g_lo_done")
        out_done = sem("out_done")
        mix_in = sem("mixer_params_in")
        lam_in = sem("eigenvalues_in")
        mpar_in = sem("mixer_small_params_in")
        prep, lam_step, powers_ready, c_ready = sem("ssm_prep_step"), sem("ssm_eigenvalue_step"), sem("ssm_phase_powers"), sem("ssm_c_powers")
        phase_c, phase_s, phase_step = sem("phase_cosines"), sem("phase_sines"), sem("phase_step")
        wb_step, wb_ready, wb_apart = sem("ssm_b_step"), sem("ssm_b_powers"), sem("ssm_b_apart")
        kernel_done, kernel_ready = sem("ssm_kernel_done"), sem("ssm_kernel_ready")
        pool_step, pooled, pool_done, y_pool = (sem("pool_step"), sem("pooled"), sem("pool_product"), sem("y_pool"))
        v_done, v_read, turn_step = sem("ssm_block_inputs"), sem("ssm_block_inputs_read"), sem("ssm_turn_step")
        scanned, re_taken, im_taken = sem("ssm_scanned"), sem("ssm_re_taken"), sem("ssm_im_taken")
        state_re, state_im = sem("ssm_state_re"), sem("ssm_state_im")
        y_done, y_skip, y_gelu = sem("ssm_y_done"), sem("ssm_y_skip"), sem("ssm_y_gelu")
        yg_hi_s, yg_lo_s, y_ssm = sem("yg_hi"), sem("yg_lo"), sem("y_ssm")
        mix_hi_s, mix_lo_s = sem("mix_hi"), sem("mix_lo")
        gu_hi, gu_lo = sem("hidden_hi"), sem("hidden_lo")
        rms_set = sem("rms_eps_set")
        pe_passed, dve_passed = sem("pe_passed"), sem("dve_passed")

        block = ctx.enter_context(nc.Block())

        def stand(eng, passed):
            eng.sem_inc(passed, 1)

        def block_view(ap):
            return ap.rearrange("p (r b c) -> p b r c", r=ROWS, b=CB)

        def kblocks(j):
            return range(1 if j == 0 else 0, 2 if j == CB - 1 else 3)

        def mask_of(j):
            return 0 if j == 0 else 2 if j == CB - 1 else 1

        def free_before(L, r, i=0):
            return L * (LAYER_R // 2) + i + r // 2 + 1

        def after_result(L, r, i=0):
            return bank_free[r % 2], free_before(L, r, i) + 1

        @block.sync
        def _(sp):
            def load(s, u):
                src = a["w"][u] if isinstance(u, int) else a["w"][bass.ds(u, 1)].rearrange("s p n -> p (s n)")
                sp.dma_start(stage[s][:, :, :].rearrange("p t n -> p (t n)"), src).then_inc(landed[s], 16)

            load(0, 0)
            for h in range(4):
                sp.dma_start(z[:, 2 * h:2 * h + 2, :], a["x"][:, 2 * h:2 * h + 2, :]).then_inc(x_in[h], 16)
                if h == 0:
                    load(1, 1)
            load(2, 2)
            load(3, 3)
            with sp.Fori(1, N_UNITS // RING) as n:
                for s in range(RING):
                    sp.wait_ge(lo_done, n * RING + (s - RING + 1))
                    load(s, n * RING + s)
            for h in range(2):
                sp.wait_ge(normed, (MIX * 2 + 2) * KT + (4 * h + 4))
                sp.dma_start(out[:, 4 * h:4 * h + 4, :], out_t[:, 4 * h:4 * h + 4, :]).then_inc(out_done, 16)
            sp.wait_ge(out_done, 32)

        @block.gpsimd
        def _(pool):
            def low_part(n, s):
                pool.wait_ge(hi_done, n * RING + (s + 1))
                pool.tensor_tensor(w_lo[s][:, :, :], stage[s][:, :, :], w_hi[s][:, :, :].bitcast(F32),
                                   ALU.subtract).then_inc(lo_done, 1)

            tt, ts = pool.tensor_tensor, pool.tensor_scalar
            lam_steps = [0]

            def step():
                lam_steps[0] += 1
                return lam_step, 1

            def settled():
                return lam_step, lam_steps[0]

            def two_ops(out, in0, scalar, in1, op0, op1):
                tmp = eig_tmp[:, 0:in0.shape[-1]]
                pool.wait_ge(*settled())
                ts(tmp, in0, scalar, None, op0).then_inc(*step())
                pool.wait_ge(*settled())
                tt(out, tmp, in1, op1).then_inc(*step())

            def exponential(dst, x, k, p, bits):
                ts(x, x, EXP_MAX, EXP_MIN, ALU.min, ALU.max).then_inc(*step())
                pool.wait_ge(*settled())
                ts(k, x, 1.0 / LN2, ROUND, ALU.mult, ALU.add).then_inc(*step())
                pool.wait_ge(*settled())
                ts(k, k, ROUND, None, ALU.subtract).then_inc(*step())
                pool.wait_ge(*settled())
                ts(bits, k, 127.0, 2.0 ** 23, ALU.add, ALU.mult).then_inc(*step())
                for part in (LN2_HI, LN2_LO):
                    two_ops(out=x, in0=k, scalar=-part, in1=x, op0=ALU.mult, op1=ALU.add)
                    pool.wait_ge(*settled())
                ts(p, x, EXP_C[0], None, ALU.mult).then_inc(*step())
                for c in EXP_C[1:]:
                    pool.wait_ge(*settled())
                    two_ops(out=p, in0=p, scalar=c, in1=x, op0=ALU.add, op1=ALU.mult)
                pool.wait_ge(*settled())
                two_ops(out=dst, in0=p, scalar=1.0, in1=bits.bitcast(F32), op0=ALU.add, op1=ALU.mult)
                pool.wait_ge(*settled())

            x, mag, angle, k, p, y, sine, cosm1 = (e[:, :] for e in eig)
            chans, by_state = slice(0, SP_T * SN), slice(SP_T * SN, LAM)
            per_q = lambda v: v.rearrange("p (q n) -> p q n", n=SN)

            def growth_and_angle():
                pool.wait_ge(lam_in, 32)
                exponential(dt[:, 3, :], dt[:, 0, :], dt[:, 1, :], dt[:, 2, :], exp2_dt[:, :])
                for part, dst in ((0, x), (1, angle)):
                    tt(per_q(dst[:, chans]), per_q(lam[:, part, chans]),
                       dt[:, 3, 0:SP_T].unsqueeze(2).to_broadcast([P, SP_T, SN]), ALU.mult).then_inc(*step())
                    tt(dst[:, by_state], lam[:, part, by_state], dt[:, 3, SP_T:SP_T + ST], ALU.mult).then_inc(*step())
                pool.wait_ge(*settled())

            def quarter_turns():
                ts(k, angle, 1.0 / QUARTER, ROUND, ALU.mult, ALU.add).then_inc(*step())
                pool.wait_ge(*settled())
                ts(k, k, ROUND, None, ALU.subtract).then_inc(*step())
                for part in (QUARTER_HI, QUARTER_MID, QUARTER_LO):
                    pool.wait_ge(*settled())
                    two_ops(out=angle, in0=k, scalar=-part, in1=angle, op0=ALU.mult, op1=ALU.add)
                ts(p, k, 0.25, ROUND, ALU.mult, ALU.add).then_inc(*step())
                pool.wait_ge(*settled())
                tt(y, angle, angle, ALU.mult).then_inc(*step())
                ts(p, p, ROUND, None, ALU.subtract).then_inc(*step())
                pool.wait_ge(*settled())
                two_ops(out=k, in0=p, scalar=-4.0, in1=k, op0=ALU.mult, op1=ALU.add)
                pool.wait_ge(*settled())

            def series():
                ts(p, y, SIN_C[0], None, ALU.mult).then_inc(*step())
                ts(x, y, COS_C[0], None, ALU.mult).then_inc(*step())
                for cs, cc in zip(SIN_C[1:], COS_C[1:]):
                    pool.wait_ge(*settled())
                    two_ops(out=p, in0=p, scalar=cs, in1=y, op0=ALU.add, op1=ALU.mult)
                    two_ops(out=x, in0=x, scalar=cc, in1=y, op0=ALU.add, op1=ALU.mult)
                pool.wait_ge(*settled())
                two_ops(out=x, in0=x, scalar=COS_C[-1], in1=y, op0=ALU.add, op1=ALU.mult)
                two_ops(out=angle, in0=p, scalar=1.0, in1=angle, op0=ALU.add, op1=ALU.mult)

            def turn():
                pool.wait_ge(*settled())
                tt(y, k, k, ALU.mult).then_inc(*step())
                pool.wait_ge(*settled())
                ts(p, y, -1.0 / 6, 7.0 / 6, ALU.mult, ALU.add).then_inc(*step())
                ts(eig_tmp[:, :], y, -1.0, 4.0, ALU.mult, ALU.add).then_inc(*step())
                pool.wait_ge(*settled())
                tt(y, y, p, ALU.mult).then_inc(*step())
                tt(k, k, eig_tmp[:, :], ALU.mult).then_inc(*step())
                pool.wait_ge(*settled())
                ts(y, y, -1.0, 1.0, ALU.mult, ALU.add).then_inc(*step())
                ts(k, k, 1.0 / 3, None, ALU.mult).then_inc(*step())
                pool.wait_ge(*settled())
                tt(cosm1, x, y, ALU.mult).then_inc(*step())
                tt(sine, angle, y, ALU.mult).then_inc(*step())
                pool.wait_ge(*settled())
                two_ops(out=x, in0=x, scalar=1.0, in1=k, op0=ALU.add, op1=ALU.mult)
                tt(angle, angle, k, ALU.mult).then_inc(*step())
                two_ops(out=cosm1, in0=y, scalar=-1.0, in1=cosm1, op0=ALU.add, op1=ALU.add)
                pool.wait_ge(*settled())
                tt(y, sine, x, ALU.add).then_inc(*step())
                tt(cosm1, cosm1, angle, ALU.subtract).then_inc(*step())
                pool.wait_ge(*settled())
                tt(sine, y, mag, ALU.mult).then_inc(*step())
                two_ops(out=x, in0=cosm1, scalar=1.0, in1=mag, op0=ALU.add, op1=ALU.mult)
                pool.wait_ge(*settled())
                pool.tensor_copy(abar[:, 0, :, :], per_q(x[:, chans])).then_inc(*step())
                pool.tensor_copy(abar[:, 1, :, :], per_q(sine[:, chans])).then_inc(*step())

            def coefficients():
                re, im, mg, cm1, ni, ar = (v[:, by_state] for v in (lam[:, 0, :], lam[:, 1, :], mag, cosm1, sine, x))
                s_ar, s_ai, cr, ci, s_mag, den, t, nr, t2, u = (st[:, i, :] for i in range(10))
                pool.tensor_copy(s_ar, ar).then_inc(*step())
                pool.tensor_copy(s_ai, ni).then_inc(*step())
                tt(s_mag, mg, mg, ALU.mult).then_inc(*step())
                tt(den, re, re, ALU.mult).then_inc(*step())
                tt(t, im, im, ALU.mult).then_inc(*step())
                tt(nr, mg, cm1, ALU.mult).then_inc(*step())
                pool.wait_ge(*settled())
                tt(den, den, t, ALU.add).then_inc(*step())
                two_ops(out=nr, in0=mg, scalar=-1.0, in1=nr, op0=ALU.add, op1=ALU.add)
                pool.wait_ge(*settled())
                tt(cr, nr, re, ALU.mult).then_inc(*step())
                tt(t, ni, im, ALU.mult).then_inc(*step())
                tt(ci, ni, re, ALU.mult).then_inc(*step())
                tt(t2, nr, im, ALU.mult).then_inc(*step())
                pool.wait_ge(*settled())
                tt(cr, cr, t, ALU.add).then_inc(*step())
                tt(ci, ci, t2, ALU.subtract).then_inc(*step())
                pool.wait_ge(*settled())

            def phase_powers(levels):
                t, nr, t2, u = (st[:, i, :] for i in range(6, 10))
                pc, ps = k[:, by_state], p[:, by_state]
                if levels[0] > 0:
                    pc, ps = (powers[:, levels[0] - 1, c, :] for c in range(2))
                else:
                    ts(pc, cosm1[:, by_state], 1.0, None, ALU.add).then_inc(*step())
                    pool.tensor_copy(ps, y[:, by_state]).then_inc(*step())
                    pool.wait_ge(*settled())
                for l in levels:
                    nc_, ns = powers[:, l, 0, :], powers[:, l, 1, :]
                    tt(t, ps, ps, ALU.mult).then_inc(*step())
                    tt(u, pc, pc, ALU.mult).then_inc(*step())
                    two_ops(out=ns, in0=pc, scalar=2.0, in1=ps, op0=ALU.mult, op1=ALU.mult)
                    pool.wait_ge(*settled())
                    tt(nc_, u, t, ALU.subtract).then_inc(*step())
                    tt(nr, ns, ns, ALU.mult).then_inc(*step())
                    pool.wait_ge(*settled())
                    tt(t2, nc_, nc_, ALU.mult).then_inc(*step())
                    pool.wait_ge(*settled())
                    tt(t2, t2, nr, ALU.add).then_inc(*step())
                    pool.wait_ge(*settled())
                    ts(t2, t2, -0.5, 1.5, ALU.mult, ALU.add).then_inc(*step())
                    pool.wait_ge(*settled())
                    tt(nc_, nc_, t2, ALU.mult).then_inc(*step())
                    pool.wait_ge(*settled())
                    tt(ns, ns, t2, ALU.mult).then_inc(powers_ready, 1)
                    pool.wait_ge(powers_ready, l + 1)
                    pc, ps = nc_, ns

            def low_parts(first, end):
                for u in range(first, end):
                    low_part(u // RING, u % RING)

            low_parts(0, 4)
            growth_and_angle()
            low_parts(4, 6)
            exponential(mag, x, k, p, exp2[:, :])
            low_parts(6, 10)
            quarter_turns()
            low_parts(10, 13)
            series()
            low_parts(13, 17)
            turn()
            low_parts(17, 21)
            coefficients()
            low_parts(21, 23)
            phase_powers(range(LEVELS // 2))
            low_parts(23, 25)
            phase_powers(range(LEVELS // 2, LEVELS))
            low_parts(25, 28)
            mixer_round = DEPTH * LAYER_U // RING
            with pool.Fori(7, mixer_round) as n:
                for s in range(RING):
                    low_part(n, s)
            for s in range(3):
                low_part(mixer_round, s)
            pool.wait_ge(mean_done, MIX * 2)
            pool.wait_ge(powers_ready, LEVELS)
            for l in range(LEVELS):
                n = 1 << l
                wc, ws = (powers[:, l, c, :].unsqueeze(2).to_broadcast([P, ST, n]) for c in range(2))
                c0, s0, c1 = phase[:, 0, :, 0:n], phase[:, 1, :, 0:n], phase[:, 0, :, n:2 * n]
                pool.wait_ge(phase_c, l + 1)
                pool.wait_ge(phase_s, l + 1)
                tt(c1, c0, wc, ALU.mult).then_inc(phase_step, 1)
                tt(phase_tp[:, :, 0:n], s0, ws, ALU.mult).then_inc(phase_step, 1)
                pool.wait_ge(phase_step, 2 * l + 2)
                tt(c1, c1, phase_tp[:, :, 0:n], ALU.subtract).then_inc(phase_c, 1)
            pool.wait_ge(mix_in, 16 * MIX_LOADS)
            pool.wait_ge(phase_c, LEVELS + 1)
            br, bi, nr, ni = (w_b[:, j, c, :, :] for j in (1, 0) for c in (0, 1))
            ar, ai = abar[:, 0, :, :], abar[:, 1, :, :]
            t0, t1 = (w_b2[:, 0, c, :, 0, :] for c in range(2))
            tt(nr, br, ar, ALU.mult).then_inc(wb_step, 1)
            tt(t0, bi, ai, ALU.mult).then_inc(wb_step, 1)
            tt(ni, br, ai, ALU.mult).then_inc(wb_step, 1)
            tt(t1, bi, ar, ALU.mult).then_inc(wb_step, 1)
            pool.wait_ge(wb_step, 4)
            tt(nr, nr, t0, ALU.subtract).then_inc(wb_ready, 1)
            tt(ni, ni, t1, ALU.add).then_inc(wb_ready, 1)
            low_part(mixer_round, 3)
            for s in range(RING):
                low_part(mixer_round + 1, s)

            def state_im_part(q):
                c, s = phase[:, 0, 4 * q:4 * q + 4, :], phase[:, 1, 4 * q:4 * q + 4, :]
                zr, zi = states[q][:, 0, :, :], states[q][:, 1, :, :]
                pool.wait_ge(scanned, 8 * q + 8)
                if q:
                    pool.wait_ge(state_im, q)
                else:
                    pool.wait_ge(wb_apart, 2 * BT)
                tt(t_p[:, :, :], zr, s, ALU.mult).then_inc(re_taken, 1)
                pool.wait_ge(im_taken, q + 1)
                tt(zi, zi, c, ALU.mult).then_inc(re_taken, 1)
                pool.wait_ge(re_taken, 2 * q + 2)
                tt(zi, zi, t_p[:, :, :], ALU.add).then_inc(state_im, 1)

            pool_steps = [0]

            def pooling(g):
                w, r = WINDOWS[g], MIN_R0 + SP_T + g
                pool.wait_ge(bank_free[r % 2], free_before(MIX, r) + 1)
                if g:
                    pool.wait_ge(pooled, 2 * g)
                u = u_all[:, g, :]

                def pool_next():
                    pool_steps[0] += 1
                    return pool_step, 1

                src, n, i = u, 1, 0
                while n < w:
                    dst = run[i][:, :]
                    tt(dst[:, n:T], src[:, n:T], src[:, 0:T - n], ALU.add).then_inc(*pool_next())
                    pool.tensor_copy(dst[:, 0:n], src[:, 0:n]).then_inc(*pool_next())
                    pool.wait_ge(pool_step, pool_steps[0])
                    src, n, i = dst, 2 * n, 1 - i
                mean = run[i]
                tt(mean[:, 0:16], src[:, 0:16], mpar[:, INV_C + 16 * g:INV_C + 16 * g + 16], ALU.mult).then_inc(*pool_next())
                pool.tensor_scalar(mean[:, 16:T], src[:, 16:T], 1.0 / w, None, ALU.mult).then_inc(*pool_next())
                pool.wait_ge(pool_step, pool_steps[0])
                tt(u[:, 0:16], mean[:, 0:16], u[:, 0:16], ALU.subtract).then_inc(pooled, 1)
                tt(u[:, 16:T], mean[:, 16:T], u[:, 16:T], ALU.subtract).then_inc(pooled, 1)

            state_im_part(0)
            low_part(mixer_round + 2, 0)
            low_part(mixer_round + 2, 1)
            low_part(mixer_round + 2, 2)
            pooling(0)
            pooling(1)
            state_im_part(1)
            pooling(2)
            pooling(3)
            state_im_part(2)
            state_im_part(3)
            low_part(mixer_round + 2, 3)
            with pool.Fori(mixer_round + 3, N_UNITS // RING) as n:
                for s in range(RING):
                    low_part(n, s)

        @block.tensor
        def _(pe):
            def passes(dst, lhs, rhs, start, stop, swapped=False):
                for n, (i, j) in enumerate(((0, 0), (0, 1), (1, 0))):
                    mm = pe.matmul(dst, lhs[i], rhs[j], start=start and n == 0, stop=stop and n == 2)
                return mm

            def take_unit(L, u, i=0):
                pe.wait_ge(lo_done, L * LAYER_U + i + u + 1)

            def take_bank(L, r, i=0):
                pe.wait_ge(bank_free[r % 2], free_before(L, r, i))
                return U_BANK[r % 2]

            def wt(u, k):
                s = u % RING
                return w_hi[s][:, k, :], w_lo[s][:, k, :]

            def feature_unit(L, u, r, rhs, ui=0, ri=0):
                take_unit(L, u, ui)
                dst = take_bank(L, r, ri)
                for k in range(KT):
                    mm = passes(dst[:, :], wt(u, k), rhs(k), k == 0, k == KT - 1)
                mm.then_inc(unit_used, 1)

            def x_parts(k):
                return xh[:, k, :], xl[:, k, :]

            def first_units(L, u, r, x_done, ui=0, ri=0):
                lag = 2
                for k in range(KT + lag):
                    for i in range(2):
                        c = k - lag * i
                        if not 0 <= c < KT:
                            continue
                        if c == 0:
                            take_unit(L, u + i, ui)
                            take_bank(L, r + i, ri)
                        if i == 0:
                            pe.wait_ge(x_lo, x_done + (c + 1))
                        mm = passes(U_BANK[(r + i) % 2][:, :], wt(u + i, c), x_parts(c), c == 0, c == KT - 1)
                        if c == KT - 1:
                            mm.then_inc(unit_used, 1)

            def token_units(L, u, r, half, ui=0, ri=0):
                take_unit(L, u + half, ui)
                for b in range(4):
                    if half == 0 and b % 2 == 0:
                        take_bank(L, r + b // 2, ri)
                    dst = U_BANK[(r + b // 2) % 2][:, b % 2 * RET_DV:(b % 2 + 1) * RET_DV]
                    for k in range(4):
                        s = (u + half) % RING
                        w_pair = [x[s][:, 2 * k:2 * k + 2, :].rearrange("p f n -> p (f n)") for x in (w_hi, w_lo)]
                        c = 4 * half + k
                        mm = passes(dst, (xh[:, c, b * P:(b + 1) * P], xl[:, c, b * P:(b + 1) * P]), w_pair,
                                    c == 0 and b % 2 == 0, c == KT - 1 and b % 2 == 1)
                mm.then_inc(unit_used, 1)

            def attention(L, t):
                it = L * 4 + t
                ui, ri = t * 12, t * 6

                def take_score(n):
                    pe.wait_ge(s_free[n % 2], it * 7 + (n // 2 + 1))
                    return S_BANK[n % 2]

                def scores(hh):
                    for r in range(2):
                        pe.wait_ge(*after_result(L, r, ri))
                    r0 = hh * NA_DH
                    q, k = na_q[r0:r0 + NA_DH, :], na_k[r0:r0 + NA_DH, :]
                    for j in range(CB):
                        dst = take_score(4 * hh + j)
                        for b in kblocks(j):
                            mm = pe.matmul(dst[:, b * P:(b + 1) * P], q[:, j * P:(j + 1) * P], k[:, (j - 1 + b) * P:(j + b) * P],
                                           start=True, stop=True)
                        mm.then_inc(score_done, 1)

                def rotate(n, src, ready):
                    pe.wait_ge(*after_result(L, ready, ri))
                    dst = take_score(n)
                    pe.matmul(dst[:, :], swap[:, :], src[:, :], start=True, stop=True).then_inc(score_done, 1)

                def turn_v():
                    pe.wait_ge(*after_result(L, 2, ri))
                    pe.wait_ge(o_norm, it * 4 + 4)
                    for b in range(CB):
                        mm = pe.transpose(O_BANK[:, b * P:(b + 1) * P], r_tmp[:, b * P:(b + 1) * P], ident[:, :])
                    mm.then_inc(vt_done, 1)

                def turn_probs(i):
                    j = i % CB
                    if i < 2:
                        pe.wait_ge(ot_read, it * 2 + (i + 1))
                    else:
                        pe.wait_ge(pt_ready, it * 8 + (i - 1))
                    pe.wait_ge(p_ready, it * 8 + (i + 1))
                    for b in kblocks(j):
                        mm = pe.transpose(T_BANK[i % 2][:, b * P:(b + 1) * P], s_t[:, i, b * P:(b + 1) * P], ident[:, :])
                    mm.then_inc(pt_done, 1)

                def pv(i):
                    hh, j = i // CB, i % CB
                    if i == 0:
                        pe.wait_ge(o_norm, it * 4 + 4)
                        pe.wait_ge(v_ready, it + 1)
                    pe.wait_ge(pt_ready, it * 8 + (i + 1))
                    r0 = hh * NA_DH
                    dst = Y_BANK[r0:r0 + NA_DH, j * P:(j + 1) * P]
                    bs = kblocks(j)
                    for b in bs:
                        mm = pe.matmul(dst, na_v[:, j - 1 + b, r0:r0 + NA_DH], pt[:, i % 2, b * P:(b + 1) * P],
                                       start=b == bs[0], stop=b == bs[-1])
                    mm.then_inc(pv_done, 1)

                first_units(L, 0, 0, L * 2 * KT, ui, ri)
                feature_unit(L, 2, 2, x_parts, ui, ri)
                scores(0)
                turn_v()
                feature_unit(L, 3, 3, x_parts, ui, ri)
                scores(1)
                rotate(8, r_q, 3)
                turn_probs(0)
                turn_probs(1)
                feature_unit(L, 4, 4, x_parts, ui, ri)
                pv(0)
                pv(1)
                turn_probs(2)
                turn_probs(3)
                rotate(9, r_k, 4)
                token_units(L, 5, 5, 0, ui, ri)
                pv(2)
                pv(3)
                turn_probs(4)
                turn_probs(5)
                token_units(L, 5, 5, 1, ui, ri)
                pv(4)
                pv(5)
                turn_probs(6)
                turn_probs(7)
                pe.wait_ge(rope_ready, it * 2 + 2)
                for m in range(4):
                    dst = take_score(10 + m)
                    pe.matmul(dst[:, :], r_k[:, m * P:(m + 1) * P], r_q[:, :], start=True, stop=True).then_inc(score_done, 1)
                feature_unit(L, 7, 7, x_parts, ui, ri)
                pv(6)
                pv(7)
                feature_unit(L, 8, 8, x_parts, ui, ri)
                for b in range(2):
                    pe.wait_ge(s_free[b], it * 7 + 8)
                for r in (5, 6):
                    pe.wait_ge(*after_result(L, r, ri))
                for n in range(4):
                    dst = (O_BANK if n < 2 else Y_BANK)[:, (n % 2) * RET_DV:(n % 2 + 1) * RET_DV]
                    if n == 2:
                        pe.wait_ge(ya_ready, it + 1)
                    for m in range(4):
                        mm = pe.matmul(dst, pr[:, m, n * P:(n + 1) * P], r_v[:, m, :], start=m == 0, stop=m == 3)
                    mm.then_inc(o_done, 1)
                feature_unit(L, 9, 9, x_parts, ui, ri)
                feature_unit(L, 10, 10, x_parts, ui, ri)
                for f in range(2):
                    pe.wait_ge(pt_ready, it * 8 + (7 + f))
                    pe.wait_ge(o_norm, it * 4 + 8)
                    for n in range(4):
                        mm = pe.transpose(T_BANK[f][:, n * P:(n + 1) * P], o_n[:, n, f * P:(f + 1) * P], ident[:, :])
                    mm.then_inc(ot_done, 1)
                feature_unit(L, 11, 11, x_parts, ui, ri)

            def branches(L, i):
                ui, ri = i * 8, i * 5
                it = L * 2 + i
                for g in range(2):
                    feature_unit(L, BR0 + g, BR_R0 + g, x_parts, ui, ri)
                pe.wait_ge(br_lo, L * 3 + 1)
                for m in range(4):
                    u = BR0 + 2 + m // 2
                    if m % 2 == 0:
                        take_unit(L, u, ui)
                    dst = take_bank(L, BR_R0 + 2 + m, ri)
                    for k in range(4):
                        mm = passes(dst[:, :], wt(u, 4 * (m % 2) + k), (ya_hi[:, k, :], ya_lo[:, k, :]), k == 0, k == 3)
                    mm.then_inc(unit_used if m % 2 else mid_done, 1)
                pe.wait_ge(br_lo, L * 3 + 3)
                for m in range(4):
                    feature_unit(L, BR0 + 4 + m, BR_R0 + 6 + m, lambda k: (yb_hi[:, k, :], yb_lo[:, k, :]), ui, ri)

            def mean_term(k, ready):
                pe.wait_ge(*ready(k))
                mm = pe.matmul(S_BANK[0][:, :], mean_w[:, :], z[:, k, :], start=k == 0, stop=k == KT - 1)
                if k == KT - 1:
                    mm.then_inc(mean_done, 1)

            def square_term(n, k, squares):
                pe.wait_ge(squared, n * KT + (k + 1))
                pe.matmul(S_BANK[1][:, :], mean_w[:, :], squares[k % 4][:, :], start=k == 0, stop=k == KT - 1)\
                    .then_inc(sq_used, 1)

            def variance(n, squares):
                for k in range(KT):
                    square_term(n, k, squares)

            def out_proj(L):
                pe.wait_ge(merged_lo, L * 8 + 8)
                ready = lambda k: (z_ready, L * KT + (k + 1))
                for k in range(KT):
                    feature_unit(L, OUT0 + k, OUT_R0 + k, lambda q: (merged_p[:, q, :], merged_p[:, 8 + q, :]))
                    if k > 0:
                        mean_term(k - 1, ready)
                mean_term(KT - 1, ready)
                variance(L * 2, sq)

            def ple(L):
                first_units(L, PLE0, PLE_R0, (L * 2 + 1) * KT)
                for h in range(2):
                    u0, r0 = PLE0 + 5 * h, PLE_R0 + 8 * h
                    for m in range(0 if h else 2, 4):
                        feature_unit(L, u0 + m, r0 + m, x_parts)
                    take_unit(L, u0 + 4)
                    if h == 0:
                        pe.wait_ge(p_lo_s, L + 1)
                    for m in range(4):
                        dst = take_bank(L, r0 + 4 + m)
                        for k in range(PLE_T):
                            mm = passes(dst[:, :], wt(u0 + 4, PLE_T * m + k), (p_hi[:, k, :], p_lo[:, k, :]), k == 0, k == PLE_T - 1)
                        mm.then_inc(unit_used if m == 3 else mid_done, 1)

            def down(L, u0, r0, split, after):
                for m in range(KT):
                    dst = take_bank(L, r0 + m)
                    for k in range(FT):
                        i = m * FT + k
                        if i % UT == 0:
                            take_unit(L, u0 + i // UT)
                        if m == 0:
                            pe.wait_ge(*split(k))
                        mm = passes(dst[:, :], wt(u0 + i // UT, i % UT), (g_hi[:, k, :], g_lo[:, k, :]), k == 0, k == FT - 1)
                        if i % UT == UT - 1:
                            mm.then_inc(unit_used, 1)
                        elif k == FT - 1:
                            mm.then_inc(mid_done, 1)
                    after(m)

            def down_layer(L):
                ready = lambda k: (bank_free[k % 2], free_before(L, DOWN_R0 + k) + 1)
                down(L, DOWN0, DOWN_R0, lambda k: (g_lo_s, L * FT + (k + 1)), lambda m: mean_term(m - 1, ready) if m else None)
                mean_term(KT - 1, ready)
                variance(L * 2 + 1, sq)

            def mixer():
                n0 = MIX * 2
                variance(n0, sq_1)
                by_place = lambda x: x.rearrange("p (b j) -> p b j", j=BT)

                def block_inputs(q):
                    if q:
                        pe.wait_ge(v_read, q)
                    for j in range(BT):
                        for k in range(4):
                            r0 = k * 2 * SCH
                            for c in range(2):
                                mm = pe.matmul(V_BANKS[:, k, c * NB:(c + 1) * NB],
                                               w_b2[r0:r0 + 2 * SCH, j, c, q, :, :].rearrange("p h n -> p (h n)"),
                                               by_place(u_all[r0:r0 + 2 * SCH, 4 + q, :])[:, :, j],
                                               start=j == 0 and c == 0, stop=j == BT - 1 and c == 1)
                    mm.then_inc(v_done, 1)

                Y = (Y_BANK, O_BANK, V_BANKS[:, 0, :], V_BANKS[:, 1, :])

                def convolve(q):
                    for k in range(BT):
                        pe.matmul(by_place(Y[q])[:, :, k:BT], k_conv[:, q, k, :], by_place(u_all[:, 4 + q, :])[:, :, 0:BT - k],
                                  start=k == 0, stop=False)

                def from_state(q):
                    pe.wait_ge(state_re, q + 1)
                    pe.wait_ge(state_im, q + 1)
                    for m in range(4):
                        r0 = m * 2 * SCH
                        for j in range(BT):
                            for c in range(2):
                                mm = pe.matmul(by_place(Y[q][r0:r0 + 2 * SCH, :])[:, 1:NB, j], c_pow[:, 4 * q + m, c, j + 1, :],
                                               states[q][:, c, m, 0:NB - 1], start=False, stop=j == BT - 1 and c == 1)
                    mm.then_inc(y_done, 1)

                first_units(MIX, MIN_U0, MIN_R0, (n0 + 1) * KT)
                for m in range(2, SP_T):
                    feature_unit(MIX, MIN_U0 + m, MIN_R0 + m, x_parts)
                for r in (SP_T - 2, SP_T - 1):
                    pe.wait_ge(*after_result(MIX, MIN_R0 + r))
                pe.wait_ge(wb_apart, 2 * BT)
                block_inputs(0)
                for m in range(SP_T, KT):
                    feature_unit(MIX, MIN_U0 + m, MIN_R0 + m, x_parts)
                block_inputs(1)
                pe.wait_ge(c_ready, 2 * BT)
                for m in range(ST):
                    q, r0 = m // 4, m % 4 * 2 * SCH
                    for c in range(2):
                        mm = pe.matmul(O_BANK[r0:r0 + 2 * SCH, q * 2 * SCH * BT:(q + 1) * 2 * SCH * BT], b_st[:, c, m, :],
                                       c_pow[:, m, c, 0:BT, :].rearrange("p k n -> p (k n)"), start=c == 0, stop=c == 1)
                mm.then_inc(kernel_done, 1)
                pe.wait_ge(kernel_ready, 4)
                convolve(0)
                block_inputs(2)
                convolve(1)
                pe.wait_ge(c_ready, 2 * BT + 2)
                from_state(0)
                block_inputs(3)
                from_state(1)
                for g in range(SP_T):
                    if g >= 2:
                        pe.wait_ge(y_pool, g - 1)
                    pe.wait_ge(pooled, 2 * g + 2)
                    pe.matmul(U_BANK[g % 2][:, :], w_pool[:, g, :], u_all[:, g, :], start=True, stop=True).then_inc(pool_done, 1)
                pe.wait_ge(v_read, SP_T)
                convolve(2)
                convolve(3)
                from_state(2)
                from_state(3)
                pe.wait_ge(yg_lo_s, SP_T)
                pe.wait_ge(y_pool, SP_T)
                for m in range(SP_T):
                    u = GLU_U0 + m // 2
                    if m % 2 == 0:
                        take_unit(MIX, u)
                    dst = take_bank(MIX, GLU_R0 + m)
                    for k in range(SP_T):
                        mm = passes(dst[:, :], wt(u, 4 * (m % 2) + k), (yg_hi[:, k, :], yg_lo[:, k, :]), k == 0, k == SP_T - 1)
                    mm.then_inc(unit_used if m % 2 else mid_done, 1)

                def mixed(k):
                    pe.wait_ge(mix_lo_s, k + 1)
                    return mix_hi[:, k, :], mix_lo[:, k, :]

                for m in range(KT):
                    feature_unit(MIX, MOUT_U0 + m, MOUT_R0 + m, mixed)
                    if m:
                        square_term(n0 + 1, m - 1, sq_2)
                square_term(n0 + 1, KT - 1, sq_2)
                with pe.Fori(0, FT // 2) as j:
                    first_units(MIX, GU_U0, GU_R0, (n0 + 2) * KT, j * 4, j * 2)
                    for m in range(2, 4):
                        feature_unit(MIX, GU_U0 + m, GU_R0 + m, x_parts, j * 4, j * 2)
                down(MIX, MDOWN_U0, MDOWN_R0, lambda k: (gu_lo, k + 1),
                     lambda m: square_term(n0 + 2, m - 1, sq_3) if m else None)
                square_term(n0 + 2, KT - 1, sq_3)

            pe.sem_inc(unit_used, 1)
            pe.wait_ge(params_in, 16 * 5)
            pe.wait_ge(consts_set, 3)
            with pe.Fori(0, DEPTH) as L:
                with pe.Fori(0, 4) as t:
                    attention(L, t)
                with pe.Fori(0, 2) as i:
                    branches(L, i)
                out_proj(L)
                ple(L)
                with pe.Fori(0, FT // 2) as j:
                    for m in range(4):
                        feature_unit(L, UP0 + m, UP_R0 + m, x_parts, j * 4, j * 2)
                down_layer(L)
            mixer()

        @block.scalar
        def _(act):
            def round_ahead(L, u, i=0):
                n = u + 3
                s = n % RING
                act.wait_ge(landed[s], (L * (LAYER_U // RING) + n // RING + 1) * 16 + i * (16 // RING))
                act.wait_ge(unit_used, L * LAYER_U + i + (u + 1))
                act.activation(w_hi[s][:, :, :], stage[s][:, :, :], ACT.Copy).then_inc(hi_done, 1)

            def unit_result(L, u, i=0):
                act.wait_ge(unit_used, L * LAYER_U + i + (u + 2))

            def attention(L, t):
                it = L * 4 + t
                ui = t * 12

                def copy_out(u, dst, scale=1.0):
                    unit_result(L, u, ui)
                    act.activation(dst, U_BANK[u % 2][:, :], ACT.Copy, scale=scale).then_inc(bank_free[u % 2], 1)

                def copy_blocks(u, dst, scale=1.0):
                    unit_result(L, u, ui)
                    act.activation(dst.rearrange("p (b r c) -> p b r c", b=CB, r=ROWS), block_view(U_BANK[u % 2][:, :]),
                                   ACT.Copy, scale=scale).then_inc(bank_free[u % 2], 1)

                def exps(hh):
                    act.wait_ge(nmax_ready, it * 2 + (hh + 1))
                    for j in range(CB):
                        i = 4 * hh + j
                        bs = kblocks(j)
                        s = s_t[:, i, bs[0] * P:(bs[-1] + 1) * P]
                        act.activation(s, s, ACT.Exp, bias=row_nmax[:, i:i + 1], accum_out=row_sum[:, i:i + 1])\
                            .then_inc(exp_done, 1)

                def probs_t(i):
                    bs = kblocks(i % CB)
                    act.wait_ge(pt_done, it * 8 + (i + 1))
                    if i >= 2:
                        act.wait_ge(pv_done, it * 8 + (i - 1))
                    act.activation(pt[:, i % 2, bs[0] * P:(bs[-1] + 1) * P],
                                   T_BANK[i % 2][:, bs[0] * P:(bs[-1] + 1) * P], ACT.Copy).then_inc(pt_ready, 1)

                act.wait_ge(unit_used, L * LAYER_U + t * 12 + 1)
                act.dma_start(bias[:, :, :].rearrange("p h n -> p (h n)"),
                              a["bias"][bass.ds(it, 1)].rearrange("s p n -> p (s n)")).then_inc(bias_in, 16)
                round_ahead(L, 0, ui)
                copy_blocks(0, na_q[:, :], NA_DH ** -0.5)
                round_ahead(L, 1, ui)
                copy_blocks(1, na_k[:, :])
                round_ahead(L, 2, ui)
                copy_blocks(2, r_tmp[:, :])
                act.wait_ge(dterm, it * 3 + 3)
                act.activation(d_tab[:, :], d_tab[:, :], ACT.Exp).then_inc(dtab_ready, 1)
                act.wait_ge(vt_done, it + 1)
                act.activation(na_v[:, :, :].rearrange("p b n -> p (b n)"), O_BANK[:, :], ACT.Copy).then_inc(v_ready, 1)
                exps(0)
                round_ahead(L, 3, ui)
                copy_out(3, r_q[:, :])
                probs_t(0)
                probs_t(1)
                exps(1)
                round_ahead(L, 4, ui)
                copy_out(4, r_k[:, :])
                probs_t(2)
                probs_t(3)
                round_ahead(L, 5, ui)
                probs_t(4)
                probs_t(5)
                round_ahead(L, 6, ui)
                unit_result(L, 6, ui)
                for r in (5, 6):
                    act.activation(r_v[:, 2 * (r - 5):2 * (r - 4), :].rearrange("p n c -> p (n c)"), U_BANK[r % 2][:, :], ACT.Copy)\
                        .then_inc(bank_free[r % 2], 1)
                probs_t(6)
                probs_t(7)
                for f in range(2):
                    round_ahead(L, 7 + f, ui)
                    unit_result(L, 7 + f, ui)
                    act.activation(sg[:, f, :], U_BANK[(7 + f) % 2][:, :], ACT.Sigmoid).then_inc(sig_ready, 1)
                    if f == 0:
                        act.wait_ge(pv_done, it * 8 + 8)
                        act.activation(ya[:, bass.ds(t, 1), :].rearrange("p s (r b c) -> p (s r) b c", r=ROWS, b=CB),
                                       Y_BANK[:, :].rearrange("p (b r c) -> p r b c", b=CB, r=ROWS), ACT.Copy)\
                            .then_inc(ya_ready, 1)
                round_ahead(L, 9, ui)
                act.wait_ge(gn_aggr, it * 4 + 4)
                act.activation(gn_std, gn_mv[:, :, 1], ACT.Sqrt, bias=gn_eps[:, :]).then_inc(std_ready, 1)
                for g in range(3):
                    if g:
                        round_ahead(L, 9 + g, ui)
                    unit_result(L, 9 + g, ui)
                    act.activation(gates[:, bass.ds(t * 3 + g, 1), :].rearrange("p s n -> p (s n)"),
                                   U_BANK[(9 + g) % 2][:, :], ACT.Sigmoid).then_inc(bank_free[(9 + g) % 2], 1)

            def branches(L, i):
                ui = i * 8
                it = L * 2 + i
                for g in range(2):
                    round_ahead(L, BR0 + g, ui)
                    unit_result(L, BR0 + g, ui)
                    act.activation(gates[:, bass.ds(i * 2 + (12 + g), 1), :].rearrange("p s n -> p (s n)"),
                                   U_BANK[g][:, :], ACT.Sigmoid).then_inc(bank_free[g], 1)
                for u in range(2, 4):
                    round_ahead(L, BR0 + u, ui)
                for m in range(4):
                    round_ahead(L, BR0 + 4 + m, ui)
                    act.wait_ge(merged, it * 4 + (m + 1))
                    act.activation(merged_p[:, bass.ds(i * 4 + m, 1), :].rearrange("p s n -> p (s n)"),
                                   m_tmp[m % 2][:, :], ACT.Copy).then_inc(merged_hi, 1)

            def split_branch_inputs(L):
                act.wait_ge(ya_ready, L * 4 + 4)
                act.wait_ge(ot_read, L * 8 + 10)
                act.activation(ya_hi[:, :, :], ya[:, :, :], ACT.Copy).then_inc(br_hi, 1)
                for h in range(2):
                    act.activation(yb_hi[:, 4 * h:4 * h + 4, :], yb[:, 4 * h:4 * h + 4, :], ACT.Copy).then_inc(br_hi, 1)

            def sqrt_table():
                act.activation(warm[:, :], ln_eps[:, :], ACT.Sqrt)

            def norm(L, which):
                n = L * 2 + which
                for k in range(KT):
                    act.wait_ge(centred, n * KT + (k + 1))
                    if k >= 4:
                        act.wait_ge(sq_used, n * KT + (k - 3))
                    act.activation(sq[k % 4][:, :], z[:, k, :], ACT.Square).then_inc(squared, 1)
                act.wait_ge(sq_used, n * KT + KT)
                act.activation(rstd[:, :], S_BANK[1][:, :], ACT.Sqrt, bias=ln_eps[:, :]).then_inc(lstd, 1)
                for k in range(KT):
                    b = lnp[:, bass.ds(L, 1), 2 * which + 1, k]
                    act.wait_ge(normed, n * KT + (k + 1))
                    act.activation(xh[:, k, :], p_sig[k % 4][:, :], ACT.Identity, bias=b).then_inc(x_hi, 1)
                    act.activation(z[:, k, :], p_sig[k % 4][:, :], ACT.Identity, bias=b).then_inc(x_ready, 1)
                act.wait_ge(x_ready, n * KT + KT)

            def ple(L):
                act.wait_ge(p_in, L * 16 + 16)
                act.activation(p_hi[:, :, :], p_raw[:, :, :], ACT.Copy).then_inc(p_hi_s, 1)
                for h in range(2):
                    u0, r0 = PLE0 + 5 * h, PLE_R0 + 8 * h
                    for m in range(4):
                        round_ahead(L, u0 + m)
                        unit_result(L, u0 + m)
                        if h:
                            act.wait_ge(zpre, L * 8 + (m + 1))
                        act.activation(p_sig[m][:, :], U_BANK[m % 2][:, :], ACT.Sigmoid).then_inc(bank_free[m % 2], 1)
                    round_ahead(L, u0 + 4)

            def up(L, j):
                it = L * FT + j * 2
                for c in range(2):
                    for half, buf in ((0, conv_a), (1, conv_b)):
                        u = UP0 + 2 * c + half
                        round_ahead(L, u, j * 4)
                        unit_result(L, u, j * 4)
                        ch = bass.ds(j * 2 + (half * FT + c), 1)
                        act.activation(buf[c][:, :], U_BANK[half][:, :], ACT.Identity,
                                       scale=convp[:, bass.ds(L, 1), 1, ch].rearrange("p l c -> p (l c)"),
                                       bias=convp[:, bass.ds(L, 1), 3, ch].rearrange("p l c -> p (l c)")).then_inc(conv_mid, 1)
                    act.wait_ge(bank_free[0], free_before(L, UP_R0 + 2 * c, j * 2) + 1)
                    act.activation(conv_a[c][:, :], conv_a[c][:, :], ACT.Gelu_apprx_tanh).then_inc(gelu_done, 1)
                    act.wait_ge(glu_done, it + (c + 1))
                    act.activation(g_hi[:, bass.ds(j * 2 + c, 1), :].rearrange("p s n -> p (s n)"), conv_b[c][:, :],
                                   ACT.Copy).then_inc(g_hi_s, 1)

            def rms_split(n, tiles):
                for k in range(KT):
                    act.wait_ge(normed, n * KT + (k + 1))
                    act.activation(xh[:, k, :], tiles[k % 4][:, :], ACT.Copy).then_inc(x_hi, 1)

            def root(n, dst):
                act.wait_ge(sq_used, n * KT + KT)
                act.wait_ge(rms_set, 1)
                act.activation(dst[:, :], S_BANK[1][:, :], ACT.Sqrt, bias=rms_eps[:, :]).then_inc(lstd, 1)

            def square(n, k, squares, ready):
                act.wait_ge(*ready)
                if k >= 4:
                    act.wait_ge(sq_used, n * KT + (k - 3))
                act.activation(squares[k % 4][:, :], z[:, k, :], ACT.Square).then_inc(squared, 1)

            def mixer():
                n0 = MIX * 2
                ahead = lambda u: round_ahead(MIX, u) if u + 3 < MIX_U else None
                after = lambda r: (bank_free[r % 2], free_before(MIX, r) + 1)
                act.wait_ge(x_lo, n0 * KT + KT)
                for dst, name in ((w_pool, "w_pool"), (b_st, "b_st"), (c_st, "c_st")):
                    act.dma_start(dst[:], a[name]).then_inc(mix_in, 16)
                act.dma_start(w_b[:, BT - 1, :, :, :], a["w_b"]).then_inc(mix_in, 16)
                for k in range(KT):
                    square(n0, k, sq_1, (x_ready, (n0 - 1) * KT + (k + 1)))
                root(n0, rstd_1)
                rms_split(n0, xn_1)
                for m in range(KT):
                    ahead(MIN_U0 + m)
                    unit_result(MIX, MIN_U0 + m)
                    act.activation(u_all[:, (m + SP_T) % KT, :], U_BANK[m % 2][:, :], ACT.Copy).then_inc(bank_free[m % 2], 1)
                    if m == 1:
                        act.wait_ge(wb_ready, 2)
                        for j in range(BT):
                            for h in range(2):
                                act.activation(w_b2[:, j, :, :, h, :].rearrange("p c q n -> p (c q) n"),
                                               w_b[:, j, :, :, :].rearrange("p c q n -> p (c q) n"), ACT.Copy,
                                               scale=mpar[:, HALF_C + h:HALF_C + h + 1]).then_inc(wb_apart, 1)
                act.wait_ge(kernel_done, 1)
                for h in range(4):
                    act.activation(k_conv[:, :, :, h * 2 * SCH:(h + 1) * 2 * SCH].rearrange("p q k n -> p (q k) n"),
                                   O_BANK[:, 0:SP_T * BT * 2 * SCH].rearrange("p (a n) -> p a n", n=2 * SCH), ACT.Copy,
                                   scale=mpar[:, QUART_C + h:QUART_C + h + 1]).then_inc(kernel_ready, 1)
                for g in range(SP_T):
                    act.wait_ge(pool_done, g + 1)
                    act.activation(u_all[:, g, :], U_BANK[g % 2][:, :], ACT.Copy,
                                   scale=mpar[:, POOLS_C + g:POOLS_C + g + 1]).then_inc(y_pool, 1)
                for q in range(SP_T):
                    act.wait_ge(y_skip, q + 1)
                    act.activation(yg[:, q, :], yg[:, q, :], ACT.Gelu_apprx_tanh).then_inc(y_gelu, 1)
                    act.wait_ge(y_gelu, q + 1)
                    act.activation(yg_hi[:, q, :], yg[:, q, :], ACT.Copy).then_inc(yg_hi_s, 1)
                for g in range(SP_T):
                    act.wait_ge(y_pool, g + 1)
                    act.activation(mix_hi[:, g, :], u_all[:, g, :], ACT.Copy).then_inc(mix_hi_s, 1)
                for m in range(SP_T):
                    if m % 2 == 0:
                        ahead(GLU_U0 + m // 2)
                        act.wait_ge(mid_done, MIX * LAYER_M + (GLU_M0 + m // 2 + 1))
                    else:
                        unit_result(MIX, GLU_U0 + m // 2)
                    if m >= 2:
                        act.wait_ge(y_ssm, m - 1)
                    act.activation(glu_sig[m % 2][:, :], U_BANK[m % 2][:, :], ACT.Sigmoid,
                                   bias=mpar[:, BGLU_C + m:BGLU_C + m + 1]).then_inc(bank_free[m % 2], 1)
                for m in range(SP_T):
                    act.wait_ge(y_ssm, m + 1)
                    act.activation(mix_hi[:, SP_T + m, :], u_all[:, SP_T + m, :], ACT.Copy).then_inc(mix_hi_s, 1)
                sqrt_table()
                for m in range(KT):
                    ahead(MOUT_U0 + m)
                    square(n0 + 1, m, sq_2, after(MOUT_R0 + m))
                root(n0 + 1, rstd_2)
                rms_split(n0 + 1, xn_2)
                with act.Fori(0, FT // 2) as j:
                    for c in range(2):
                        u = GU_U0 + 2 * c
                        round_ahead(MIX, u, j * 4)
                        unit_result(MIX, u, j * 4)
                        act.activation(silu[c][:, :], U_BANK[0][:, :], ACT.Silu).then_inc(bank_free[0], 1)
                        round_ahead(MIX, u + 1, j * 4)
                        act.wait_ge(bank_free[1], free_before(MIX, GU_R0 + 2 * c + 1, j * 2) + 1)
                        act.activation(g_hi[:, bass.ds(j * 2 + c, 1), :].rearrange("p s n -> p (s n)"), hidden[c][:, :],
                                       ACT.Copy).then_inc(gu_hi, 1)
                sqrt_table()
                sq_m = 0
                for u in range(DOWN_U):
                    ahead(MDOWN_U0 + u)
                    while sq_m < KT and ((sq_m + 1) * FT - 1) // UT < u:
                        square(n0 + 2, sq_m, sq_3, after(MDOWN_R0 + sq_m))
                        sq_m += 1
                for m in range(sq_m, KT):
                    square(n0 + 2, m, sq_3, after(MDOWN_R0 + m))
                root(n0 + 2, rstd_3)

            act.sem_inc(bank_free[0], 1)
            act.sem_inc(bank_free[1], 1)
            for dst, src in ((ident, "ident"), (swap, "swap"), (lnp, "lnp"), (convp, "convp"), (decay, "decay")):
                act.dma_start(dst[:], a[src]).then_inc(params_in, 16)
            act.dma_start(lam[:, :, :], a["lam"]).then_inc(lam_in, 16)
            act.dma_start(dt[:, 0, :], a["log_dt"]).then_inc(lam_in, 16)
            act.dma_start(mpar[:, :], a["mpar"]).then_inc(mpar_in, 16)
            def first_high(n):
                act.wait_ge(landed[n], 16)
                act.activation(w_hi[n][:, :, :], stage[n][:, :, :], ACT.Copy).then_inc(hi_done, 1)

            first_high(0)
            for k in range(KT):
                if k % 2 == 0:
                    act.wait_ge(x_in[k // 2], 16)
                act.activation(xh[:, k, :], z[:, k, :], ACT.Copy).then_inc(x_hi, 1)
                if k == 1:
                    first_high(1)
            first_high(2)
            act.wait_ge(params_in, 16 * 5)
            flat = decay[:, :, :].rearrange("p d n -> p (d n)")
            act.activation(decay_a[:, :], flat, ACT.Abs).then_inc(decay_step, 1)
            act.wait_ge(decay_step, 1)
            act.activation(decay_a[:, :], decay_a[:, :], ACT.Exp, scale=-1.0).then_inc(decay_step, 1)
            act.wait_ge(decay_step, 2)
            act.activation(decay_a[:, :], decay_a[:, :], ACT.Ln, bias=1.0).then_inc(decay_step, 1)
            with act.Fori(0, DEPTH) as L:
                act.wait_ge(x_lo, (L * 2 + 1) * KT)
                act.dma_start(rope[:, :, :], a["rope"]).then_inc(tables_in, 16)
                act.dma_start(delta[:, :], a["delta"]).then_inc(tables_in, 16)
                act.dma_start(masks[:, :, :], a["masks"]).then_inc(tables_in, 16)
                with act.Fori(0, 4) as t:
                    attention(L, t)
                split_branch_inputs(L)
                act.dma_start(p_raw[:, :, :], a["p"][bass.ds(L, 1)].rearrange("s p k n -> p (s k) n")).then_inc(p_in, 16)
                with act.Fori(0, 2) as i:
                    branches(L, i)
                sqrt_table()
                for k in range(KT):
                    round_ahead(L, OUT0 + k)
                norm(L, 0)
                ple(L)
                with act.Fori(0, FT // 2) as j:
                    up(L, j)
                sqrt_table()
                for k in range(DOWN_U):
                    round_ahead(L, DOWN0 + k)
                norm(L, 1)
            mixer()

        @block.vector
        def _(dve):
            def unit_result(L, u, i=0):
                dve.wait_ge(unit_used, L * LAYER_U + i + (u + 2))

            def attention(L, t):
                it = L * 4 + t
                ui, ri = t * 12, t * 6

                def after_score(n):
                    return s_free[n % 2], it * 7 + (n // 2 + 2)

                dve.tensor_copy(lg_now, decay[:, :, bass.ds(it, 1)].rearrange("p d s -> p (d s)")).then_inc(dterm_copy, 1)
                dve.wait_ge(dterm_copy, it + 1)
                dve.tensor_scalar(d_tmp[:, :], delta[:, :], 0.0, lg_now[:, 1:2], ALU.min, ALU.mult).then_inc(dterm, 1)
                dve.tensor_scalar(d_tab[:, :], delta[:, :], 0.0, lg_now[:, 0:1], ALU.max, ALU.mult).then_inc(dterm, 1)
                dve.wait_ge(dterm, it * 3 + 2)
                dve.tensor_tensor(d_tab[:, :], d_tab[:, :], d_tmp[:, :], ALU.subtract).then_inc(dterm, 1)

                def mask_scores(hh):
                    dve.wait_ge(bias_in, it * 16 + 16)
                    for j in range(CB):
                        i = 4 * hh + j
                        bs = kblocks(j)
                        cols = slice(bs[0] * P, (bs[-1] + 1) * P)
                        dve.wait_ge(score_done, it * 14 + (i + 1))
                        dve.tensor_tensor(s_t[:, i, cols], S_BANK[i % 2][:, cols], bias[:, hh, cols], ALU.add)\
                            .then_inc(s_free[i % 2], 1)
                        dve.wait_ge(*after_score(i))
                        stand(dve, dve_passed)
                        dve.tensor_tensor_reduce(s_t[:, i, cols], s_t[:, i, cols], masks[:, mask_of(j), cols], 1.0, -3.0e38,
                                                 ALU.add, ALU.max, row_max[:, i:i + 1]).then_inc(masked, 1)
                    dve.wait_ge(masked, it * 8 + (4 * hh + 4))
                    dve.tensor_scalar(row_nmax[:, 4 * hh:4 * hh + 4], row_max[:, 4 * hh:4 * hh + 4], -1.0, None, ALU.mult)\
                        .then_inc(nmax_ready, 1)

                def normalise(hh):
                    dve.wait_ge(exp_done, it * 8 + (4 * hh + 4))
                    dve.reciprocal(row_inv[:, 4 * hh:4 * hh + 4], row_sum[:, 4 * hh:4 * hh + 4]).then_inc(inv_ready, 1)
                    dve.wait_ge(inv_ready, it * 2 + (hh + 1))
                    for j in range(CB):
                        i = 4 * hh + j
                        bs = kblocks(j)
                        s = s_t[:, i, bs[0] * P:(bs[-1] + 1) * P]
                        dve.tensor_scalar(s, s, row_inv[:, i:i + 1], None, ALU.mult).then_inc(p_ready, 1)

                def rotate(n, x):
                    k = n - 8
                    dve.wait_ge(score_done, it * 14 + (n + 1))
                    dve.tensor_tensor(r_tmp[:, :], S_BANK[n % 2][:, :], rope[:, 1, :], ALU.mult).then_inc(s_free[n % 2], 1)
                    dve.tensor_tensor(x[:, :], x[:, :], rope[:, 0, :], ALU.mult).then_inc(rope_cos, 1)
                    dve.wait_ge(*after_score(n))
                    dve.wait_ge(rope_cos, it * 2 + (k + 1))
                    dve.tensor_tensor(x[:, :], x[:, :], r_tmp[:, :], ALU.add).then_inc(rope_ready, 1)

                mask_scores(0)
                normalise(0)
                mask_scores(1)
                rotate(8, r_q)
                normalise(1)
                rotate(9, r_k)
                dve.wait_ge(rope_ready, it * 2 + 2)
                dve.wait_ge(dtab_ready, it + 1)
                for m in range(4):
                    dve.wait_ge(score_done, it * 14 + (11 + m))
                    dve.scalar_tensor_tensor(out=pr[:, m, :], in0=S_BANK[m % 2][:, :], scalar=RET_DK ** -0.5,
                                             in1=d_tab[:, (3 - m) * P:(7 - m) * P], op0=ALU.mult, op1=ALU.mult)\
                        .then_inc(s_free[m % 2], 1)
                for f in range(2):
                    dve.wait_ge(sig_ready, it * 2 + (f + 1))
                    dve.tensor_tensor(sg[:, f, :], U_BANK[(7 + f) % 2][:, :], sg[:, f, :], ALU.mult)\
                        .then_inc(bank_free[(7 + f) % 2], 1)

                def o_tile(n):
                    return (O_BANK if n < 2 else Y_BANK)[:, (n % 2) * RET_DV:(n % 2 + 1) * RET_DV]

                for n in range(4):
                    dve.wait_ge(o_done, it * 4 + (2 * (n // 2) + 2))
                    dve.bn_stats(gn_st[:, n, :], o_tile(n)).then_inc(gn_stat, 1)
                dve.wait_ge(gn_stat, it * 4 + 4)
                stand(dve, dve_passed)
                for n in range(4):
                    dve.bn_aggr(gn_mv[:, n, :], gn_st[:, n, :]).then_inc(gn_aggr, 1)
                dve.wait_ge(std_ready, it + 1)
                dve.reciprocal(gn_inv, gn_std).then_inc(ginv_ready, 1)
                dve.wait_ge(ginv_ready, it + 1)
                for n in range(4):
                    dve.tensor_scalar(o_n[:, n, :], o_tile(n), gn_mv[:, n, 0:1], gn_inv[:, n:n + 1], ALU.subtract, ALU.mult)\
                        .then_inc(o_norm, 1)
                for f in range(2):
                    dve.wait_ge(ot_done, it * 2 + (f + 1))
                    dve.tensor_tensor(yb[:, bass.ds(t * 2 + f, 1), :].rearrange("p s n -> p (s n)"), T_BANK[f][:, :],
                                      sg[:, f, :], ALU.mult).then_inc(ot_read, 1)

            def split_branch_inputs(L):
                dve.wait_ge(br_hi, L * 3 + 1)
                dve.tensor_tensor(ya_lo[:, :, :], ya[:, :, :], ya_hi[:, :, :].bitcast(F32), ALU.subtract).then_inc(br_lo, 1)
                for h in range(2):
                    dve.wait_ge(br_hi, L * 3 + (2 + h))
                    q = slice(4 * h, 4 * h + 4)
                    dve.tensor_tensor(yb_lo[:, q, :], yb[:, q, :], yb_hi[:, q, :].bitcast(F32), ALU.subtract).then_inc(br_lo, 1)

            def branches(L, i):
                ui, ri = i * 8, i * 5
                it = L * 2 + i
                g_a = lambda m: gates[:, bass.ds(i * 4 + m, 1), :].rearrange("p s n -> p (s n)")
                g_b = lambda m: gates[:, bass.ds(i * 4 + (8 + m), 1), :].rearrange("p s n -> p (s n)")
                for m in range(4):
                    r = BR_R0 + 2 + m
                    if m % 2:
                        unit_result(L, BR0 + 2 + m // 2, ui)
                    else:
                        dve.wait_ge(mid_done, L * LAYER_M + i * 2 + (BR_M0 + m // 2 + 1))
                    dve.tensor_tensor(g_a(m), U_BANK[r % 2][:, :], g_a(m), ALU.mult).then_inc(bank_free[r % 2], 1)
                for m in range(4):
                    r = BR_R0 + 6 + m
                    unit_result(L, BR0 + 4 + m, ui)
                    dve.tensor_tensor(g_b(m), U_BANK[r % 2][:, :], g_b(m), ALU.mult).then_inc(bank_free[r % 2], 1)
                    dve.wait_ge(bank_free[r % 2], free_before(L, r, ri) + 1)
                    dve.tensor_tensor(m_tmp[m % 2][:, :], g_a(m), g_b(m), ALU.add).then_inc(merged, 1)
                    dve.wait_ge(merged_hi, it * 4 + (m + 1))
                    dve.tensor_tensor(merged_p[:, bass.ds(i * 4 + (8 + m), 1), :].rearrange("p s n -> p (s n)"), m_tmp[m % 2][:, :],
                                      merged_p[:, bass.ds(i * 4 + m, 1), :].rearrange("p s n -> p (s n)").bitcast(F32),
                                      ALU.subtract).then_inc(merged_lo, 1)

            def residual_out(L):
                for k in range(KT):
                    unit_result(L, OUT0 + k)
                    dve.scalar_tensor_tensor(out=z[:, k, :], in0=xh[:, k, :].bitcast(F32), scalar=ALPHA,
                                             in1=U_BANK[k % 2][:, :], op0=ALU.mult, op1=ALU.add).then_inc(bank_free[k % 2], 1)
                    dve.wait_ge(bank_free[k % 2], free_before(L, OUT_R0 + k) + 1)
                    dve.scalar_tensor_tensor(out=z[:, k, :], in0=xl[:, k, :].bitcast(F32), scalar=ALPHA,
                                             in1=z[:, k, :], op0=ALU.mult, op1=ALU.add).then_inc(z_ready, 1)

            def norm(L, which):
                n = L * 2 + which
                dve.wait_ge(mean_done, n + 1)
                for k in range(KT):
                    dve.tensor_tensor(z[:, k, :], z[:, k, :], S_BANK[0][:, :], ALU.subtract).then_inc(centred, 1)
                dve.wait_ge(lstd, n + 1)
                dve.reciprocal(rstd[:, :], rstd[:, :]).then_inc(lrstd, 1)
                dve.wait_ge(lrstd, n + 1)

                def low(k):
                    dve.wait_ge(x_hi, n * KT + (KT + k + 1))
                    dve.scalar_tensor_tensor(out=xl[:, k, :], in0=p_sig[k % 4][:, :], scalar=lnp[:, bass.ds(L, 1), 2 * which + 1, k],
                                             in1=xh[:, k, :].bitcast(F32), op0=ALU.add, op1=ALU.subtract).then_inc(x_lo, 1)

                for k in range(KT):
                    if k >= 4:
                        dve.wait_ge(x_ready, n * KT + (k - 3))
                        dve.wait_ge(x_lo, n * KT + (KT + k - 3))
                    dve.scalar_tensor_tensor(out=p_sig[k % 4][:, :], in0=z[:, k, :], scalar=lnp[:, bass.ds(L, 1), 2 * which, k],
                                             in1=rstd[:, :], op0=ALU.mult, op1=ALU.mult).then_inc(normed, 1)
                    if k >= 1:
                        low(k - 1)
                low(KT - 1)

            def ple(L):
                dve.wait_ge(x_ready, L * 2 * KT + KT)
                dve.wait_ge(p_hi_s, L + 1)
                dve.tensor_tensor(p_lo[:, :, :], p_raw[:, :, :], p_hi[:, :, :].bitcast(F32), ALU.subtract).then_inc(p_lo_s, 1)
                for h in range(2):
                    for m in range(4):
                        r = PLE_R0 + 8 * h + 4 + m
                        if m == 3:
                            unit_result(L, PLE0 + 5 * h + 4)
                        else:
                            dve.wait_ge(mid_done, L * LAYER_M + (PLE_M0 + 3 * h + m + 1))
                        dve.tensor_tensor(p_sig[m][:, :], U_BANK[r % 2][:, :], p_sig[m][:, :], ALU.mult)\
                            .then_inc(bank_free[r % 2], 1)
                        dve.wait_ge(bank_free[r % 2], free_before(L, r) + 1)
                        dve.scalar_tensor_tensor(out=z[:, 4 * h + m, :], in0=z[:, 4 * h + m, :], scalar=ALPHA, in1=p_sig[m][:, :],
                                                 op0=ALU.mult, op1=ALU.add).then_inc(zpre, 1)

            def up(L, j):
                it = L * FT + j * 2
                for c in range(2):
                    for half, buf in ((0, conv_a), (1, conv_b)):
                        n = 2 * c + half
                        ch = bass.ds(j * 2 + (half * FT + c), 1)
                        tap = lambda w: convp[:, bass.ds(L, 1), w, ch].rearrange("p l c -> p (l c)")
                        ps, y = U_BANK[half], buf[c]
                        dve.wait_ge(conv_mid, it * 2 + (n + 1))
                        dve.scalar_tensor_tensor(out=y[:, 1:T], in0=ps[:, 0:T - 1], scalar=tap(0), in1=y[:, 1:T],
                                                 op0=ALU.mult, op1=ALU.add).then_inc(conv_left, 1)
                        dve.wait_ge(conv_left, it * 2 + (n + 1))
                        dve.scalar_tensor_tensor(out=y[:, 0:T - 1], in0=ps[:, 1:T], scalar=tap(2), in1=y[:, 0:T - 1],
                                                 op0=ALU.mult, op1=ALU.add).then_inc(bank_free[half], 1)
                    dve.wait_ge(gelu_done, it + (c + 1))
                    dve.wait_ge(bank_free[1], free_before(L, UP_R0 + 2 * c + 1, j * 2) + 1)
                    dve.tensor_tensor(conv_b[c][:, :], conv_a[c][:, :], conv_b[c][:, :], ALU.mult).then_inc(glu_done, 1)
                    dve.wait_ge(g_hi_s, it + (c + 1))
                    g = bass.ds(j * 2 + c, 1)
                    dve.tensor_tensor(g_lo[:, g, :].rearrange("p s n -> p (s n)"), conv_b[c][:, :],
                                      g_hi[:, g, :].rearrange("p s n -> p (s n)").bitcast(F32), ALU.subtract).then_inc(g_lo_s, 1)

            def residual_down(L):
                done = 0
                for m in range(KT):
                    last = (m + 1) * FT - 1
                    if last % UT == UT - 1:
                        unit_result(L, DOWN0 + last // UT)
                    else:
                        done += 1
                        dve.wait_ge(mid_done, L * LAYER_M + (DOWN_M0 + done))
                    dve.tensor_tensor(z[:, m, :], z[:, m, :], U_BANK[m % 2][:, :], ALU.add).then_inc(bank_free[m % 2], 1)

            def rms(n, which, rs, tiles):
                dve.wait_ge(lstd, n + 1)
                dve.reciprocal(rs[:, :], rs[:, :]).then_inc(lrstd, 1)
                dve.wait_ge(lrstd, n + 1)

                def low(k):
                    dve.wait_ge(x_hi, (n + 1) * KT + (k + 1))
                    dve.tensor_tensor(xl[:, k, :], tiles[k % 4][:, :], xh[:, k, :].bitcast(F32), ALU.subtract).then_inc(x_lo, 1)

                for k in range(KT):
                    g = mpar[:, NORM_C + which * KT + k:NORM_C + which * KT + k + 1]
                    dst = out_t[:, k, :] if tiles is None else tiles[k % 4][:, :]
                    if tiles is not None and k >= 4:
                        dve.wait_ge(x_lo, (n + 1) * KT + (k - 3))
                    dve.scalar_tensor_tensor(out=dst, in0=z[:, k, :], scalar=g, in1=rs[:, :],
                                             op0=ALU.mult, op1=ALU.mult).then_inc(normed, 1)
                    if tiles is not None and k >= 1:
                        low(k - 1)
                if tiles is not None:
                    low(KT - 1)

            prep_steps = [0]

            def step():
                prep_steps[0] += 1
                return prep, 1

            def settled():
                return prep, prep_steps[0]

            tt, stt, ts = dve.tensor_tensor, dve.scalar_tensor_tensor, dve.tensor_scalar

            def phase_sines(l):
                n = 1 << l
                wc, ws = (powers[:, l, c, :].unsqueeze(2).to_broadcast([P, ST, n]) for c in range(2))
                c0, s0, s1 = phase[:, 0, :, 0:n], phase[:, 1, :, 0:n], phase[:, 1, :, n:2 * n]
                dve.wait_ge(phase_s, l + 1)
                dve.wait_ge(phase_c, l + 1)
                tt(s1, s0, wc, ALU.mult).then_inc(*step())
                tt(phase_td[:, :, 0:n], c0, ws, ALU.mult).then_inc(*step())
                dve.wait_ge(*settled())
                tt(s1, s1, phase_td[:, :, 0:n], ALU.add).then_inc(phase_s, 1)

            def c_powers():
                wide = lambda x: x.unsqueeze(2).to_broadcast([P, ST, 2 * SCH])
                s_cr, s_ci, den = (st[:, i, :] for i in (2, 3, 5))
                dve.reciprocal(den, den).then_inc(*step())
                dve.wait_ge(*settled())
                tt(s_cr, s_cr, den, ALU.mult).then_inc(*step())
                tt(s_ci, s_ci, den, ALU.mult).then_inc(*step())
                dve.wait_ge(*settled())
                cr, ci, ar, ai = (wide(st[:, i, :]) for i in (2, 3, 0, 1))
                c_r, c_i = c_st[:, 0, :, :], c_st[:, 1, :, :]
                t0, t1 = t_c[0][:, :, :], t_c[1][:, :, :]
                dve.wait_ge(mix_in, 16 * MIX_LOADS)
                dve.wait_ge(phase_s, LEVELS + 1)
                r, n = c_pow[:, :, 0, 0, :], c_pow[:, :, 1, 0, :]
                tt(r, c_r, cr, ALU.mult).then_inc(*step())
                tt(t0, c_i, ci, ALU.mult).then_inc(*step())
                tt(n, c_r, ci, ALU.mult).then_inc(*step())
                tt(t1, c_i, cr, ALU.mult).then_inc(*step())
                dve.wait_ge(*settled())
                tt(r, r, t0, ALU.subtract).then_inc(c_ready, 1)
                stt(out=n, in0=n, scalar=-1.0, in1=t1, op0=ALU.mult, op1=ALU.subtract).then_inc(c_ready, 1)
                for k in range(BT):
                    r, n, r2, n2 = (c_pow[:, :, c, i, :] for i in (k, k + 1) for c in (0, 1))
                    dve.wait_ge(c_ready, 2 * k + 2)
                    tt(r2, r, ar, ALU.mult).then_inc(*step())
                    tt(t0, n, ai, ALU.mult).then_inc(*step())
                    tt(n2, n, ar, ALU.mult).then_inc(*step())
                    tt(t1, r, ai, ALU.mult).then_inc(*step())
                    dve.wait_ge(*settled())
                    tt(r2, r2, t0, ALU.add).then_inc(c_ready, 1)
                    tt(n2, n2, t1, ALU.subtract).then_inc(c_ready, 1)

            def state_tiles(q):
                c, s = phase[:, 0, 4 * q:4 * q + 4, :], phase[:, 1, 4 * q:4 * q + 4, :]
                vr, vi = V_BANKS[:, :, 0:NB], V_BANKS[:, :, NB:2 * NB]
                zr, zi, t = states[q][:, 0, :, :], states[q][:, 1, :, :], t_s[:, :, :]
                dve.wait_ge(v_done, q + 1)
                if q == 0:
                    dve.wait_ge(c_ready, 2 * BT + 2)
                    dve.wait_ge(phase_c, LEVELS + 1)
                else:
                    dve.wait_ge(state_re, q)
                tt(zr, vr, c, ALU.mult).then_inc(*step())
                tt(t, vi, s, ALU.mult).then_inc(*step())
                dve.wait_ge(*settled())
                tt(zr, zr, t, ALU.add).then_inc(*step())
                tt(zi, vi, c, ALU.mult).then_inc(*step())
                dve.wait_ge(*settled())
                tt(t, vr, s, ALU.mult).then_inc(v_read, 1)
                dve.wait_ge(v_read, q + 1)
                tt(zi, zi, t, ALU.subtract).then_inc(*step())
                dve.wait_ge(*settled())
                for m in range(4):
                    for x in (zr, zi):
                        dve.tensor_tensor_scan(x[:, m, :], st[:, 4, 4 * q + m:4 * q + m + 1].to_broadcast([P, NB]), x[:, m, :], 0.0,
                                               ALU.mult, ALU.add).then_inc(scanned, 1)
                dve.wait_ge(scanned, 8 * q + 8)
                tt(t, zi, s, ALU.mult).then_inc(im_taken, 1)
                dve.wait_ge(re_taken, 2 * q + 1)
                tt(zr, zr, c, ALU.mult).then_inc(*step())
                dve.wait_ge(*settled())
                dve.wait_ge(im_taken, q + 1)
                tt(zr, zr, t, ALU.subtract).then_inc(state_re, 1)

            def mixer():
                n0 = MIX * 2
                dve.wait_ge(mean_done, n0)
                dve.memset(phase[:, 0, :, 0:1], 1.0).then_inc(phase_c, 1)
                dve.memset(phase[:, 1, :, 0:1], 0.0).then_inc(phase_s, 1)
                for l in range(LEVELS - 1):
                    phase_sines(l)
                rms(n0, 0, rstd_1, xn_1)
                phase_sines(LEVELS - 1)
                c_powers()
                for q in range(SP_T):
                    state_tiles(q)
                Y = (Y_BANK, O_BANK, V_BANKS[:, 0, :], V_BANKS[:, 1, :])
                dve.wait_ge(state_im, SP_T)
                for q in range(SP_T):
                    dve.wait_ge(y_done, q + 1)
                    dve.scalar_tensor_tensor(out=yg[:, q, :], in0=u_all[:, SP_T + q, :], scalar=mpar[:, SKIP_C + q:SKIP_C + q + 1],
                                             in1=Y[q][:, :], op0=ALU.mult, op1=ALU.add).then_inc(y_skip, 1)
                for q in range(SP_T):
                    dve.wait_ge(yg_hi_s, q + 1)
                    dve.tensor_tensor(yg_lo[:, q, :], yg[:, q, :], yg_hi[:, q, :].bitcast(F32), ALU.subtract).then_inc(yg_lo_s, 1)

                def mix_low(m):
                    dve.wait_ge(mix_hi_s, m + 1)
                    dve.tensor_tensor(mix_lo[:, m, :], u_all[:, m, :], mix_hi[:, m, :].bitcast(F32), ALU.subtract)\
                        .then_inc(mix_lo_s, 1)

                for m in range(SP_T):
                    mix_low(m)
                for m in range(SP_T):
                    dve.wait_ge(bank_free[m % 2], free_before(MIX, GLU_R0 + m) + 1)
                    dve.tensor_tensor(u_all[:, SP_T + m, :], yg[:, m, :], glu_sig[m % 2][:, :], ALU.mult).then_inc(y_ssm, 1)
                for m in range(SP_T, KT):
                    mix_low(m)
                for m in range(KT):
                    unit_result(MIX, MOUT_U0 + m)
                    dve.tensor_tensor(z[:, m, :], z[:, m, :], U_BANK[m % 2][:, :], ALU.add).then_inc(bank_free[m % 2], 1)
                rms(n0 + 1, 1, rstd_2, xn_2)
                with dve.Fori(0, FT // 2) as j:
                    for c in range(2):
                        unit_result(MIX, GU_U0 + 2 * c + 1, j * 4)
                        dve.wait_ge(bank_free[0], free_before(MIX, GU_R0 + 2 * c, j * 2) + 1)
                        dve.tensor_tensor(hidden[c][:, :], U_BANK[1][:, :], silu[c][:, :], ALU.mult).then_inc(bank_free[1], 1)
                        dve.wait_ge(gu_hi, j * 2 + (c + 1))
                        g = bass.ds(j * 2 + c, 1)
                        dve.tensor_tensor(g_lo[:, g, :].rearrange("p s n -> p (s n)"), hidden[c][:, :],
                                          g_hi[:, g, :].rearrange("p s n -> p (s n)").bitcast(F32), ALU.subtract).then_inc(gu_lo, 1)
                done = 0
                for m in range(KT):
                    last = (m + 1) * FT - 1
                    if last % UT == UT - 1:
                        unit_result(MIX, MDOWN_U0 + last // UT)
                    else:
                        done += 1
                        dve.wait_ge(mid_done, MIX * LAYER_M + (MDOWN_M0 + done))
                    dve.tensor_tensor(z[:, m, :], z[:, m, :], U_BANK[m % 2][:, :], ALU.add).then_inc(bank_free[m % 2], 1)
                rms(n0 + 2, 2, rstd_3, None)

            for b in range(2):
                dve.sem_inc(s_free[b], 1)
            dve.sem_inc(ot_read, 2)
            dve.sem_inc(o_norm, 4)
            dve.memset(mean_w[:, :], 1.0 / D).then_inc(consts_set, 1)
            dve.memset(ln_eps[:, :], LN_EPS).then_inc(consts_set, 1)
            dve.memset(gn_eps[:, :], GN_EPS).then_inc(consts_set, 1)
            dve.memset(rms_eps[:, :], RMS_EPS).then_inc(rms_set, 1)
            for k in range(KT):
                dve.wait_ge(x_hi, k + 1)
                dve.tensor_tensor(xl[:, k, :], z[:, k, :], xh[:, k, :].bitcast(F32), ALU.subtract).then_inc(x_lo, 1)
            dve.wait_ge(decay_step, 3)
            flat = decay[:, :, :].rearrange("p d n -> p (d n)")
            dve.tensor_scalar(decay_b[:, :], flat, 0.0, None, ALU.min).then_inc(decay_step, 1)
            dve.wait_ge(decay_step, 4)
            dve.tensor_tensor(flat, decay_b[:, :], decay_a[:, :], ALU.subtract).then_inc(decay_step, 1)
            dve.wait_ge(decay_step, 5)
            dve.wait_ge(mpar_in, 16)
            with dve.Fori(0, DEPTH) as L:
                dve.wait_ge(tables_in, L * 48 + 48)
                stand(dve, dve_passed)
                with dve.Fori(0, 4) as t:
                    attention(L, t)
                split_branch_inputs(L)
                with dve.Fori(0, 2) as i:
                    branches(L, i)
                residual_out(L)
                norm(L, 0)
                ple(L)
                with dve.Fori(0, FT // 2) as j:
                    up(L, j)
                residual_down(L)
                norm(L, 1)
            mixer()


def weight_tiles(w):
    import numpy as np
    k, m = w.shape
    return np.ascontiguousarray(w.reshape(k // P, P, m // P, P).transpose(0, 2, 1, 3))


def layer_stream(inp, i):
    w_in, w_a, w_b, w_o, w_up, w_dn, w_pg, w_pp = (
        weight_tiles(inp[n][i]) for n in
        ("w_in", "w_branch_a", "w_branch_b", "w_out", "w_up", "w_down", "w_ple_gate", "w_ple_proj"))
    col = lambda w, m: [w[k, m] for k in range(w.shape[0])]
    q_na, k_na, v_na, q_r, k_r, v_r, g_r, gate = 0, 4, 8, 12, 16, 20, 28, 36
    out = []
    for t in range(4):
        for m in (q_na + t, k_na + t, v_na + t, q_r + t, k_r + t):
            out += col(w_in, m)
        for k in range(KT):
            out += [w_in[k, v_r + 2 * t], w_in[k, v_r + 2 * t + 1]]
        for m in (g_r + 2 * t, g_r + 2 * t + 1, gate + 3 * t, gate + 3 * t + 1, gate + 3 * t + 2):
            out += col(w_in, m)
    for h in range(2):
        for g in range(2):
            out += col(w_in, gate + 12 + 2 * h + g)
        for w in (w_a, w_b):
            for m in range(4):
                out += col(w, 4 * h + m)
    for m in range(KT):
        out += col(w_o, m)
    for h in range(2):
        for w in (w_pg, w_pp):
            for m in range(4):
                out += col(w, 4 * h + m)
    for j in range(FT):
        out += col(w_up, j) + col(w_up, FT + j)
    for m in range(KT):
        out += col(w_dn, m)
    return out


def mixer_stream(inp):
    w_in, w_glu, w_o, w_g, w_up, w_dn = (
        weight_tiles(inp[n + "_2"][0]) for n in ("w_in", "w_glu", "w_out", "w_gate", "w_up", "w_down"))
    col = lambda w, m: [w[k, m] for k in range(w.shape[0])]
    out = []
    for m in range(KT):
        out += col(w_in, (m + SP_T) % KT)
    for m in range(SP_T):
        out += col(w_glu, m)
    for m in range(KT):
        out += col(w_o, m)
    for j in range(FT):
        out += col(w_g, j) + col(w_up, j)
    for m in range(KT):
        out += col(w_dn, m)
    return out


def unit_array(tiles):
    import numpy as np
    w = np.stack(tiles)
    return np.ascontiguousarray(w.reshape(-1, UT, P, P).transpose(0, 2, 1, 3)).reshape(-1, P, UT * P)


def feature_major(v):
    import numpy as np
    return np.ascontiguousarray(np.moveaxis(v.reshape(*v.shape[:-1], -1, P), -1, 0))


def layout(inp):
    import numpy as np
    f32 = np.float32
    a = {}
    tiles = []
    for i in range(DEPTH):
        tiles += layer_stream(inp, i)
    tiles += mixer_stream(inp)
    a["w"] = unit_array(tiles)
    a["x"] = np.ascontiguousarray(inp["x"][0].T.reshape(KT, P, T).transpose(1, 0, 2))
    a["p"] = np.ascontiguousarray(inp["p"][:, 0].transpose(0, 2, 1).reshape(DEPTH, PLE_T, P, T).transpose(0, 2, 1, 3))
    a["lnp"] = feature_major(np.stack([inp["ln1_g"], inp["ln1_b"], inp["ln2_g"], inp["ln2_b"]], 1))
    a["convp"] = feature_major(np.concatenate([inp["conv_w"], inp["conv_b"][:, None]], 1))
    rates = np.stack([inp["ret_decay_f"].reshape(-1), inp["ret_decay_b"].reshape(-1)])
    a["decay"] = np.ascontiguousarray(np.broadcast_to(rates[None], (P, 2, DEPTH * RET_H)))
    rows, cols = np.arange(ROWS), np.arange(16)
    dr = rows[None, :] - rows[:, None] + WIN_ROWS - 1
    dc = 16 * np.arange(3)[None, :, None] - 16 + cols[None, None, :] - cols[:, None, None] + WIN_COLS - 1
    table = np.pad(inp["na_rpb"], ((0, 0), (0, 0), (0, 0), (16, 16)))
    spread = table[:, :, dr[:, None, None, :, None], dc[None, :, :, None, :] + 16]
    a["bias"] = np.ascontiguousarray(spread.reshape(DEPTH, 4, 2, P, 3 * P).transpose(0, 1, 3, 2, 4)).reshape(DEPTH * 4, P, 6 * P)
    a["ident"] = np.eye(P, dtype=f32)
    half = RET_DK // 2
    sw = np.zeros((P, P), f32)
    sw[np.arange(half) + half, np.arange(half)] = 1.0
    sw[np.arange(half), np.arange(half) + half] = 1.0
    a["swap"] = sw
    inv = f32(10000.0) ** (-np.arange(half, dtype=f32) / f32(half))
    ang = np.arange(T, dtype=f32)[None, :] * inv[:, None]
    c, s = np.cos(ang), np.sin(ang)
    a["rope"] = np.ascontiguousarray(np.stack([np.concatenate([c, c]), np.concatenate([-s, s])], 1).astype(f32))
    a["delta"] = (np.arange(7 * P)[None, :] - 3 * P - np.arange(P)[:, None]).astype(f32)
    masks = np.zeros((P, 3, 3, ROWS, 16), f32)
    for m, j in enumerate((0, 1, CB - 1)):
        q = 16 * j + cols
        first = np.clip(q - WIN_COLS // 2, 0, GRID_W - WIN_COLS)
        key = 16 * (j - 1) + 16 * np.arange(3)[:, None] + cols[None, :]
        ok = (key[None] >= first[:, None, None]) & (key[None] < first[:, None, None] + WIN_COLS)
        neg = np.where(ok, 0.0, -1e30).astype(f32)
        masks[:, m] = np.tile(neg, (ROWS, 1, 1))[:, :, None, :]
    a["masks"] = masks.reshape(P, 3, 3 * P)
    two = SG // ST
    by_channel = lambda v: np.repeat(v.reshape(SP_T, P // SCH, SN), SCH, 1).transpose(1, 0, 2).reshape(P, SP_T * SN)
    by_state = lambda v: v.reshape(ST, two * SN).T
    re, im = inp["lam_re_2"][0], inp["lam_im_2"][0]
    a["lam"] = np.stack([np.concatenate([by_channel(v), by_state(v)], 1) for v in (re, im)], 1)
    log_dt = inp["log_dt_2"][0]
    a["log_dt"] = np.concatenate([np.repeat(log_dt.reshape(SP_T, P // SCH).T, SCH, 0),
                                  np.repeat(log_dt.reshape(ST, two).T, SN, 0)], 1)
    b_cs = np.stack([inp["b_re_2"][0], inp["b_im_2"][0]])
    a["w_b"] = b_cs.reshape(2, SP_T, P // SCH, SN, SCH).transpose(2, 4, 0, 1, 3).reshape(P, 2, SP_T, SN)
    apart = np.zeros((two, SN, 2, ST, two, SCH), f32)
    for h in range(two):
        apart[h, :, :, :, h] = b_cs.reshape(2, ST, two, SN, SCH)[:, :, h].transpose(2, 0, 1, 3)
    a["b_st"] = apart.reshape(P, 2, ST, two * SCH)
    c_cs = np.stack([inp["c_re_2"][0], inp["c_im_2"][0]])
    apart = np.zeros((two, SN, 2, ST, two, SCH), f32)
    for h in range(two):
        apart[h, :, :, :, h] = c_cs.reshape(2, ST, two, SCH, SN)[:, :, h].transpose(3, 0, 1, 2)
    a["c_st"] = apart.reshape(P, 2, ST, two * SCH)
    a["w_pool"] = inp["w_pool_2"][0].transpose(1, 0, 2)
    part = np.arange(P)[:, None]
    counts = [np.broadcast_to((f32(1.0) / np.minimum(np.arange(1, 17), w).astype(f32))[None], (P, 16)) for w in WINDOWS]
    cols = [feature_major(v) for v in (inp["norm_mix_2"][0], inp["norm_ffn_2"][0], inp["norm_final_2"], inp["pool_scale_2"][0],
                                       inp["d_skip_2"][0].reshape(-1), inp["b_glu_2"][0])]
    a["mpar"] = np.concatenate(cols + [(part // SCH % 2 == np.arange(2)).astype(f32),
                                       (part // (2 * SCH) == np.arange(4)).astype(f32)] + counts, 1)
    return {n: np.ascontiguousarray(v) for n, v in a.items()}


def kernel(**inputs):
    import numpy as np
    import concourse.bacc as bacc
    from concourse.bass_utils import run_bass_kernel_spmd

    arrays = layout({n: np.asarray(v) for n, v in inputs.items()})
    nc = bacc.Bacc("TRN2", target_bir_lowering=False, num_devices=1)
    dram = {n: nc.dram_tensor(f"in_{n}", v.shape, F32, kind="ExternalInput").ap() for n, v in arrays.items()}
    out = nc.dram_tensor("out_x", (P, KT, T), F32, kind="ExternalOutput").ap()
    build(nc, dram, out)
    r = run_bass_kernel_spmd(nc, [{f"in_{n}": v for n, v in arrays.items()}], core_ids=[0])
    got = r.results[0]["out_x"]
    return np.ascontiguousarray(got.transpose(1, 0, 2).reshape(D, T).T).reshape(1, T, D)
```

```python
import concourse.bass as bass
from concourse import mybir
from contextlib import ExitStack

F32 = mybir.dt.float32
F32R = mybir.dt.float32r
ALU = mybir.AluOpType
ACT = mybir.ActivationFunctionType

P = 128
T = 512
D = 1024
KT = D // P
DEPTH = 2
GRID_W, ROWS, WIN_ROWS, WIN_COLS = 64, 8, 8, 16
NA_HEADS, NA_DH = 8, 64
CB = GRID_W // 16
RET_H, RET_DK, RET_DV = 4, 128, 256
FF = 2816
FT = FF // P
PLE_T = 2
ALPHA = (2.0 * DEPTH) ** 0.25
LN_EPS, GN_EPS, RMS_EPS = 1e-5, 1e-6, 1e-6
RING = 4
UT = 8

ATT_U, BR_U, OUT_U, PLE_U, UP_U, DOWN_U = 4 * 12, 2 * 8, 8, 10, 2 * FT, FT
ATT0 = 0
BR0 = ATT0 + ATT_U
OUT0 = BR0 + BR_U
PLE0 = OUT0 + OUT_U
UP0 = PLE0 + PLE_U
DOWN0 = UP0 + UP_U
LAYER_U = DOWN0 + DOWN_U
ATT_R0 = 0
BR_R0 = ATT_R0 + 48
OUT_R0 = BR_R0 + 20
PLE_R0 = OUT_R0 + 8
UP_R0 = PLE_R0 + 12
DOWN_R0 = UP_R0 + 44
LAYER_R = DOWN_R0 + 8
BR_M0 = 0
PLE_M0 = BR_M0 + 4
DOWN_M0 = PLE_M0 + 6
LAYER_M = DOWN_M0 + 6
MIX = DEPTH
MIN_U0, GLU_U0, MOUT_U0, GU_U0 = 0, 8, 10, 18
MDOWN_U0 = GU_U0 + UP_U
MIX_U = MDOWN_U0 + DOWN_U
MIN_R0, GLU_R0, MOUT_R0, GU_R0 = 0, 8, 12, 20
MDOWN_R0 = GU_R0 + UP_U
GLU_M0, MDOWN_M0 = 0, 2
N_UNITS = DEPTH * LAYER_U + MIX_U
MIX_LOADS = 4
WINDOWS = (2, 4, 8, 16)
SP_T = 4
SG, SCH, SN = 32, 16, 64
ST = SG * SN // P
BT = 2
NB = T // BT
LAM = SP_T * SN + ST
NORM_C, POOLS_C, SKIP_C, BGLU_C, HALF_C, QUART_C, INV_C = 0, 24, 28, 32, 36, 38, 42
MPAR = INV_C + SP_T * 16
LEVELS = NB.bit_length() - 1
QUARTER = 1.5707963267948966
QUARTER_HI = 1.5703125
QUARTER_MID = 0.00048375129699707031
QUARTER_LO = QUARTER - QUARTER_HI - QUARTER_MID
LN2 = 0.6931471805599453
LN2_HI = 0.693359375
LN2_LO = LN2 - LN2_HI
ROUND = 1.5 * 2.0 ** 23
EXP_MAX, EXP_MIN = 88.0, -87.0
EXP_C = [1 / 5040, 1 / 720, 1 / 120, 1 / 24, 1 / 6, 1 / 2, 1.0]
SIN_C = [1 / 362880, -1 / 5040, 1 / 120, -1 / 6]
COS_C = [-1 / 3628800, 1 / 40320, -1 / 720, 1 / 24, -1 / 2]


def build(nc, a, out):
    ctx = ExitStack()
    with ctx:
        at = [nc.sbuf_base]

        def place(name, shape, dt=F32, offset=None):
            size = 4
            for s in shape[1:]:
                size *= s
            if offset is None:
                offset, at[0] = at[0], at[0] + (size + 31) // 32 * 32
            return nc.alloc_sbuf_tensor_at(name, shape, dt, offset=offset)

        def sem(name):
            return ctx.enter_context(nc.semaphore(name))

        at[0] = (at[0] + 31) // 32 * 32
        stage = [place(f"stage{i}", [P, UT, P]) for i in range(RING)]
        w_hi = [place(f"w_hi{i}", [P, UT, P], F32R) for i in range(RING)]
        w_lo = [place(f"w_lo{i}", [P, UT, P], F32R) for i in range(RING)]
        xh = place("xh", [P, KT, T], F32R)
        xl = place("xl", [P, KT, T], F32R)
        z_at = at[0]
        z = place("z", [P, KT, T])
        ident = place("ident", [P, P])
        mean_w = place("mean_w", [P, P])
        pick = place("pick", [P, 4, P])
        ln_eps = place("ln_eps", [P, 1])
        warm = place("warm", [P, 1])
        gn_eps = place("gn_eps", [P, 1])
        lnp = place("lnp", [P, DEPTH, 4, KT])
        convp = place("convp", [P, DEPTH, 4, 2 * FT])
        decay = place("decay", [P, 2, DEPTH * RET_H])
        decay_a = place("decay_a", [P, 2 * DEPTH * RET_H])
        decay_b = place("decay_b", [P, 2 * DEPTH * RET_H])
        at[0] = (at[0] + 31) // 32 * 32
        c_at = at[0]
        rope = place("rope", [P, 2, T])
        delta = place("delta", [P, 7 * P])
        masks = place("masks", [P, 3, 3 * P])
        conv_a = [place(f"conv_a{i}", [P, T], offset=c_at + 2048 * i) for i in range(2)]
        conv_b = [place(f"conv_b{i}", [P, T], offset=c_at + 4096 + 2048 * i) for i in range(2)]
        a_at = at[0]
        gates = place("gates", [P, 16, T])
        merged_p = place("merged_p", [P, 16, T], F32R, offset=a_at)
        yb = place("yb", [P, KT, T])
        yb_lo = place("yb_lo", [P, KT, T], F32R, offset=a_at + 32768)
        ya = place("ya", [P, 4, T])
        ya_lo = place("ya_lo", [P, 4, T], F32R, offset=a_at + 49152)
        tmp_at = at[0]
        yb_hi = place("yb_hi", [P, KT, T], F32R)
        ya_hi = place("ya_hi", [P, 4, T], F32R)
        p_at = at[0]
        p_raw = place("p_raw", [P, PLE_T, T])
        p_hi = place("p_hi", [P, PLE_T, T], F32R, offset=a_at + 32768)
        p_lo = place("p_lo", [P, PLE_T, T], F32R, offset=a_at + 36864)
        s_t = place("s_t", [P, 8, 3 * P], offset=z_at)
        pr_hi = place("pr_hi", [P, 4, T], F32R, offset=z_at)
        pr_lo = place("pr_lo", [P, 4, T], F32R, offset=z_at + 8192)
        bias = place("bias", [P, 2, 3 * P], offset=z_at + 12288)
        na_q, na_k = (place(f"na_{n}", [P, T], F32R, offset=tmp_at + 2048 * i) for i, n in enumerate("qk"))
        r_v_lo = place("r_v_lo", [P, 4, RET_DV], F32R, offset=tmp_at)
        na_v = place("na_v", [P, CB, P], offset=tmp_at + 4096)
        r_q, r_k = (place(f"r_{n}", [P, T], offset=tmp_at + 6144 + 2048 * i) for i, n in enumerate("qk"))
        r_lo = [place(f"r_{n}_lo", [P, T], F32R, offset=tmp_at + 6144 + 2048 * i) for i, n in enumerate("qk")]
        r_tmp = place("r_tmp", [P, T], offset=tmp_at + 10240)
        na_lo = [place(f"na_{n}_lo", [P, T], F32R, offset=tmp_at + 12288 + 2048 * i) for i, n in enumerate("qk")]
        r_v = place("r_v", [P, 4, RET_DV], F32R, offset=tmp_at + 12288)
        r_hi = [place(f"r_{n}_hi", [P, T], F32R, offset=tmp_at + 16384 + 2048 * i) for i, n in enumerate("qk")]
        sg = place("sg", [P, 2, T], offset=tmp_at + 16384)
        pt = place("pt", [P, 2, 3 * P], offset=tmp_at + 20480)
        o_n = place("o_n", [P, 4, RET_DV], offset=tmp_at + 23552)
        pr = [place(f"pr{i}", [P, T], offset=tmp_at + 23552 + 2048 * i) for i in range(2)]
        d_tmp = place("d_tmp", [P, 7 * P], offset=tmp_at + 23552)
        d_tab = place("d_tab", [P, 7 * P])
        m_tmp = [place(f"m_tmp{i}", [P, T], offset=z_at + 2048 * i) for i in range(2)]
        sq = [place(f"sq{i}", [P, T], offset=a_at + 8192 + 2048 * i) for i in range(4)]
        rstd = place("rstd", [P, T], offset=a_at + 16384)
        p_sig = [place(f"p_sig{i}", [P, T], offset=a_at + 18432 + 2048 * i) for i in range(4)]
        g_hi = place("g_hi", [P, FT, T], F32R, offset=a_at)
        g_lo = place("g_lo", [P, FT, T], F32R, offset=a_at + FT * T * 4)
        at[0] = max(at[0], a_at + 2 * FT * T * 4)
        z_sum = place("z_sum", [P, T], offset=c_at)
        abar = place("abar", [P, 2, SP_T, SN])
        st = place("st", [P, 10, ST])
        powers = place("powers", [P, LEVELS, 2, ST])
        mpar = place("mpar", [P, MPAR])
        rms_eps = place("rms_eps", [P, 1])
        dt = place("dt", [P, 4, SP_T + ST])
        assert at[0] <= nc.sbuf_usable_end, (at[0], nc.sbuf_usable_end)
        eig = [place(f"eig{i}", [P, LAM], offset=a_at + 16384 + LAM * 4 * i) for i in range(8)]
        lam = place("lam", [P, 2, LAM], offset=a_at + 16384 + LAM * 32)
        int_at = a_at + 16384 + LAM * 40
        eig_tmp = place("eig_tmp", [P, LAM], offset=a_at + 16384 + LAM * 48)
        exp2 = place("exp2", [P, LAM], mybir.dt.int32, offset=int_at)
        exp2_dt = place("exp2_dt", [P, SP_T + ST], mybir.dt.int32, offset=int_at + LAM * 4)
        phase = place("phase", [P, 2, ST, NB], offset=c_at)
        u_all = place("u_all", [P, KT, T], offset=c_at + 32768)
        mix_lo = place("mix_lo", [P, KT, T], F32R, offset=c_at + 32768)
        w_b = place("w_b", [P, BT, 2, SP_T, SN], offset=c_at + 49152)
        t_p = place("t_p", [P, 4, NB], offset=c_at + 49152)
        w_b2 = place("w_b2", [P, BT, 2, SP_T, 2, SN], offset=c_at + 53248)
        phase_tp = place("phase_tp", [P, ST, NB // 2], offset=c_at + 53248)
        c_pow = place("c_pow", [P, ST, 2, BT + 1, 2 * SCH], offset=c_at + 61440)
        phase_td = place("phase_td", [P, ST, NB // 2], offset=c_at + 61440)
        k_conv = place("k_conv", [P, SP_T, BT, P], offset=c_at + 73728)
        b_st = place("b_st", [P, 2, ST, 2 * SCH], offset=c_at + 77824)
        c_st = place("c_st", [P, 2, ST, 2 * SCH], offset=c_at + 81920)
        t_c = [place(f"t_c{i}", [P, ST, 2 * SCH], offset=c_at + 86016 + 2048 * i) for i in range(2)]
        run = [place(f"run{i}", [P, T], offset=c_at + 90112 + 2048 * i) for i in range(2)]
        w_pool = place("w_pool", [P, SP_T, P], offset=c_at + 94208)
        t_s = place("t_s", [P, 4, NB], offset=c_at + 96256)
        yg = place("yg", [P, SP_T, T], offset=c_at)
        yg_hi = place("yg_hi", [P, SP_T, T], F32R, offset=c_at + 8192)
        yg_lo = place("yg_lo", [P, SP_T, T], F32R, offset=c_at + 16384)
        glu_sig = [place(f"glu_sig{i}", [P, T], offset=c_at + 24576 + 2048 * i) for i in range(2)]
        mix_hi = place("mix_hi", [P, KT, T], F32R, offset=c_at + 49152)
        sq_1 = [place(f"sq_1{i}", [P, T], offset=c_at + 32768 + 2048 * i) for i in range(4)]
        xn_1 = [place(f"xn_1{i}", [P, T], offset=c_at + 40960 + 2048 * i) for i in range(4)]
        rstd_1 = place("rstd_1", [P, T], offset=c_at + 96256)
        sq_2 = [place(f"sq_2{i}", [P, T], offset=c_at + 65536 + 2048 * i) for i in range(4)]
        xn_2 = [place(f"xn_2{i}", [P, T], offset=c_at + 2048 * i) for i in range(4)]
        rstd_2 = place("rstd_2", [P, T], offset=c_at + 98304)
        xh_at = z_at - 2 * KT * T * 4
        sq_3 = [place(f"sq_3{i}", [P, T], offset=c_at + 2048 * i) for i in range(4)]
        out_t = place("out_t", [P, KT, T], offset=xh_at)
        rstd_3 = place("rstd_3", [P, T], offset=xh_at + KT * T * 4)
        states = [place("states0", [P, 2, 4, NB], offset=c_at + 81920)]
        states += [place(f"states{q}", [P, 2, 4, NB], offset=xh_at + 8192 * (q - 1)) for q in range(1, SP_T)]
        silu = [place(f"silu{i}", [P, T], offset=c_at + 2048 * i) for i in range(2)]
        hidden = [place(f"hidden{i}", [P, T], offset=c_at + 4096 + 2048 * i) for i in range(2)]
        small = place("small", [P, 64])
        row_max, row_nmax, row_sum, row_inv = (small[:, 8 * i:8 * i + 8] for i in range(4))
        gn_std, gn_inv = small[:, 32:36], small[:, 36:40]
        lg_now = small[:, 40:42]
        gn_st = place("gn_st", [P, 4, 6])
        gn_mv = place("gn_mv", [P, 4, 2])
        assert at[0] <= nc.sbuf_usable_end, (at[0], nc.sbuf_usable_end)

        psum = ctx.enter_context(nc.psum_tensor("psum", [P, 8, T], F32))
        bank = [psum[:, i, :] for i in range(8)]
        U_BANK, S_BANK, T_BANK, Y_BANK, O_BANK = bank[0:2], bank[2:4], bank[4:6], bank[6], bank[7]
        V_BANKS = psum[:, 2:6, :]
        PLE_BANK = (*T_BANK, Y_BANK, O_BANK)

        landed = [sem(f"unit_landed{i}") for i in range(RING)]
        hi_done = sem("unit_hi_done")
        lo_done = sem("unit_lo_done")
        unit_used = sem("unit_used")
        mid_done = sem("mid_unit_result_done")
        bank_free = [sem(f"unit_bank_free{i}") for i in range(2)]
        params_in = sem("params_in")
        x_in = [sem(f"x_in{i}") for i in range(4)]
        consts_set = sem("consts_set")
        x_hi, x_lo = sem("x_hi"), sem("x_lo")
        decay_step = sem("decay_step")
        tables_in = sem("tables_in")
        bias_in = sem("bias_in")
        na_hi, rope_hi, rope_lo, rv_hi = sem("na_qk_hi"), sem("rope_hi"), sem("rope_lo"), sem("ret_v_hi")
        pr_hi_s, pr_lo_s = sem("ret_scores_hi"), sem("ret_scores_lo")
        vt_done, v_ready = sem("v_turned"), sem("v_ready")
        dterm_copy = sem("decay_rates_copied")
        dterm, dtab_ready = sem("decay_terms"), sem("decay_table_ready")
        score_done = sem("score_done")
        s_free = [sem(f"score_bank_free{i}") for i in range(2)]
        masked, nmax_ready = sem("scores_masked"), sem("neg_max_ready")
        exp_done, inv_ready, p_ready = sem("exp_done"), sem("row_inverse"), sem("probs_ready")
        pt_done, pt_ready, pv_done = sem("probs_turned"), sem("probs_t_ready"), sem("pv_done")
        ya_ready = sem("ya_ready")
        rope_in, rope_sin, rope_cos, rope_ready = (sem(f"rope_{n}") for n in ("in", "sin", "cos", "ready"))
        o_done, gn_stat, gn_aggr = sem("ret_out_done"), sem("gn_stats"), sem("gn_aggr")
        std_ready, ginv_ready, o_norm = sem("gn_std"), sem("gn_inv"), sem("ret_out_normed")
        ot_done, ot_read = sem("ret_out_turned"), sem("yb_ready")
        sig_ready = sem("silu_sigmoid")
        br_hi, br_lo = sem("branch_in_hi"), sem("branch_in_lo")
        merged, merged_hi, merged_lo = sem("merged"), sem("merged_hi"), sem("merged_lo")
        z_ready, mean_done, centred = sem("z_ready"), sem("mean_done"), sem("centred")
        z_summed, sq_summed, square_mean = sem("z_summed"), sem("squares_summed"), sem("square_mean_done")
        squared, sq_used = sem("squared"), sem("square_used")
        rstd_spread = sem("rstd_spread")
        lstd, lrstd, normed = sem("ln_std"), sem("ln_rstd"), sem("ln_normed")
        x_ready = sem("x_ready")
        p_in, p_hi_s, p_lo_s = sem("p_in"), sem("p_hi_done"), sem("p_lo_done")
        ple_term, zpre = sem("ple_term"), sem("z_pre_ready")
        conv_mid, conv_left = sem("conv_centre"), sem("conv_left")
        gelu_done, glu_done = sem("gelu_done"), sem("glu_done")
        g_hi_s, g_lo_s = sem("g_hi_done"), sem("g_lo_done")
        out_done = sem("out_done")
        mix_in = sem("mixer_params_in")
        lam_in = sem("eigenvalues_in")
        mpar_in = sem("mixer_small_params_in")
        prep, lam_step, powers_ready, c_ready = sem("ssm_prep_step"), sem("ssm_eigenvalue_step"), sem("ssm_phase_powers"), sem("ssm_c_powers")
        phase_c, phase_s, phase_step = sem("phase_cosines"), sem("phase_sines"), sem("phase_step")
        wb_step, wb_ready, wb_apart = sem("ssm_b_step"), sem("ssm_b_powers"), sem("ssm_b_apart")
        kernel_done, kernel_ready = sem("ssm_kernel_done"), sem("ssm_kernel_ready")
        pool_step, pooled, pool_done, y_pool = (sem("pool_step"), sem("pooled"), sem("pool_product"), sem("y_pool"))
        v_done, v_read, turn_step = sem("ssm_block_inputs"), sem("ssm_block_inputs_read"), sem("ssm_turn_step")
        scanned, re_taken, im_taken = sem("ssm_scanned"), sem("ssm_re_taken"), sem("ssm_im_taken")
        state_re, state_im = sem("ssm_state_re"), sem("ssm_state_im")
        y_done, y_skip, y_gelu = sem("ssm_y_done"), sem("ssm_y_skip"), sem("ssm_y_gelu")
        yg_hi_s, yg_lo_s, y_ssm = sem("yg_hi"), sem("yg_lo"), sem("y_ssm")
        mix_hi_s, mix_lo_s = sem("mix_hi"), sem("mix_lo")
        gu_hi, gu_lo = sem("hidden_hi"), sem("hidden_lo")
        rms_set = sem("rms_eps_set")
        dve_passed = sem("dve_passed")

        block = ctx.enter_context(nc.Block())

        def stand(eng, passed):
            eng.sem_inc(passed, 1)

        def block_view(ap):
            return ap.rearrange("p (r b c) -> p b r c", r=ROWS, b=CB)

        def kblocks(j):
            return range(1 if j == 0 else 0, 2 if j == CB - 1 else 3)

        def mask_of(j):
            return 0 if j == 0 else 2 if j == CB - 1 else 1

        def free_before(L, r, i=0):
            return L * (LAYER_R // 2) + i + r // 2 + 1

        def after_result(L, r, i=0):
            return bank_free[r % 2], free_before(L, r, i) + 1

        @block.sync
        def _(sp):
            def load(s, u):
                src = a["w"][u] if isinstance(u, int) else a["w"][bass.ds(u, 1)].rearrange("s p n -> p (s n)")
                sp.dma_start(stage[s][:, :, :].rearrange("p t n -> p (t n)"), src).then_inc(landed[s], 16)

            load(0, 0)
            for h in range(4):
                sp.dma_start(z[:, 2 * h:2 * h + 2, :], a["x"][:, 2 * h:2 * h + 2, :]).then_inc(x_in[h], 16)
                if h == 0:
                    load(1, 1)
            load(2, 2)
            load(3, 3)
            with sp.Fori(1, N_UNITS // RING) as n:
                for s in range(RING):
                    sp.wait_ge(lo_done, n * RING + (s - RING + 1))
                    load(s, n * RING + s)
            for first in range(0, KT, 2):
                sp.wait_ge(normed, (MIX * 2 + 2) * KT + (first + 2))
                sp.dma_start(out[:, first:first + 2, :], out_t[:, first:first + 2, :]).then_inc(out_done, 16)
            sp.wait_ge(out_done, 16 * (KT // 2))

        @block.gpsimd
        def _(pool):
            def low_part(n, s):
                pool.wait_ge(hi_done, n * RING + (s + 1))
                pool.tensor_tensor(w_lo[s][:, :, :], stage[s][:, :, :], w_hi[s][:, :, :].bitcast(F32),
                                   ALU.subtract).then_inc(lo_done, 1)

            tt, ts = pool.tensor_tensor, pool.tensor_scalar
            lam_steps = [0]

            def step():
                lam_steps[0] += 1
                return lam_step, 1

            def settled():
                return lam_step, lam_steps[0]

            def two_ops(out, in0, scalar, in1, op0, op1):
                tmp = eig_tmp[:, 0:in0.shape[-1]]
                pool.wait_ge(*settled())
                ts(tmp, in0, scalar, None, op0).then_inc(*step())
                pool.wait_ge(*settled())
                tt(out, tmp, in1, op1).then_inc(*step())

            def exp_rest(x, k, bits):
                ts(x, x, EXP_MAX, EXP_MIN, ALU.min, ALU.max).then_inc(*step())
                pool.wait_ge(*settled())
                ts(k, x, 1.0 / LN2, ROUND, ALU.mult, ALU.add).then_inc(*step())
                pool.wait_ge(*settled())
                ts(k, k, ROUND, None, ALU.subtract).then_inc(*step())
                pool.wait_ge(*settled())
                ts(bits, k, 127.0, 2.0 ** 23, ALU.add, ALU.mult).then_inc(*step())
                for part in (LN2_HI, LN2_LO):
                    two_ops(out=x, in0=k, scalar=-part, in1=x, op0=ALU.mult, op1=ALU.add)
                    pool.wait_ge(*settled())

            def exp_series(dst, x, p, bits):
                ts(p, x, EXP_C[0], None, ALU.mult).then_inc(*step())
                for c in EXP_C[1:]:
                    pool.wait_ge(*settled())
                    two_ops(out=p, in0=p, scalar=c, in1=x, op0=ALU.add, op1=ALU.mult)
                pool.wait_ge(*settled())
                two_ops(out=dst, in0=p, scalar=1.0, in1=bits.bitcast(F32), op0=ALU.add, op1=ALU.mult)
                pool.wait_ge(*settled())

            x, mag, angle, k, p, y, sine, cosm1 = (e[:, :] for e in eig)
            chans, by_state = slice(0, SP_T * SN), slice(SP_T * SN, LAM)
            per_q = lambda v: v.rearrange("p (q n) -> p q n", n=SN)

            def growth_and_angle():
                pool.wait_ge(lam_in, 32)
                exp_rest(dt[:, 0, :], dt[:, 1, :], exp2_dt[:, :])
                exp_series(dt[:, 3, :], dt[:, 0, :], dt[:, 2, :], exp2_dt[:, :])
                for part, dst in ((0, x), (1, angle)):
                    tt(per_q(dst[:, chans]), per_q(lam[:, part, chans]),
                       dt[:, 3, 0:SP_T].unsqueeze(2).to_broadcast([P, SP_T, SN]), ALU.mult).then_inc(*step())
                    tt(dst[:, by_state], lam[:, part, by_state], dt[:, 3, SP_T:SP_T + ST], ALU.mult).then_inc(*step())
                pool.wait_ge(*settled())

            def quarter_turns():
                ts(k, angle, 1.0 / QUARTER, ROUND, ALU.mult, ALU.add).then_inc(*step())
                pool.wait_ge(*settled())
                ts(k, k, ROUND, None, ALU.subtract).then_inc(*step())
                for part in (QUARTER_HI, QUARTER_MID, QUARTER_LO):
                    pool.wait_ge(*settled())
                    two_ops(out=angle, in0=k, scalar=-part, in1=angle, op0=ALU.mult, op1=ALU.add)
                ts(p, k, 0.25, ROUND, ALU.mult, ALU.add).then_inc(*step())
                pool.wait_ge(*settled())
                tt(y, angle, angle, ALU.mult).then_inc(*step())
                ts(p, p, ROUND, None, ALU.subtract).then_inc(*step())
                pool.wait_ge(*settled())
                two_ops(out=k, in0=p, scalar=-4.0, in1=k, op0=ALU.mult, op1=ALU.add)
                pool.wait_ge(*settled())

            def series():
                ts(p, y, SIN_C[0], None, ALU.mult).then_inc(*step())
                ts(x, y, COS_C[0], None, ALU.mult).then_inc(*step())
                for cs, cc in zip(SIN_C[1:], COS_C[1:]):
                    pool.wait_ge(*settled())
                    two_ops(out=p, in0=p, scalar=cs, in1=y, op0=ALU.add, op1=ALU.mult)
                    two_ops(out=x, in0=x, scalar=cc, in1=y, op0=ALU.add, op1=ALU.mult)
                pool.wait_ge(*settled())
                two_ops(out=x, in0=x, scalar=COS_C[-1], in1=y, op0=ALU.add, op1=ALU.mult)
                two_ops(out=angle, in0=p, scalar=1.0, in1=angle, op0=ALU.add, op1=ALU.mult)

            def turn():
                pool.wait_ge(*settled())
                tt(y, k, k, ALU.mult).then_inc(*step())
                pool.wait_ge(*settled())
                ts(p, y, -1.0 / 6, 7.0 / 6, ALU.mult, ALU.add).then_inc(*step())
                ts(eig_tmp[:, :], y, -1.0, 4.0, ALU.mult, ALU.add).then_inc(*step())
                pool.wait_ge(*settled())
                tt(y, y, p, ALU.mult).then_inc(*step())
                tt(k, k, eig_tmp[:, :], ALU.mult).then_inc(*step())
                pool.wait_ge(*settled())
                ts(y, y, -1.0, 1.0, ALU.mult, ALU.add).then_inc(*step())
                ts(k, k, 1.0 / 3, None, ALU.mult).then_inc(*step())
                pool.wait_ge(*settled())
                tt(cosm1, x, y, ALU.mult).then_inc(*step())
                tt(sine, angle, y, ALU.mult).then_inc(*step())
                pool.wait_ge(*settled())
                two_ops(out=x, in0=x, scalar=1.0, in1=k, op0=ALU.add, op1=ALU.mult)
                tt(angle, angle, k, ALU.mult).then_inc(*step())
                two_ops(out=cosm1, in0=y, scalar=-1.0, in1=cosm1, op0=ALU.add, op1=ALU.add)
                pool.wait_ge(*settled())
                tt(y, sine, x, ALU.add).then_inc(*step())
                tt(cosm1, cosm1, angle, ALU.subtract).then_inc(*step())
                pool.wait_ge(*settled())
                tt(sine, y, mag, ALU.mult).then_inc(*step())
                two_ops(out=x, in0=cosm1, scalar=1.0, in1=mag, op0=ALU.add, op1=ALU.mult)
                pool.wait_ge(*settled())
                pool.tensor_copy(abar[:, 0, :, :], per_q(x[:, chans])).then_inc(*step())
                pool.tensor_copy(abar[:, 1, :, :], per_q(sine[:, chans])).then_inc(*step())

            def coefficients():
                re, im, mg, cm1, ni, ar = (v[:, by_state] for v in (lam[:, 0, :], lam[:, 1, :], mag, cosm1, sine, x))
                s_ar, s_ai, cr, ci, s_mag, den, t, nr, t2, u = (st[:, i, :] for i in range(10))
                pool.tensor_copy(s_ar, ar).then_inc(*step())
                pool.tensor_copy(s_ai, ni).then_inc(*step())
                tt(s_mag, mg, mg, ALU.mult).then_inc(*step())
                tt(den, re, re, ALU.mult).then_inc(*step())
                tt(t, im, im, ALU.mult).then_inc(*step())
                tt(nr, mg, cm1, ALU.mult).then_inc(*step())
                pool.wait_ge(*settled())
                tt(den, den, t, ALU.add).then_inc(*step())
                two_ops(out=nr, in0=mg, scalar=-1.0, in1=nr, op0=ALU.add, op1=ALU.add)
                pool.wait_ge(*settled())
                tt(cr, nr, re, ALU.mult).then_inc(*step())
                tt(t, ni, im, ALU.mult).then_inc(*step())
                tt(ci, ni, re, ALU.mult).then_inc(*step())
                tt(t2, nr, im, ALU.mult).then_inc(*step())
                pool.wait_ge(*settled())
                tt(cr, cr, t, ALU.add).then_inc(*step())
                tt(ci, ci, t2, ALU.subtract).then_inc(*step())
                pool.wait_ge(*settled())

            def phase_powers(levels):
                t, nr, t2, u = (st[:, i, :] for i in range(6, 10))
                pc, ps = k[:, by_state], p[:, by_state]
                if levels[0] > 0:
                    pc, ps = (powers[:, levels[0] - 1, c, :] for c in range(2))
                else:
                    ts(pc, cosm1[:, by_state], 1.0, None, ALU.add).then_inc(*step())
                    pool.tensor_copy(ps, y[:, by_state]).then_inc(*step())
                    pool.wait_ge(*settled())
                for l in levels:
                    nc_, ns = powers[:, l, 0, :], powers[:, l, 1, :]
                    tt(t, ps, ps, ALU.mult).then_inc(*step())
                    tt(u, pc, pc, ALU.mult).then_inc(*step())
                    two_ops(out=ns, in0=pc, scalar=2.0, in1=ps, op0=ALU.mult, op1=ALU.mult)
                    pool.wait_ge(*settled())
                    tt(nc_, u, t, ALU.subtract).then_inc(*step())
                    tt(nr, ns, ns, ALU.mult).then_inc(*step())
                    pool.wait_ge(*settled())
                    tt(t2, nc_, nc_, ALU.mult).then_inc(*step())
                    pool.wait_ge(*settled())
                    tt(t2, t2, nr, ALU.add).then_inc(*step())
                    pool.wait_ge(*settled())
                    ts(t2, t2, -0.5, 1.5, ALU.mult, ALU.add).then_inc(*step())
                    pool.wait_ge(*settled())
                    tt(nc_, nc_, t2, ALU.mult).then_inc(*step())
                    pool.wait_ge(*settled())
                    tt(ns, ns, t2, ALU.mult).then_inc(powers_ready, 1)
                    pool.wait_ge(powers_ready, l + 1)
                    pc, ps = nc_, ns

            def low_parts(first, end):
                for u in range(first, end):
                    low_part(u // RING, u % RING)

            low_parts(0, 4)
            growth_and_angle()
            low_parts(4, 6)
            exp_rest(x, k, exp2[:, :])
            low_parts(6, 9)
            exp_series(mag, x, p, exp2[:, :])
            low_parts(9, 13)
            quarter_turns()
            low_parts(13, 17)
            series()
            low_parts(17, 22)
            turn()
            low_parts(22, 26)
            coefficients()
            low_parts(26, 28)
            phase_powers(range(LEVELS // 2))
            low_parts(28, 30)
            phase_powers(range(LEVELS // 2, LEVELS))
            low_parts(30, 32)

            def add_tile(total, tiles, k, summed, before, ready):
                pool.wait_ge(*ready)
                if k > 1:
                    pool.wait_ge(summed, before + (k - 1))
                pool.tensor_tensor(total[:, :], tiles(0) if k == 1 else total[:, :], tiles(k), ALU.add).then_inc(summed, 1)

            z_tile = lambda k: z[:, k, :]
            for L in range(DEPTH):
                base = L * LAYER_U // RING
                with pool.Fori(base + (0 if L else 8), base + OUT0 // RING + 1) as n:
                    for s in range(RING):
                        low_part(n, s)
                if L:
                    pool.wait_ge(mean_done, 2 * L)
                for k in range(KT):
                    low_part(base + OUT0 // RING + 1 + k // RING, k % RING)
                    if 1 <= k < KT - 1:
                        add_tile(z_sum, z_tile, k, z_summed, 2 * L * (KT - 2), (z_ready, L * KT + (k + 1)))
                down_round = DOWN0 // RING + 1
                with pool.Fori(base + OUT0 // RING + 3, base + down_round) as n:
                    for s in range(RING):
                        low_part(n, s)
                pool.wait_ge(mean_done, 2 * L + 1)
                k = 1
                for u in range(down_round * RING, LAYER_U):
                    low_part(base + u // RING, u % RING)
                    if k < KT - 1 and (u == LAYER_U - 1 or DOWN0 + ((k + 1) * FT - 1) // UT + RING <= u):
                        add_tile(z_sum, z_tile, k, z_summed, (2 * L + 1) * (KT - 2), after_result(L, DOWN_R0 + k))
                        k += 1
                for k in range(k, KT - 1):
                    add_tile(z_sum, z_tile, k, z_summed, (2 * L + 1) * (KT - 2), after_result(L, DOWN_R0 + k))
            mixer_round = DEPTH * LAYER_U // RING
            for s in range(3):
                low_part(mixer_round, s)
            pool.wait_ge(mean_done, MIX * 2)
            pool.wait_ge(powers_ready, LEVELS)
            for l in range(LEVELS):
                n = 1 << l
                wc, ws = (powers[:, l, c, :].unsqueeze(2).to_broadcast([P, ST, n]) for c in range(2))
                c0, s0, c1 = phase[:, 0, :, 0:n], phase[:, 1, :, 0:n], phase[:, 0, :, n:2 * n]
                pool.wait_ge(phase_c, l + 1)
                pool.wait_ge(phase_s, l + 1)
                tt(c1, c0, wc, ALU.mult).then_inc(phase_step, 1)
                tt(phase_tp[:, :, 0:n], s0, ws, ALU.mult).then_inc(phase_step, 1)
                pool.wait_ge(phase_step, 2 * l + 2)
                tt(c1, c1, phase_tp[:, :, 0:n], ALU.subtract).then_inc(phase_c, 1)
            pool.wait_ge(mix_in, 16 * MIX_LOADS)
            pool.wait_ge(phase_c, LEVELS + 1)
            br, bi, nr, ni = (w_b[:, j, c, :, :] for j in (1, 0) for c in (0, 1))
            ar, ai = abar[:, 0, :, :], abar[:, 1, :, :]
            t0, t1 = (w_b2[:, 0, c, :, 0, :] for c in range(2))
            tt(nr, br, ar, ALU.mult).then_inc(wb_step, 1)
            tt(t0, bi, ai, ALU.mult).then_inc(wb_step, 1)
            tt(ni, br, ai, ALU.mult).then_inc(wb_step, 1)
            tt(t1, bi, ar, ALU.mult).then_inc(wb_step, 1)
            pool.wait_ge(wb_step, 4)
            tt(nr, nr, t0, ALU.subtract).then_inc(wb_ready, 1)
            tt(ni, ni, t1, ALU.add).then_inc(wb_ready, 1)
            low_part(mixer_round, 3)
            for s in range(RING):
                low_part(mixer_round + 1, s)

            def state_im_part(q):
                c, s = phase[:, 0, 4 * q:4 * q + 4, :], phase[:, 1, 4 * q:4 * q + 4, :]
                zr, zi = states[q][:, 0, :, :], states[q][:, 1, :, :]
                pool.wait_ge(scanned, 8 * q + 8)
                if q:
                    pool.wait_ge(state_im, q)
                else:
                    pool.wait_ge(wb_apart, 2 * BT)
                tt(t_p[:, :, :], zr, s, ALU.mult).then_inc(re_taken, 1)
                pool.wait_ge(im_taken, q + 1)
                tt(zi, zi, c, ALU.mult).then_inc(re_taken, 1)
                pool.wait_ge(re_taken, 2 * q + 2)
                tt(zi, zi, t_p[:, :, :], ALU.add).then_inc(state_im, 1)

            pool_steps = [0]

            def pooling(g):
                w, r = WINDOWS[g], MIN_R0 + SP_T + g
                pool.wait_ge(bank_free[r % 2], free_before(MIX, r) + 1)
                if g:
                    pool.wait_ge(pooled, 2 * g)
                u = u_all[:, g, :]

                def pool_next():
                    pool_steps[0] += 1
                    return pool_step, 1

                src, n, i = u, 1, 0
                while n < w:
                    dst = run[i][:, :]
                    tt(dst[:, n:T], src[:, n:T], src[:, 0:T - n], ALU.add).then_inc(*pool_next())
                    pool.tensor_copy(dst[:, 0:n], src[:, 0:n]).then_inc(*pool_next())
                    pool.wait_ge(pool_step, pool_steps[0])
                    src, n, i = dst, 2 * n, 1 - i
                mean = run[i]
                tt(mean[:, 0:16], src[:, 0:16], mpar[:, INV_C + 16 * g:INV_C + 16 * g + 16], ALU.mult).then_inc(*pool_next())
                pool.tensor_scalar(mean[:, 16:T], src[:, 16:T], 1.0 / w, None, ALU.mult).then_inc(*pool_next())
                pool.wait_ge(pool_step, pool_steps[0])
                tt(u[:, 0:16], mean[:, 0:16], u[:, 0:16], ALU.subtract).then_inc(pooled, 1)
                tt(u[:, 16:T], mean[:, 16:T], u[:, 16:T], ALU.subtract).then_inc(pooled, 1)

            state_im_part(0)
            low_part(mixer_round + 2, 0)
            low_part(mixer_round + 2, 1)
            low_part(mixer_round + 2, 2)
            pooling(0)
            pooling(1)
            state_im_part(1)
            pooling(2)
            pooling(3)
            state_im_part(2)
            state_im_part(3)
            low_part(mixer_round + 2, 3)
            sq_tile = lambda k: sq_2[k % 4][:, :]
            for k in range(KT + RING):
                low_part(mixer_round + 3 + k // RING, k % RING)
                if 2 <= k < KT:
                    add_tile(rstd_2, sq_tile, k - 1, sq_summed, 0, (squared, (MIX * 2 + 1) * KT + k))
            with pool.Fori(mixer_round + 6, mixer_round + (MDOWN_U0 + 10) // RING) as n:
                for s in range(RING):
                    low_part(n, s)
            sq_tile = lambda k: sq_3[k % 4][:, :]
            k = 1
            for u in range(MDOWN_U0 + 10, MIX_U):
                if k < KT - 1 and MDOWN_U0 + ((k + 1) * FT - 1) // UT + RING < u:
                    add_tile(rstd_3, sq_tile, k, sq_summed, KT - 2, (squared, (MIX * 2 + 2) * KT + (k + 1)))
                    k += 1
                low_part(mixer_round + u // RING, u % RING)
            for k in range(k, KT - 1):
                add_tile(rstd_3, sq_tile, k, sq_summed, KT - 2, (squared, (MIX * 2 + 2) * KT + (k + 1)))

        @block.tensor
        def _(pe):
            def passes(dst, lhs, rhs, start, stop, swapped=False):
                for n, (i, j) in enumerate(((0, 0), (0, 1), (1, 0))):
                    mm = pe.matmul(dst, lhs[i], rhs[j], start=start and n == 0, stop=stop and n == 2)
                return mm

            def take_unit(L, u, i=0):
                pe.wait_ge(lo_done, L * LAYER_U + i + u + 1)

            def take_bank(L, r, i=0):
                pe.wait_ge(bank_free[r % 2], free_before(L, r, i))
                return U_BANK[r % 2]

            def wt(u, k):
                s = u % RING
                return w_hi[s][:, k, :], w_lo[s][:, k, :]

            def feature_unit(L, u, r, rhs, ui=0, ri=0):
                take_unit(L, u, ui)
                dst = take_bank(L, r, ri)
                for k in range(KT):
                    mm = passes(dst[:, :], wt(u, k), rhs(k), k == 0, k == KT - 1)
                mm.then_inc(unit_used, 1)

            def x_parts(k):
                return xh[:, k, :], xl[:, k, :]

            def first_units(L, u, r, x_done, ui=0, ri=0):
                lag = 2
                for k in range(KT + lag):
                    for i in range(2):
                        c = k - lag * i
                        if not 0 <= c < KT:
                            continue
                        if c == 0:
                            take_unit(L, u + i, ui)
                            take_bank(L, r + i, ri)
                        if i == 0:
                            pe.wait_ge(x_lo, x_done + (c + 1))
                        mm = passes(U_BANK[(r + i) % 2][:, :], wt(u + i, c), x_parts(c), c == 0, c == KT - 1)
                        if c == KT - 1:
                            mm.then_inc(unit_used, 1)

            def token_units(L, u, r, half, ui=0, ri=0):
                take_unit(L, u + half, ui)
                for b in range(4):
                    if half == 0 and b % 2 == 0:
                        take_bank(L, r + b // 2, ri)
                    dst = U_BANK[(r + b // 2) % 2][:, b % 2 * RET_DV:(b % 2 + 1) * RET_DV]
                    for k in range(4):
                        s = (u + half) % RING
                        w_pair = [x[s][:, 2 * k:2 * k + 2, :].rearrange("p f n -> p (f n)") for x in (w_hi, w_lo)]
                        c = 4 * half + k
                        mm = passes(dst, (xh[:, c, b * P:(b + 1) * P], xl[:, c, b * P:(b + 1) * P]), w_pair,
                                    c == 0 and b % 2 == 0, c == KT - 1 and b % 2 == 1)
                mm.then_inc(unit_used, 1)

            def attention(L, t):
                it = L * 4 + t
                ui, ri = t * 12, t * 6

                def take_score(n):
                    pe.wait_ge(s_free[n % 2], it * 6 + (n // 2 + 1))
                    return S_BANK[n % 2]

                def scores(hh, js):
                    for r in range(2):
                        pe.wait_ge(*after_result(L, r, ri))
                    r0 = hh * NA_DH
                    q, k = ([v[r0:r0 + NA_DH, :] for v in parts] for parts in ((na_q, na_lo[0]), (na_k, na_lo[1])))
                    for j in js:
                        dst = take_score(4 * hh + j)
                        bs = kblocks(j)
                        keys = slice((j - 1 + bs[0]) * P, (j + bs[-1]) * P)
                        passes(dst[:, bs[0] * P:(bs[-1] + 1) * P], [v[:, j * P:(j + 1) * P] for v in q], [v[:, keys] for v in k],
                               True, True).then_inc(score_done, 1)

                def turn_v():
                    pe.wait_ge(*after_result(L, 2, ri))
                    pe.wait_ge(o_norm, it * 4 + 4)
                    for b in range(CB):
                        mm = pe.transpose(O_BANK[:, b * P:(b + 1) * P], r_tmp[:, b * P:(b + 1) * P], ident[:, :])
                    mm.then_inc(vt_done, 1)

                def turn_probs(i):
                    j = i % CB
                    if i < 2:
                        pe.wait_ge(ot_read, it * 2 + (i + 1))
                    else:
                        pe.wait_ge(pt_ready, it * 8 + (i - 1))
                    pe.wait_ge(p_ready, it * 8 + (i + 1))
                    for b in kblocks(j):
                        mm = pe.transpose(T_BANK[i % 2][:, b * P:(b + 1) * P], s_t[:, i, b * P:(b + 1) * P], ident[:, :])
                    mm.then_inc(pt_done, 1)

                def pv(i):
                    hh, j = i // CB, i % CB
                    if i == 0:
                        pe.wait_ge(o_norm, it * 4 + 4)
                        pe.wait_ge(v_ready, it + 1)
                    pe.wait_ge(pt_ready, it * 8 + (i + 1))
                    r0 = hh * NA_DH
                    dst = Y_BANK[r0:r0 + NA_DH, j * P:(j + 1) * P]
                    bs = kblocks(j)
                    for b in bs:
                        mm = pe.matmul(dst, na_v[:, j - 1 + b, r0:r0 + NA_DH], pt[:, i % 2, b * P:(b + 1) * P],
                                       start=b == bs[0], stop=b == bs[-1])
                    mm.then_inc(pv_done, 1)

                first_units(L, 0, 0, L * 2 * KT, ui, ri)
                feature_unit(L, 2, 2, x_parts, ui, ri)
                scores(0, (0, 1))
                turn_v()
                scores(0, (2, 3))
                feature_unit(L, 3, 3, x_parts, ui, ri)
                scores(1, (0, 1))
                turn_probs(0)
                turn_probs(1)
                scores(1, (2, 3))
                feature_unit(L, 4, 4, x_parts, ui, ri)
                pv(0)
                pv(1)
                turn_probs(2)
                turn_probs(3)
                token_units(L, 5, 5, 0, ui, ri)
                pv(2)
                pv(3)
                turn_probs(4)
                turn_probs(5)
                token_units(L, 5, 5, 1, ui, ri)
                pv(4)
                pv(5)
                turn_probs(6)
                turn_probs(7)
                pe.wait_ge(rope_lo, it * 2 + 2)
                for m in range(4):
                    dst = take_score(8 + m)
                    passes(dst[:, :], [v[1][:, m * P:(m + 1) * P] for v in (r_hi, r_lo)], [v[0][:, :] for v in (r_hi, r_lo)],
                           True, True).then_inc(score_done, 1)
                feature_unit(L, 7, 7, x_parts, ui, ri)
                pv(6)
                pv(7)
                feature_unit(L, 8, 8, x_parts, ui, ri)
                pe.wait_ge(pr_lo_s, it * 4 + 4)
                for r in (5, 6):
                    pe.wait_ge(*after_result(L, r, ri))
                for n in range(4):
                    dst = (O_BANK if n < 2 else Y_BANK)[:, (n % 2) * RET_DV:(n % 2 + 1) * RET_DV]
                    if n == 2:
                        pe.wait_ge(ya_ready, it + 1)
                    for m in range(4):
                        mm = passes(dst, [v[:, m, n * P:(n + 1) * P] for v in (pr_hi, pr_lo)], [v[:, m, :] for v in (r_v, r_v_lo)],
                                    m == 0, m == 3)
                    mm.then_inc(o_done, 1)
                feature_unit(L, 9, 9, x_parts, ui, ri)
                feature_unit(L, 10, 10, x_parts, ui, ri)
                for f in range(2):
                    pe.wait_ge(pt_ready, it * 8 + (7 + f))
                    pe.wait_ge(o_norm, it * 4 + 8)
                    for n in range(4):
                        mm = pe.transpose(T_BANK[f][:, n * P:(n + 1) * P], o_n[:, n, f * P:(f + 1) * P], ident[:, :])
                    mm.then_inc(ot_done, 1)
                feature_unit(L, 11, 11, x_parts, ui, ri)

            def branches(L, i):
                ui, ri = i * 8, i * 5
                it = L * 2 + i
                for g in range(2):
                    feature_unit(L, BR0 + g, BR_R0 + g, x_parts, ui, ri)
                pe.wait_ge(br_lo, L * 3 + 1)
                for m in range(4):
                    u = BR0 + 2 + m // 2
                    if m % 2 == 0:
                        take_unit(L, u, ui)
                    dst = take_bank(L, BR_R0 + 2 + m, ri)
                    for k in range(4):
                        mm = passes(dst[:, :], wt(u, 4 * (m % 2) + k), (ya_hi[:, k, :], ya_lo[:, k, :]), k == 0, k == 3)
                    mm.then_inc(unit_used if m % 2 else mid_done, 1)
                pe.wait_ge(br_lo, L * 3 + 3)
                for m in range(4):
                    feature_unit(L, BR0 + 4 + m, BR_R0 + 6 + m, lambda k: (yb_hi[:, k, :], yb_lo[:, k, :]), ui, ri)

            def mean(n, ready):
                pe.wait_ge(z_summed, n * (KT - 2) + (KT - 2))
                pe.matmul(S_BANK[0][:, :], mean_w[:, :], z_sum[:, :], start=True, stop=False)
                pe.wait_ge(*ready)
                pe.matmul(S_BANK[0][:, :], mean_w[:, :], z[:, KT - 1, :], start=False, stop=True).then_inc(mean_done, 1)

            def square_sum(tile, first, last):
                for i in range(4):
                    mm = pe.matmul(S_BANK[1][32 * i:32 * i + 32, 0:P], mean_w[:, 0:32], tile[:, i * P:(i + 1) * P], start=first, stop=last)
                return mm

            def mean_square(n, total, last):
                i = n - MIX * 2 - 1
                pe.wait_ge(sq_summed, i * (KT - 2) + (KT - 2))
                square_sum(total, True, False)
                pe.wait_ge(squared, n * KT + KT)
                square_sum(last, False, True).then_inc(square_mean, 1)

            def spread(n, rs):
                pe.wait_ge(lrstd, n + 1)
                for i in range(4):
                    mm = pe.matmul(S_BANK[0][:, i * P:(i + 1) * P], pick[:, i, :], rs[:, 0:P], start=True, stop=True)
                mm.then_inc(rstd_spread, 1)

            def square_term(n, k, squares):
                pe.wait_ge(squared, n * KT + (k + 1))
                square_sum(squares[k % 4], k == 0, k == KT - 1).then_inc(sq_used, 1)

            def variance(n, squares):
                for k in range(KT):
                    square_term(n, k, squares)

            def out_proj(L):
                def merged_parts(k):
                    pe.wait_ge(merged_lo, L * 8 + (k + 1))
                    return merged_p[:, k, :], merged_p[:, 8 + k, :]

                for m in range(KT):
                    feature_unit(L, OUT0 + m, OUT_R0 + m, merged_parts)
                mean(L * 2, (z_ready, L * KT + KT))
                variance(L * 2, sq)
                pe.wait_ge(p_lo_s, L + 1)
                take_unit(L, PLE0)
                for m in range(4):
                    if m == 2:
                        spread(L * 2, rstd)
                    for k in range(PLE_T):
                        mm = passes(PLE_BANK[m][:, :], wt(PLE0, PLE_T * m + k), (p_hi[:, k, :], p_lo[:, k, :]), k == 0, k == PLE_T - 1)
                    mm.then_inc(unit_used if m == 3 else mid_done, 1)

            def ple(L):
                first_units(L, PLE0 + 1, PLE_R0, (L * 2 + 1) * KT)
                for m in range(2, KT):
                    feature_unit(L, PLE0 + 1 + m, PLE_R0 + m, x_parts)
                take_unit(L, PLE0 + 9)
                for m in range(4):
                    dst = take_bank(L, PLE_R0 + KT + m)
                    for k in range(PLE_T):
                        mm = passes(dst[:, :], wt(PLE0 + 9, PLE_T * m + k), (p_hi[:, k, :], p_lo[:, k, :]), k == 0, k == PLE_T - 1)
                    mm.then_inc(unit_used if m == 3 else mid_done, 1)

            def down(L, u0, r0, split):
                for m in range(KT):
                    dst = take_bank(L, r0 + m)
                    for k in range(FT):
                        i = m * FT + k
                        if i % UT == 0:
                            take_unit(L, u0 + i // UT)
                        if m == 0:
                            pe.wait_ge(*split(k))
                        mm = passes(dst[:, :], wt(u0 + i // UT, i % UT), (g_hi[:, k, :], g_lo[:, k, :]), k == 0, k == FT - 1)
                        if i % UT == UT - 1:
                            mm.then_inc(unit_used, 1)
                        elif k == FT - 1:
                            mm.then_inc(mid_done, 1)

            def down_layer(L):
                down(L, DOWN0, DOWN_R0, lambda k: (g_lo_s, L * FT + (k + 1)))
                mean(L * 2 + 1, after_result(L, DOWN_R0 + KT - 1))
                variance(L * 2 + 1, sq)
                spread(L * 2 + 1, rstd)

            def mixer():
                n0 = MIX * 2
                variance(n0, sq_1)
                spread(n0, rstd_1)
                by_place = lambda x: x.rearrange("p (b j) -> p b j", j=BT)

                def block_inputs(q):
                    if q:
                        pe.wait_ge(v_read, q)
                    for j in range(BT):
                        for k in range(4):
                            r0 = k * 2 * SCH
                            for c in range(2):
                                mm = pe.matmul(V_BANKS[:, k, c * NB:(c + 1) * NB],
                                               w_b2[r0:r0 + 2 * SCH, j, c, q, :, :].rearrange("p h n -> p (h n)"),
                                               by_place(u_all[r0:r0 + 2 * SCH, 4 + q, :])[:, :, j],
                                               start=j == 0 and c == 0, stop=j == BT - 1 and c == 1)
                    mm.then_inc(v_done, 1)

                Y = (Y_BANK, O_BANK, V_BANKS[:, 0, :], V_BANKS[:, 1, :])

                def convolve(q):
                    for k in range(BT):
                        pe.matmul(by_place(Y[q])[:, :, k:BT], k_conv[:, q, k, :], by_place(u_all[:, 4 + q, :])[:, :, 0:BT - k],
                                  start=k == 0, stop=False)

                def from_state(q):
                    pe.wait_ge(state_re, q + 1)
                    pe.wait_ge(state_im, q + 1)
                    for m in range(4):
                        r0 = m * 2 * SCH
                        for j in range(BT):
                            for c in range(2):
                                mm = pe.matmul(by_place(Y[q][r0:r0 + 2 * SCH, :])[:, 1:NB, j], c_pow[:, 4 * q + m, c, j + 1, :],
                                               states[q][:, c, m, 0:NB - 1], start=False, stop=j == BT - 1 and c == 1)
                    mm.then_inc(y_done, 1)

                first_units(MIX, MIN_U0, MIN_R0, (n0 + 1) * KT)
                for m in range(2, SP_T):
                    feature_unit(MIX, MIN_U0 + m, MIN_R0 + m, x_parts)
                for r in (SP_T - 2, SP_T - 1):
                    pe.wait_ge(*after_result(MIX, MIN_R0 + r))
                pe.wait_ge(wb_apart, 2 * BT)
                block_inputs(0)
                for m in range(SP_T, KT):
                    feature_unit(MIX, MIN_U0 + m, MIN_R0 + m, x_parts)
                block_inputs(1)
                pe.wait_ge(c_ready, 2 * BT)
                for m in range(ST):
                    q, r0 = m // 4, m % 4 * 2 * SCH
                    for c in range(2):
                        mm = pe.matmul(O_BANK[r0:r0 + 2 * SCH, q * 2 * SCH * BT:(q + 1) * 2 * SCH * BT], b_st[:, c, m, :],
                                       c_pow[:, m, c, 0:BT, :].rearrange("p k n -> p (k n)"), start=c == 0, stop=c == 1)
                mm.then_inc(kernel_done, 1)
                pe.wait_ge(kernel_ready, 4)
                convolve(0)
                block_inputs(2)
                convolve(1)
                pe.wait_ge(c_ready, 2 * BT + 2)
                from_state(0)
                block_inputs(3)
                from_state(1)
                for g in range(SP_T):
                    if g >= 2:
                        pe.wait_ge(y_pool, g - 1)
                    pe.wait_ge(pooled, 2 * g + 2)
                    pe.matmul(U_BANK[g % 2][:, :], w_pool[:, g, :], u_all[:, g, :], start=True, stop=True).then_inc(pool_done, 1)
                pe.wait_ge(v_read, SP_T)
                convolve(2)
                convolve(3)
                from_state(2)
                from_state(3)
                pe.wait_ge(y_pool, SP_T)
                for m in range(SP_T):
                    u = GLU_U0 + m // 2
                    if m % 2 == 0:
                        take_unit(MIX, u)
                    dst = take_bank(MIX, GLU_R0 + m)
                    for k in range(SP_T):
                        pe.wait_ge(yg_lo_s, k + 1)
                        mm = passes(dst[:, :], wt(u, 4 * (m % 2) + k), (yg_hi[:, k, :], yg_lo[:, k, :]), k == 0, k == SP_T - 1)
                    mm.then_inc(unit_used if m % 2 else mid_done, 1)

                def mixed(k):
                    pe.wait_ge(mix_lo_s, k + 1)
                    return mix_hi[:, k, :], mix_lo[:, k, :]

                for half in range(2):
                    for m in range(2):
                        if half == 0:
                            take_unit(MIX, MOUT_U0 + m)
                            take_bank(MIX, MOUT_R0 + m)
                        for k in range(SP_T * half, SP_T * (half + 1)):
                            mm = passes(U_BANK[m][:, :], wt(MOUT_U0 + m, k), mixed(k), k == 0, k == KT - 1)
                        if half:
                            mm.then_inc(unit_used, 1)
                for m in range(2, KT):
                    feature_unit(MIX, MOUT_U0 + m, MOUT_R0 + m, mixed)
                mean_square(n0 + 1, rstd_2, sq_2[(KT - 1) % 4])
                spread(n0 + 1, rstd_2)
                with pe.Fori(0, FT // 2) as j:
                    first_units(MIX, GU_U0, GU_R0, (n0 + 2) * KT, j * 4, j * 2)
                    for m in range(2, 4):
                        feature_unit(MIX, GU_U0 + m, GU_R0 + m, x_parts, j * 4, j * 2)
                down(MIX, MDOWN_U0, MDOWN_R0, lambda k: (gu_lo, k + 1))
                mean_square(n0 + 2, rstd_3, sq_3[(KT - 1) % 4])
                spread(n0 + 2, rstd_3)

            pe.sem_inc(unit_used, 1)
            pe.wait_ge(params_in, 16 * 5)
            pe.wait_ge(consts_set, 3)
            with pe.Fori(0, DEPTH) as L:
                with pe.Fori(0, 4) as t:
                    attention(L, t)
                with pe.Fori(0, 2) as i:
                    branches(L, i)
                out_proj(L)
                ple(L)
                with pe.Fori(0, FT // 2) as j:
                    for m in range(4):
                        feature_unit(L, UP0 + m, UP_R0 + m, x_parts, j * 4, j * 2)
                down_layer(L)
            mixer()

        @block.scalar
        def _(act):
            def round_ahead(L, u, i=0):
                n = u + 3
                s = n % RING
                act.wait_ge(landed[s], (L * (LAYER_U // RING) + n // RING + 1) * 16 + i * (16 // RING))
                act.wait_ge(unit_used, L * LAYER_U + i + (u + 1))
                act.activation(w_hi[s][:, :, :], stage[s][:, :, :], ACT.Copy).then_inc(hi_done, 1)

            def unit_result(L, u, i=0):
                act.wait_ge(unit_used, L * LAYER_U + i + (u + 2))

            def attention(L, t):
                it = L * 4 + t
                ui = t * 12

                def copy_out(u, dst):
                    unit_result(L, u, ui)
                    act.activation(dst, U_BANK[u % 2][:, :], ACT.Copy).then_inc(rope_in, 1)

                def copy_blocks(u, dst, scale, done):
                    unit_result(L, u, ui)
                    act.activation(dst.rearrange("p (b r c) -> p b r c", b=CB, r=ROWS), block_view(U_BANK[u % 2][:, :]),
                                   ACT.Copy, scale=scale).then_inc(done, 1)

                def ret_score_hi(m):
                    act.wait_ge(s_free[m % 2], it * 6 + (4 + m // 2 + 2))
                    act.activation(pr_hi[:, m, :], pr[m % 2][:, :], ACT.Copy).then_inc(pr_hi_s, 1)

                def exps(hh):
                    act.wait_ge(nmax_ready, it * 2 + (hh + 1))
                    for j in range(CB):
                        i = 4 * hh + j
                        bs = kblocks(j)
                        s = s_t[:, i, bs[0] * P:(bs[-1] + 1) * P]
                        act.activation(s, s, ACT.Exp, bias=row_nmax[:, i:i + 1], accum_out=row_sum[:, i:i + 1])\
                            .then_inc(exp_done, 1)

                def probs_t(i):
                    bs = kblocks(i % CB)
                    act.wait_ge(pt_done, it * 8 + (i + 1))
                    if i >= 2:
                        act.wait_ge(pv_done, it * 8 + (i - 1))
                    act.activation(pt[:, i % 2, bs[0] * P:(bs[-1] + 1) * P],
                                   T_BANK[i % 2][:, bs[0] * P:(bs[-1] + 1) * P], ACT.Copy).then_inc(pt_ready, 1)

                act.wait_ge(unit_used, L * LAYER_U + t * 12 + 1)
                act.dma_start(bias[:, :, :].rearrange("p h n -> p (h n)"),
                              a["bias"][bass.ds(it, 1)].rearrange("s p n -> p (s n)")).then_inc(bias_in, 16)
                round_ahead(L, 0, ui)
                copy_blocks(0, na_q[:, :], NA_DH ** -0.5, na_hi)
                round_ahead(L, 1, ui)
                copy_blocks(1, na_k[:, :], 1.0, na_hi)
                round_ahead(L, 2, ui)
                copy_blocks(2, r_tmp[:, :], 1.0, bank_free[0])
                act.wait_ge(dterm, it * 3 + 3)
                act.activation(d_tab[:, :], d_tab[:, :], ACT.Exp).then_inc(dtab_ready, 1)
                act.wait_ge(vt_done, it + 1)
                act.activation(na_v[:, :, :].rearrange("p b n -> p (b n)"), O_BANK[:, :], ACT.Copy).then_inc(v_ready, 1)
                exps(0)
                round_ahead(L, 3, ui)
                copy_out(3, r_q[:, :])
                probs_t(0)
                probs_t(1)
                exps(1)
                round_ahead(L, 4, ui)
                copy_out(4, r_k[:, :])
                probs_t(2)
                probs_t(3)
                round_ahead(L, 5, ui)
                for k, x in enumerate((r_q, r_k)):
                    act.wait_ge(rope_ready, it * 2 + (k + 1))
                    act.activation(r_hi[k][:, :], x[:, :], ACT.Copy).then_inc(rope_hi, 1)
                probs_t(4)
                probs_t(5)
                round_ahead(L, 6, ui)
                unit_result(L, 6, ui)
                for r in (5, 6):
                    act.activation(r_v[:, 2 * (r - 5):2 * (r - 4), :].rearrange("p n c -> p (n c)"), U_BANK[r % 2][:, :], ACT.Copy)\
                        .then_inc(rv_hi, 1)
                probs_t(6)
                probs_t(7)
                for m in range(4):
                    ret_score_hi(m)
                for f in range(2):
                    round_ahead(L, 7 + f, ui)
                    unit_result(L, 7 + f, ui)
                    act.activation(sg[:, f, :], U_BANK[(7 + f) % 2][:, :], ACT.Sigmoid).then_inc(sig_ready, 1)
                    if f == 0:
                        act.wait_ge(pv_done, it * 8 + 8)
                        act.activation(ya[:, bass.ds(t, 1), :].rearrange("p s (r b c) -> p (s r) b c", r=ROWS, b=CB),
                                       Y_BANK[:, :].rearrange("p (b r c) -> p r b c", b=CB, r=ROWS), ACT.Copy)\
                            .then_inc(ya_ready, 1)
                round_ahead(L, 9, ui)
                act.wait_ge(gn_aggr, it * 4 + 4)
                act.activation(gn_std, gn_mv[:, :, 1], ACT.Sqrt, bias=gn_eps[:, :]).then_inc(std_ready, 1)
                for g in range(3):
                    if g:
                        round_ahead(L, 9 + g, ui)
                    unit_result(L, 9 + g, ui)
                    act.activation(gates[:, bass.ds(t * 3 + g, 1), :].rearrange("p s n -> p (s n)"),
                                   U_BANK[(9 + g) % 2][:, :], ACT.Sigmoid).then_inc(bank_free[(9 + g) % 2], 1)

            def branches(L, i):
                ui = i * 8
                it = L * 2 + i
                for g in range(2):
                    round_ahead(L, BR0 + g, ui)
                    unit_result(L, BR0 + g, ui)
                    act.activation(gates[:, bass.ds(i * 2 + (12 + g), 1), :].rearrange("p s n -> p (s n)"),
                                   U_BANK[g][:, :], ACT.Sigmoid).then_inc(bank_free[g], 1)
                for u in range(2, 4):
                    round_ahead(L, BR0 + u, ui)
                for m in range(4):
                    round_ahead(L, BR0 + 4 + m, ui)
                    act.wait_ge(merged, it * 4 + (m + 1))
                    act.activation(merged_p[:, bass.ds(i * 4 + m, 1), :].rearrange("p s n -> p (s n)"),
                                   m_tmp[m % 2][:, :], ACT.Copy).then_inc(merged_hi, 1)

            def split_branch_inputs(L):
                act.wait_ge(ya_ready, L * 4 + 4)
                act.wait_ge(ot_read, L * 8 + 10)
                act.activation(ya_hi[:, :, :], ya[:, :, :], ACT.Copy).then_inc(br_hi, 1)
                for h in range(2):
                    act.activation(yb_hi[:, 4 * h:4 * h + 4, :], yb[:, 4 * h:4 * h + 4, :], ACT.Copy).then_inc(br_hi, 1)

            def sqrt_table():
                act.activation(warm[:, :], ln_eps[:, :], ACT.Sqrt)

            def norm(L, which):
                n = L * 2 + which
                for k in range(KT):
                    act.wait_ge(centred, n * KT + (k + 1))
                    if k >= 4:
                        act.wait_ge(sq_used, n * KT + (k - 3))
                    act.activation(sq[k % 4][:, :], z[:, k, :], ACT.Square).then_inc(squared, 1)
                act.wait_ge(sq_used, n * KT + KT)
                act.activation(rstd[:, 0:P], S_BANK[1][:, 0:P], ACT.Sqrt, bias=ln_eps[:, :]).then_inc(lstd, 1)
                for k in range(KT):
                    b = lnp[:, bass.ds(L, 1), 2 * which + 1, k]
                    act.wait_ge(normed, n * KT + (k + 1))
                    act.activation(xh[:, k, :], p_sig[k % 4][:, :], ACT.Identity, bias=b).then_inc(x_hi, 1)
                    act.activation(z[:, k, :], p_sig[k % 4][:, :], ACT.Identity, bias=b).then_inc(x_ready, 1)
                act.wait_ge(x_ready, n * KT + KT)

            def ple(L):
                round_ahead(L, PLE0)
                for m in range(KT):
                    round_ahead(L, PLE0 + 1 + m)
                    unit_result(L, PLE0 + 1 + m)
                    if m >= 4:
                        act.wait_ge(zpre, L * 8 + (m - 3))
                    act.activation(p_sig[m % 4][:, :], U_BANK[m % 2][:, :], ACT.Sigmoid).then_inc(bank_free[m % 2], 1)
                round_ahead(L, PLE0 + 9)

            def up(L, j):
                it = L * FT + j * 2
                for c in range(2):
                    for half, buf in ((0, conv_a), (1, conv_b)):
                        u = UP0 + 2 * c + half
                        round_ahead(L, u, j * 4)
                        unit_result(L, u, j * 4)
                        ch = bass.ds(j * 2 + (half * FT + c), 1)
                        act.activation(buf[c][:, :], U_BANK[half][:, :], ACT.Identity,
                                       scale=convp[:, bass.ds(L, 1), 1, ch].rearrange("p l c -> p (l c)"),
                                       bias=convp[:, bass.ds(L, 1), 3, ch].rearrange("p l c -> p (l c)")).then_inc(conv_mid, 1)
                    act.wait_ge(bank_free[0], free_before(L, UP_R0 + 2 * c, j * 2) + 1)
                    act.activation(conv_a[c][:, :], conv_a[c][:, :], ACT.Gelu_apprx_tanh).then_inc(gelu_done, 1)
                    act.wait_ge(glu_done, it + (c + 1))
                    act.activation(g_hi[:, bass.ds(j * 2 + c, 1), :].rearrange("p s n -> p (s n)"), conv_b[c][:, :],
                                   ACT.Copy).then_inc(g_hi_s, 1)

            def rms_split(n, tiles):
                for k in range(KT):
                    act.wait_ge(normed, n * KT + (k + 1))
                    act.activation(xh[:, k, :], tiles[k % 4][:, :], ACT.Copy).then_inc(x_hi, 1)

            def root(n, dst, ready):
                act.wait_ge(*ready)
                act.wait_ge(rms_set, 1)
                act.activation(dst[:, 0:P], S_BANK[1][:, 0:P], ACT.Sqrt, bias=rms_eps[:, :]).then_inc(lstd, 1)

            def square(n, k, squares, ready):
                act.wait_ge(*ready)
                if k >= 4 and n == MIX * 2:
                    act.wait_ge(sq_used, n * KT + (k - 3))
                elif k >= 4:
                    act.wait_ge(sq_summed, (n - MIX * 2 - 1) * (KT - 2) + max(k - 4, 1))
                act.activation(squares[k % 4][:, :], z[:, k, :], ACT.Square).then_inc(squared, 1)

            def mixer():
                n0 = MIX * 2
                ahead = lambda u: round_ahead(MIX, u) if u + 3 < MIX_U else None
                after = lambda r: (bank_free[r % 2], free_before(MIX, r) + 1)
                act.wait_ge(x_lo, n0 * KT + KT)
                for dst, name in ((w_pool, "w_pool"), (b_st, "b_st"), (c_st, "c_st")):
                    act.dma_start(dst[:], a[name]).then_inc(mix_in, 16)
                act.dma_start(w_b[:, BT - 1, :, :, :], a["w_b"]).then_inc(mix_in, 16)
                for k in range(KT):
                    square(n0, k, sq_1, (x_ready, (n0 - 1) * KT + (k + 1)))
                root(n0, rstd_1, (sq_used, n0 * KT + KT))
                rms_split(n0, xn_1)
                for m in range(KT):
                    ahead(MIN_U0 + m)
                    unit_result(MIX, MIN_U0 + m)
                    act.activation(u_all[:, (m + SP_T) % KT, :], U_BANK[m % 2][:, :], ACT.Copy).then_inc(bank_free[m % 2], 1)
                    if m == 1:
                        act.wait_ge(wb_ready, 2)
                        for j in range(BT):
                            for h in range(2):
                                act.activation(w_b2[:, j, :, :, h, :].rearrange("p c q n -> p (c q) n"),
                                               w_b[:, j, :, :, :].rearrange("p c q n -> p (c q) n"), ACT.Copy,
                                               scale=mpar[:, HALF_C + h:HALF_C + h + 1]).then_inc(wb_apart, 1)
                act.wait_ge(kernel_done, 1)
                for h in range(4):
                    act.activation(k_conv[:, :, :, h * 2 * SCH:(h + 1) * 2 * SCH].rearrange("p q k n -> p (q k) n"),
                                   O_BANK[:, 0:SP_T * BT * 2 * SCH].rearrange("p (a n) -> p a n", n=2 * SCH), ACT.Copy,
                                   scale=mpar[:, QUART_C + h:QUART_C + h + 1]).then_inc(kernel_ready, 1)
                for g in range(SP_T):
                    act.wait_ge(pool_done, g + 1)
                    act.activation(u_all[:, g, :], U_BANK[g % 2][:, :], ACT.Copy,
                                   scale=mpar[:, POOLS_C + g:POOLS_C + g + 1]).then_inc(y_pool, 1)
                for q in range(SP_T):
                    act.wait_ge(y_skip, q + 1)
                    act.activation(yg[:, q, :], yg[:, q, :], ACT.Gelu_apprx_tanh).then_inc(y_gelu, 1)
                    act.wait_ge(y_gelu, q + 1)
                    act.activation(yg_hi[:, q, :], yg[:, q, :], ACT.Copy).then_inc(yg_hi_s, 1)
                for g in range(SP_T):
                    act.wait_ge(y_pool, g + 1)
                    act.activation(mix_hi[:, g, :], u_all[:, g, :], ACT.Copy).then_inc(mix_hi_s, 1)
                for m in range(SP_T):
                    if m % 2 == 0:
                        ahead(GLU_U0 + m // 2)
                        act.wait_ge(mid_done, MIX * LAYER_M + (GLU_M0 + m // 2 + 1))
                    else:
                        unit_result(MIX, GLU_U0 + m // 2)
                    if m >= 2:
                        act.wait_ge(y_ssm, m - 1)
                    act.activation(glu_sig[m % 2][:, :], U_BANK[m % 2][:, :], ACT.Sigmoid,
                                   bias=mpar[:, BGLU_C + m:BGLU_C + m + 1]).then_inc(bank_free[m % 2], 1)
                for m in range(SP_T):
                    act.wait_ge(y_ssm, m + 1)
                    act.activation(mix_hi[:, SP_T + m, :], u_all[:, SP_T + m, :], ACT.Copy).then_inc(mix_hi_s, 1)
                sqrt_table()
                for m in range(KT):
                    ahead(MOUT_U0 + m)
                    square(n0 + 1, m, sq_2, after(MOUT_R0 + m))
                root(n0 + 1, rstd_2, (square_mean, 1))
                rms_split(n0 + 1, xn_2)
                with act.Fori(0, FT // 2) as j:
                    for c in range(2):
                        u = GU_U0 + 2 * c
                        round_ahead(MIX, u, j * 4)
                        unit_result(MIX, u, j * 4)
                        act.activation(silu[c][:, :], U_BANK[0][:, :], ACT.Silu).then_inc(bank_free[0], 1)
                        round_ahead(MIX, u + 1, j * 4)
                        act.wait_ge(bank_free[1], free_before(MIX, GU_R0 + 2 * c + 1, j * 2) + 1)
                        act.activation(g_hi[:, bass.ds(j * 2 + c, 1), :].rearrange("p s n -> p (s n)"), hidden[c][:, :],
                                       ACT.Copy).then_inc(gu_hi, 1)
                sqrt_table()
                sq_m = 0
                for u in range(DOWN_U):
                    ahead(MDOWN_U0 + u)
                    while sq_m < KT and ((sq_m + 1) * FT - 1) // UT < u:
                        square(n0 + 2, sq_m, sq_3, after(MDOWN_R0 + sq_m))
                        sq_m += 1
                for m in range(sq_m, KT):
                    square(n0 + 2, m, sq_3, after(MDOWN_R0 + m))
                root(n0 + 2, rstd_3, (square_mean, 2))

            act.sem_inc(bank_free[0], 1)
            act.sem_inc(bank_free[1], 1)
            for dst, src in ((ident, "ident"), (pick, "pick"), (lnp, "lnp"), (convp, "convp"), (decay, "decay")):
                act.dma_start(dst[:], a[src]).then_inc(params_in, 16)
            act.dma_start(lam[:, :, :], a["lam"]).then_inc(lam_in, 16)
            act.dma_start(dt[:, 0, :], a["log_dt"]).then_inc(lam_in, 16)
            act.dma_start(mpar[:, :], a["mpar"]).then_inc(mpar_in, 16)
            def first_high(n):
                act.wait_ge(landed[n], 16)
                act.activation(w_hi[n][:, :, :], stage[n][:, :, :], ACT.Copy).then_inc(hi_done, 1)

            first_high(0)
            for k in range(KT):
                if k % 2 == 0:
                    act.wait_ge(x_in[k // 2], 16)
                act.activation(xh[:, k, :], z[:, k, :], ACT.Copy).then_inc(x_hi, 1)
                if k == 1:
                    first_high(1)
            first_high(2)
            act.wait_ge(params_in, 16 * 5)
            flat = decay[:, :, :].rearrange("p d n -> p (d n)")
            act.activation(decay_a[:, :], flat, ACT.Abs).then_inc(decay_step, 1)
            act.wait_ge(decay_step, 1)
            act.activation(decay_a[:, :], decay_a[:, :], ACT.Exp, scale=-1.0).then_inc(decay_step, 1)
            act.wait_ge(decay_step, 2)
            act.activation(decay_a[:, :], decay_a[:, :], ACT.Ln, bias=1.0).then_inc(decay_step, 1)
            with act.Fori(0, DEPTH) as L:
                act.wait_ge(x_lo, (L * 2 + 1) * KT)
                act.dma_start(rope[:, :, :], a["rope"]).then_inc(tables_in, 16)
                act.dma_start(delta[:, :], a["delta"]).then_inc(tables_in, 16)
                act.dma_start(masks[:, :, :], a["masks"]).then_inc(tables_in, 16)
                with act.Fori(0, 4) as t:
                    attention(L, t)
                split_branch_inputs(L)
                act.dma_start(p_raw[:, :, :], a["p"][bass.ds(L, 1)].rearrange("s p k n -> p (s k) n")).then_inc(p_in, 16)
                with act.Fori(0, 2) as i:
                    branches(L, i)
                sqrt_table()
                for k in range(KT):
                    round_ahead(L, OUT0 + k)
                    if k == 0:
                        act.wait_ge(p_in, L * 16 + 16)
                        act.activation(p_hi[:, :, :], p_raw[:, :, :], ACT.Copy).then_inc(p_hi_s, 1)
                norm(L, 0)
                ple(L)
                with act.Fori(0, FT // 2) as j:
                    up(L, j)
                sqrt_table()
                for k in range(DOWN_U):
                    round_ahead(L, DOWN0 + k)
                norm(L, 1)
            mixer()

        @block.vector
        def _(dve):
            def unit_result(L, u, i=0):
                dve.wait_ge(unit_used, L * LAYER_U + i + (u + 2))

            def attention(L, t):
                it = L * 4 + t
                ui, ri = t * 12, t * 6

                def after_score(n):
                    return s_free[n % 2], it * 6 + (n // 2 + 2)

                dve.tensor_copy(lg_now, decay[:, :, bass.ds(it, 1)].rearrange("p d s -> p (d s)")).then_inc(dterm_copy, 1)
                dve.wait_ge(dterm_copy, it + 1)
                dve.tensor_scalar(d_tmp[:, :], delta[:, :], 0.0, lg_now[:, 1:2], ALU.min, ALU.mult).then_inc(dterm, 1)
                dve.tensor_scalar(d_tab[:, :], delta[:, :], 0.0, lg_now[:, 0:1], ALU.max, ALU.mult).then_inc(dterm, 1)
                dve.wait_ge(dterm, it * 3 + 2)
                dve.tensor_tensor(d_tab[:, :], d_tab[:, :], d_tmp[:, :], ALU.subtract).then_inc(dterm, 1)

                def mask_scores(hh):
                    dve.wait_ge(bias_in, it * 16 + 16)
                    def add_bias(j):
                        i, bs = 4 * hh + j, kblocks(j)
                        cols = slice(bs[0] * P, (bs[-1] + 1) * P)
                        dve.wait_ge(score_done, it * 12 + (i + 1))
                        dve.tensor_tensor(s_t[:, i, cols], S_BANK[i % 2][:, cols], bias[:, hh, cols], ALU.add)\
                            .then_inc(s_free[i % 2], 1)

                    def mask_row_max(j):
                        i, bs = 4 * hh + j, kblocks(j)
                        cols = slice(bs[0] * P, (bs[-1] + 1) * P)
                        dve.wait_ge(*after_score(i))
                        stand(dve, dve_passed)
                        dve.tensor_tensor_reduce(s_t[:, i, cols], s_t[:, i, cols], masks[:, mask_of(j), cols], 1.0, -3.0e38,
                                                 ALU.add, ALU.max, row_max[:, i:i + 1]).then_inc(masked, 1)

                    add_bias(0)
                    for j in range(1, CB):
                        add_bias(j)
                        mask_row_max(j - 1)
                    mask_row_max(CB - 1)
                    dve.wait_ge(masked, it * 8 + (4 * hh + 4))
                    dve.tensor_scalar(row_nmax[:, 4 * hh:4 * hh + 4], row_max[:, 4 * hh:4 * hh + 4], -1.0, None, ALU.mult)\
                        .then_inc(nmax_ready, 1)

                def normalise(hh):
                    dve.wait_ge(exp_done, it * 8 + (4 * hh + 4))
                    dve.reciprocal(row_inv[:, 4 * hh:4 * hh + 4], row_sum[:, 4 * hh:4 * hh + 4]).then_inc(inv_ready, 1)
                    dve.wait_ge(inv_ready, it * 2 + (hh + 1))
                    for j in range(CB):
                        i = 4 * hh + j
                        bs = kblocks(j)
                        s = s_t[:, i, bs[0] * P:(bs[-1] + 1) * P]
                        dve.tensor_scalar(s, s, row_inv[:, i:i + 1], None, ALU.mult).then_inc(p_ready, 1)

                def rotate(k, x):
                    half = RET_DK // 2
                    r = 3 + k
                    dve.wait_ge(rope_in, it * 2 + (k + 1))
                    dve.tensor_tensor(r_tmp[0:half, :], U_BANK[r % 2][half:P, :], rope[0:half, 1, :], ALU.mult).then_inc(rope_sin, 1)
                    dve.tensor_tensor(r_tmp[half:P, :], U_BANK[r % 2][0:half, :], rope[half:P, 1, :], ALU.mult)\
                        .then_inc(bank_free[r % 2], 1)
                    dve.tensor_tensor(x[:, :], x[:, :], rope[:, 0, :], ALU.mult).then_inc(rope_cos, 1)
                    dve.wait_ge(bank_free[r % 2], free_before(L, r, ri) + 1)
                    dve.wait_ge(rope_sin, it * 2 + (k + 1))
                    dve.wait_ge(rope_cos, it * 2 + (k + 1))
                    dve.tensor_tensor(x[:, :], x[:, :], r_tmp[:, :], ALU.add).then_inc(rope_ready, 1)

                def na_low(i, hi, scale):
                    dve.wait_ge(na_hi, it * 2 + (i + 1))
                    for b in range(CB):
                        part = slice(b * P, (b + 1) * P)
                        op = dve.scalar_tensor_tensor(out=na_lo[i][:, part].rearrange("p (r c) -> p r c", r=ROWS),
                                                      in0=block_view(U_BANK[i][:, :])[:, b], scalar=scale,
                                                      in1=hi[:, part].rearrange("p (r c) -> p r c", r=ROWS).bitcast(F32),
                                                      op0=ALU.mult, op1=ALU.subtract)
                    op.then_inc(bank_free[i], 1)

                na_low(0, na_q, NA_DH ** -0.5)
                na_low(1, na_k, 1.0)
                mask_scores(0)
                normalise(0)
                mask_scores(1)
                rotate(0, r_q)
                normalise(1)
                rotate(1, r_k)
                for k, x in enumerate((r_q, r_k)):
                    dve.wait_ge(rope_hi, it * 2 + (k + 1))
                    dve.tensor_tensor(r_lo[k][:, :], x[:, :], r_hi[k][:, :].bitcast(F32), ALU.subtract).then_inc(rope_lo, 1)
                for r in (5, 6):
                    dve.wait_ge(rv_hi, it * 2 + (r - 4))
                    blocks = slice(2 * (r - 5), 2 * (r - 4))
                    dve.tensor_tensor(r_v_lo[:, blocks, :].rearrange("p n c -> p (n c)"), U_BANK[r % 2][:, :],
                                      r_v[:, blocks, :].rearrange("p n c -> p (n c)").bitcast(F32), ALU.subtract)\
                        .then_inc(bank_free[r % 2], 1)
                dve.wait_ge(dtab_ready, it + 1)

                def decay_scores(m):
                    dve.wait_ge(score_done, it * 12 + (9 + m))
                    dve.scalar_tensor_tensor(out=pr[m % 2][:, :], in0=S_BANK[m % 2][:, :], scalar=RET_DK ** -0.5,
                                             in1=d_tab[:, (3 - m) * P:(7 - m) * P], op0=ALU.mult, op1=ALU.mult)\
                        .then_inc(s_free[m % 2], 1)

                def decayed_low(m):
                    dve.wait_ge(pr_hi_s, it * 4 + (m + 1))
                    dve.tensor_tensor(pr_lo[:, m, :], pr[m % 2][:, :], pr_hi[:, m, :].bitcast(F32), ALU.subtract).then_inc(pr_lo_s, 1)

                decay_scores(0)
                decay_scores(1)
                decayed_low(0)
                dve.wait_ge(pr_lo_s, it * 4 + 1)
                stand(dve, dve_passed)
                decay_scores(2)
                decayed_low(1)
                dve.wait_ge(pr_lo_s, it * 4 + 2)
                stand(dve, dve_passed)
                decay_scores(3)
                decayed_low(2)
                decayed_low(3)
                for f in range(2):
                    dve.wait_ge(sig_ready, it * 2 + (f + 1))
                    dve.tensor_tensor(sg[:, f, :], U_BANK[(7 + f) % 2][:, :], sg[:, f, :], ALU.mult)\
                        .then_inc(bank_free[(7 + f) % 2], 1)

                def o_tile(n):
                    return (O_BANK if n < 2 else Y_BANK)[:, (n % 2) * RET_DV:(n % 2 + 1) * RET_DV]

                for n in range(4):
                    dve.wait_ge(o_done, it * 4 + (2 * (n // 2) + 2))
                    dve.bn_stats(gn_st[:, n, :], o_tile(n)).then_inc(gn_stat, 1)
                dve.wait_ge(gn_stat, it * 4 + 4)
                stand(dve, dve_passed)
                for n in range(4):
                    dve.bn_aggr(gn_mv[:, n, :], gn_st[:, n, :]).then_inc(gn_aggr, 1)
                dve.wait_ge(std_ready, it + 1)
                dve.reciprocal(gn_inv, gn_std).then_inc(ginv_ready, 1)
                dve.wait_ge(ginv_ready, it + 1)
                for n in range(4):
                    dve.tensor_scalar(o_n[:, n, :], o_tile(n), gn_mv[:, n, 0:1], gn_inv[:, n:n + 1], ALU.subtract, ALU.mult)\
                        .then_inc(o_norm, 1)
                for f in range(2):
                    dve.wait_ge(ot_done, it * 2 + (f + 1))
                    dve.tensor_tensor(yb[:, bass.ds(t * 2 + f, 1), :].rearrange("p s n -> p (s n)"), T_BANK[f][:, :],
                                      sg[:, f, :], ALU.mult).then_inc(ot_read, 1)

            def split_branch_inputs(L):
                dve.wait_ge(br_hi, L * 3 + 1)
                dve.tensor_tensor(ya_lo[:, :, :], ya[:, :, :], ya_hi[:, :, :].bitcast(F32), ALU.subtract).then_inc(br_lo, 1)
                for h in range(2):
                    dve.wait_ge(br_hi, L * 3 + (2 + h))
                    q = slice(4 * h, 4 * h + 4)
                    dve.tensor_tensor(yb_lo[:, q, :], yb[:, q, :], yb_hi[:, q, :].bitcast(F32), ALU.subtract).then_inc(br_lo, 1)

            def branches(L, i):
                ui, ri = i * 8, i * 5
                it = L * 2 + i
                g_a = lambda m: gates[:, bass.ds(i * 4 + m, 1), :].rearrange("p s n -> p (s n)")
                g_b = lambda m: gates[:, bass.ds(i * 4 + (8 + m), 1), :].rearrange("p s n -> p (s n)")
                for m in range(4):
                    r = BR_R0 + 2 + m
                    if m % 2:
                        unit_result(L, BR0 + 2 + m // 2, ui)
                    else:
                        dve.wait_ge(mid_done, L * LAYER_M + i * 2 + (BR_M0 + m // 2 + 1))
                    dve.tensor_tensor(g_a(m), U_BANK[r % 2][:, :], g_a(m), ALU.mult).then_inc(bank_free[r % 2], 1)
                for m in range(4):
                    r = BR_R0 + 6 + m
                    unit_result(L, BR0 + 4 + m, ui)
                    dve.tensor_tensor(g_b(m), U_BANK[r % 2][:, :], g_b(m), ALU.mult).then_inc(bank_free[r % 2], 1)
                    dve.wait_ge(bank_free[r % 2], free_before(L, r, ri) + 1)
                    dve.tensor_tensor(m_tmp[m % 2][:, :], g_a(m), g_b(m), ALU.add).then_inc(merged, 1)
                    dve.wait_ge(merged_hi, it * 4 + (m + 1))
                    dve.tensor_tensor(merged_p[:, bass.ds(i * 4 + (8 + m), 1), :].rearrange("p s n -> p (s n)"), m_tmp[m % 2][:, :],
                                      merged_p[:, bass.ds(i * 4 + m, 1), :].rearrange("p s n -> p (s n)").bitcast(F32),
                                      ALU.subtract).then_inc(merged_lo, 1)

            def residual_out(L):
                for k in range(KT):
                    if k == 1:
                        dve.wait_ge(p_hi_s, L + 1)
                        stand(dve, dve_passed)
                        dve.tensor_tensor(p_lo[:, :, :], p_raw[:, :, :], p_hi[:, :, :].bitcast(F32), ALU.subtract).then_inc(p_lo_s, 1)
                    unit_result(L, OUT0 + k)
                    dve.scalar_tensor_tensor(out=z[:, k, :], in0=xh[:, k, :].bitcast(F32), scalar=ALPHA,
                                             in1=U_BANK[k % 2][:, :], op0=ALU.mult, op1=ALU.add).then_inc(bank_free[k % 2], 1)
                    dve.wait_ge(bank_free[k % 2], free_before(L, OUT_R0 + k) + 1)
                    dve.scalar_tensor_tensor(out=z[:, k, :], in0=xl[:, k, :].bitcast(F32), scalar=ALPHA,
                                             in1=z[:, k, :], op0=ALU.mult, op1=ALU.add).then_inc(z_ready, 1)

            def norm(L, which):
                n = L * 2 + which
                dve.wait_ge(mean_done, n + 1)
                for k in range(KT):
                    dve.tensor_tensor(z[:, k, :], z[:, k, :], S_BANK[0][:, :], ALU.subtract).then_inc(centred, 1)
                dve.wait_ge(lstd, n + 1)
                dve.reciprocal(rstd[:, 0:P], rstd[:, 0:P]).then_inc(lrstd, 1)
                dve.wait_ge(rstd_spread, n + 1)

                def low(k):
                    dve.wait_ge(x_hi, n * KT + (KT + k + 1))
                    dve.scalar_tensor_tensor(out=xl[:, k, :], in0=p_sig[k % 4][:, :], scalar=lnp[:, bass.ds(L, 1), 2 * which + 1, k],
                                             in1=xh[:, k, :].bitcast(F32), op0=ALU.add, op1=ALU.subtract).then_inc(x_lo, 1)

                for k in range(KT):
                    if k >= 4:
                        dve.wait_ge(x_ready, n * KT + (k - 3))
                        dve.wait_ge(x_lo, n * KT + (KT + k - 3))
                    dve.scalar_tensor_tensor(out=p_sig[k % 4][:, :], in0=z[:, k, :], scalar=lnp[:, bass.ds(L, 1), 2 * which, k],
                                             in1=S_BANK[0][:, :], op0=ALU.mult, op1=ALU.mult).then_inc(normed, 1)
                    if k >= 1:
                        low(k - 1)
                low(KT - 1)

            def ple(L):
                dve.wait_ge(x_ready, L * 2 * KT + KT)
                for m in range(KT):
                    sig = p_sig[m % 4]
                    gate = PLE_R0 + m
                    dve.wait_ge(bank_free[gate % 2], free_before(L, gate) + 1)
                    if m < 4:
                        dve.tensor_tensor(sig[:, :], PLE_BANK[m][:, :], sig[:, :], ALU.mult).then_inc(ple_term, 1)
                        dve.wait_ge(ple_term, L * 4 + (m + 1))
                    else:
                        r = PLE_R0 + KT + m - 4
                        if m == KT - 1:
                            unit_result(L, PLE0 + 9)
                        else:
                            dve.wait_ge(mid_done, L * LAYER_M + (PLE_M0 + 3 + m - 4 + 1))
                        dve.tensor_tensor(sig[:, :], U_BANK[r % 2][:, :], sig[:, :], ALU.mult).then_inc(bank_free[r % 2], 1)
                        dve.wait_ge(bank_free[r % 2], free_before(L, r) + 1)
                    dve.scalar_tensor_tensor(out=z[:, m, :], in0=z[:, m, :], scalar=ALPHA, in1=sig[:, :],
                                             op0=ALU.mult, op1=ALU.add).then_inc(zpre, 1)

            def up(L, j):
                it = L * FT + j * 2
                for c in range(2):
                    for half, buf in ((0, conv_a), (1, conv_b)):
                        n = 2 * c + half
                        ch = bass.ds(j * 2 + (half * FT + c), 1)
                        tap = lambda w: convp[:, bass.ds(L, 1), w, ch].rearrange("p l c -> p (l c)")
                        ps, y = U_BANK[half], buf[c]
                        dve.wait_ge(conv_mid, it * 2 + (n + 1))
                        dve.scalar_tensor_tensor(out=y[:, 1:T], in0=ps[:, 0:T - 1], scalar=tap(0), in1=y[:, 1:T],
                                                 op0=ALU.mult, op1=ALU.add).then_inc(conv_left, 1)
                        dve.wait_ge(conv_left, it * 2 + (n + 1))
                        dve.scalar_tensor_tensor(out=y[:, 0:T - 1], in0=ps[:, 1:T], scalar=tap(2), in1=y[:, 0:T - 1],
                                                 op0=ALU.mult, op1=ALU.add).then_inc(bank_free[half], 1)
                    dve.wait_ge(gelu_done, it + (c + 1))
                    dve.wait_ge(bank_free[1], free_before(L, UP_R0 + 2 * c + 1, j * 2) + 1)
                    dve.tensor_tensor(conv_b[c][:, :], conv_a[c][:, :], conv_b[c][:, :], ALU.mult).then_inc(glu_done, 1)
                    dve.wait_ge(g_hi_s, it + (c + 1))
                    g = bass.ds(j * 2 + c, 1)
                    dve.tensor_tensor(g_lo[:, g, :].rearrange("p s n -> p (s n)"), conv_b[c][:, :],
                                      g_hi[:, g, :].rearrange("p s n -> p (s n)").bitcast(F32), ALU.subtract).then_inc(g_lo_s, 1)

            def residual_down(L):
                done = 0
                for m in range(KT):
                    last = (m + 1) * FT - 1
                    if last % UT == UT - 1:
                        unit_result(L, DOWN0 + last // UT)
                    else:
                        done += 1
                        dve.wait_ge(mid_done, L * LAYER_M + (DOWN_M0 + done))
                    dve.tensor_tensor(z[:, m, :], z[:, m, :], U_BANK[m % 2][:, :], ALU.add).then_inc(bank_free[m % 2], 1)

            def rms(n, which, rs, tiles):
                dve.wait_ge(lstd, n + 1)
                dve.reciprocal(rs[:, 0:P], rs[:, 0:P]).then_inc(lrstd, 1)
                dve.wait_ge(rstd_spread, n + 1)

                def low(k):
                    dve.wait_ge(x_hi, (n + 1) * KT + (k + 1))
                    dve.tensor_tensor(xl[:, k, :], tiles[k % 4][:, :], xh[:, k, :].bitcast(F32), ALU.subtract).then_inc(x_lo, 1)

                for k in range(KT):
                    g = mpar[:, NORM_C + which * KT + k:NORM_C + which * KT + k + 1]
                    dst = out_t[:, k, :] if tiles is None else tiles[k % 4][:, :]
                    if tiles is not None and k >= 4:
                        dve.wait_ge(x_lo, (n + 1) * KT + (k - 3))
                    dve.scalar_tensor_tensor(out=dst, in0=z[:, k, :], scalar=g, in1=S_BANK[0][:, :],
                                             op0=ALU.mult, op1=ALU.mult).then_inc(normed, 1)
                    if tiles is not None and k >= 1:
                        low(k - 1)
                if tiles is not None:
                    low(KT - 1)

            prep_steps = [0]

            def step():
                prep_steps[0] += 1
                return prep, 1

            def settled():
                return prep, prep_steps[0]

            tt, stt, ts = dve.tensor_tensor, dve.scalar_tensor_tensor, dve.tensor_scalar

            def phase_sines(l):
                n = 1 << l
                wc, ws = (powers[:, l, c, :].unsqueeze(2).to_broadcast([P, ST, n]) for c in range(2))
                c0, s0, s1 = phase[:, 0, :, 0:n], phase[:, 1, :, 0:n], phase[:, 1, :, n:2 * n]
                dve.wait_ge(phase_s, l + 1)
                dve.wait_ge(phase_c, l + 1)
                tt(s1, s0, wc, ALU.mult).then_inc(*step())
                tt(phase_td[:, :, 0:n], c0, ws, ALU.mult).then_inc(*step())
                dve.wait_ge(*settled())
                tt(s1, s1, phase_td[:, :, 0:n], ALU.add).then_inc(phase_s, 1)

            def c_powers():
                wide = lambda x: x.unsqueeze(2).to_broadcast([P, ST, 2 * SCH])
                s_cr, s_ci, den = (st[:, i, :] for i in (2, 3, 5))
                dve.reciprocal(den, den).then_inc(*step())
                dve.wait_ge(*settled())
                tt(s_cr, s_cr, den, ALU.mult).then_inc(*step())
                tt(s_ci, s_ci, den, ALU.mult).then_inc(*step())
                dve.wait_ge(*settled())
                cr, ci, ar, ai = (wide(st[:, i, :]) for i in (2, 3, 0, 1))
                c_r, c_i = c_st[:, 0, :, :], c_st[:, 1, :, :]
                t0, t1 = t_c[0][:, :, :], t_c[1][:, :, :]
                dve.wait_ge(mix_in, 16 * MIX_LOADS)
                dve.wait_ge(phase_s, LEVELS + 1)
                r, n = c_pow[:, :, 0, 0, :], c_pow[:, :, 1, 0, :]
                tt(r, c_r, cr, ALU.mult).then_inc(*step())
                tt(t0, c_i, ci, ALU.mult).then_inc(*step())
                tt(n, c_r, ci, ALU.mult).then_inc(*step())
                tt(t1, c_i, cr, ALU.mult).then_inc(*step())
                dve.wait_ge(*settled())
                tt(r, r, t0, ALU.subtract).then_inc(c_ready, 1)
                stt(out=n, in0=n, scalar=-1.0, in1=t1, op0=ALU.mult, op1=ALU.subtract).then_inc(c_ready, 1)
                for k in range(BT):
                    r, n, r2, n2 = (c_pow[:, :, c, i, :] for i in (k, k + 1) for c in (0, 1))
                    dve.wait_ge(c_ready, 2 * k + 2)
                    tt(r2, r, ar, ALU.mult).then_inc(*step())
                    tt(t0, n, ai, ALU.mult).then_inc(*step())
                    tt(n2, n, ar, ALU.mult).then_inc(*step())
                    tt(t1, r, ai, ALU.mult).then_inc(*step())
                    dve.wait_ge(*settled())
                    tt(r2, r2, t0, ALU.add).then_inc(c_ready, 1)
                    tt(n2, n2, t1, ALU.subtract).then_inc(c_ready, 1)

            def state_tiles(q):
                c, s = phase[:, 0, 4 * q:4 * q + 4, :], phase[:, 1, 4 * q:4 * q + 4, :]
                vr, vi = V_BANKS[:, :, 0:NB], V_BANKS[:, :, NB:2 * NB]
                zr, zi, t = states[q][:, 0, :, :], states[q][:, 1, :, :], t_s[:, :, :]
                dve.wait_ge(v_done, q + 1)
                if q == 0:
                    dve.wait_ge(c_ready, 2 * BT + 2)
                    dve.wait_ge(phase_c, LEVELS + 1)
                else:
                    dve.wait_ge(state_re, q)
                tt(zr, vr, c, ALU.mult).then_inc(*step())
                tt(t, vi, s, ALU.mult).then_inc(*step())
                dve.wait_ge(*settled())
                tt(zr, zr, t, ALU.add).then_inc(*step())
                tt(zi, vi, c, ALU.mult).then_inc(*step())
                dve.wait_ge(*settled())
                tt(t, vr, s, ALU.mult).then_inc(v_read, 1)
                dve.wait_ge(v_read, q + 1)
                tt(zi, zi, t, ALU.subtract).then_inc(*step())
                dve.wait_ge(*settled())
                for m in range(4):
                    for x in (zr, zi):
                        dve.tensor_tensor_scan(x[:, m, :], st[:, 4, 4 * q + m:4 * q + m + 1].to_broadcast([P, NB]), x[:, m, :], 0.0,
                                               ALU.mult, ALU.add).then_inc(scanned, 1)
                dve.wait_ge(scanned, 8 * q + 8)
                tt(t, zi, s, ALU.mult).then_inc(im_taken, 1)
                dve.wait_ge(re_taken, 2 * q + 1)
                tt(zr, zr, c, ALU.mult).then_inc(*step())
                dve.wait_ge(*settled())
                dve.wait_ge(im_taken, q + 1)
                tt(zr, zr, t, ALU.subtract).then_inc(state_re, 1)

            def mixer():
                n0 = MIX * 2
                dve.wait_ge(mean_done, n0)
                dve.memset(phase[:, 0, :, 0:1], 1.0).then_inc(phase_c, 1)
                dve.memset(phase[:, 1, :, 0:1], 0.0).then_inc(phase_s, 1)
                for l in range(LEVELS - 1):
                    phase_sines(l)
                rms(n0, 0, rstd_1, xn_1)
                phase_sines(LEVELS - 1)
                c_powers()
                for q in range(SP_T):
                    state_tiles(q)
                Y = (Y_BANK, O_BANK, V_BANKS[:, 0, :], V_BANKS[:, 1, :])
                dve.wait_ge(state_im, SP_T)
                def skip(q):
                    dve.wait_ge(y_done, q + 1)
                    dve.scalar_tensor_tensor(out=yg[:, q, :], in0=u_all[:, SP_T + q, :], scalar=mpar[:, SKIP_C + q:SKIP_C + q + 1],
                                             in1=Y[q][:, :], op0=ALU.mult, op1=ALU.add).then_inc(y_skip, 1)

                def yg_low(q):
                    dve.wait_ge(yg_hi_s, q + 1)
                    dve.tensor_tensor(yg_lo[:, q, :], yg[:, q, :], yg_hi[:, q, :].bitcast(F32), ALU.subtract).then_inc(yg_lo_s, 1)

                skip(0)
                skip(1)
                yg_low(0)
                skip(2)
                yg_low(1)
                yg_low(2)
                skip(3)
                yg_low(3)

                def mix_low(m):
                    dve.wait_ge(mix_hi_s, m + 1)
                    dve.tensor_tensor(mix_lo[:, m, :], u_all[:, m, :], mix_hi[:, m, :].bitcast(F32), ALU.subtract)\
                        .then_inc(mix_lo_s, 1)

                for m in range(SP_T):
                    mix_low(m)
                for m in range(SP_T):
                    dve.wait_ge(bank_free[m % 2], free_before(MIX, GLU_R0 + m) + 1)
                    dve.tensor_tensor(u_all[:, SP_T + m, :], yg[:, m, :], glu_sig[m % 2][:, :], ALU.mult).then_inc(y_ssm, 1)
                for m in range(SP_T, KT):
                    mix_low(m)
                for m in range(KT):
                    unit_result(MIX, MOUT_U0 + m)
                    dve.tensor_tensor(z[:, m, :], z[:, m, :], U_BANK[m % 2][:, :], ALU.add).then_inc(bank_free[m % 2], 1)
                rms(n0 + 1, 1, rstd_2, xn_2)
                with dve.Fori(0, FT // 2) as j:
                    for c in range(2):
                        unit_result(MIX, GU_U0 + 2 * c + 1, j * 4)
                        dve.wait_ge(bank_free[0], free_before(MIX, GU_R0 + 2 * c, j * 2) + 1)
                        dve.tensor_tensor(hidden[c][:, :], U_BANK[1][:, :], silu[c][:, :], ALU.mult).then_inc(bank_free[1], 1)
                        dve.wait_ge(gu_hi, j * 2 + (c + 1))
                        g = bass.ds(j * 2 + c, 1)
                        dve.tensor_tensor(g_lo[:, g, :].rearrange("p s n -> p (s n)"), hidden[c][:, :],
                                          g_hi[:, g, :].rearrange("p s n -> p (s n)").bitcast(F32), ALU.subtract).then_inc(gu_lo, 1)
                done = 0
                for m in range(KT):
                    last = (m + 1) * FT - 1
                    if last % UT == UT - 1:
                        unit_result(MIX, MDOWN_U0 + last // UT)
                    else:
                        done += 1
                        dve.wait_ge(mid_done, MIX * LAYER_M + (MDOWN_M0 + done))
                    dve.tensor_tensor(z[:, m, :], z[:, m, :], U_BANK[m % 2][:, :], ALU.add).then_inc(bank_free[m % 2], 1)
                rms(n0 + 2, 2, rstd_3, None)

            for b in range(2):
                dve.sem_inc(s_free[b], 1)
            dve.sem_inc(ot_read, 2)
            dve.sem_inc(o_norm, 4)
            dve.memset(mean_w[:, :], 1.0 / D).then_inc(consts_set, 1)
            dve.memset(ln_eps[:, :], LN_EPS).then_inc(consts_set, 1)
            dve.memset(gn_eps[:, :], GN_EPS).then_inc(consts_set, 1)
            dve.memset(rms_eps[:, :], RMS_EPS).then_inc(rms_set, 1)
            for k in range(KT):
                dve.wait_ge(x_hi, k + 1)
                dve.tensor_tensor(xl[:, k, :], z[:, k, :], xh[:, k, :].bitcast(F32), ALU.subtract).then_inc(x_lo, 1)
            dve.wait_ge(decay_step, 3)
            flat = decay[:, :, :].rearrange("p d n -> p (d n)")
            dve.tensor_scalar(decay_b[:, :], flat, 0.0, None, ALU.min).then_inc(decay_step, 1)
            dve.wait_ge(decay_step, 4)
            dve.tensor_tensor(flat, decay_b[:, :], decay_a[:, :], ALU.subtract).then_inc(decay_step, 1)
            dve.wait_ge(decay_step, 5)
            dve.wait_ge(mpar_in, 16)
            with dve.Fori(0, DEPTH) as L:
                dve.wait_ge(tables_in, L * 48 + 48)
                stand(dve, dve_passed)
                with dve.Fori(0, 4) as t:
                    attention(L, t)
                split_branch_inputs(L)
                with dve.Fori(0, 2) as i:
                    branches(L, i)
                residual_out(L)
                norm(L, 0)
                ple(L)
                with dve.Fori(0, FT // 2) as j:
                    up(L, j)
                residual_down(L)
                norm(L, 1)
            mixer()


def weight_tiles(w):
    import numpy as np
    k, m = w.shape
    return np.ascontiguousarray(w.reshape(k // P, P, m // P, P).transpose(0, 2, 1, 3))


def layer_stream(inp, i):
    w_in, w_a, w_b, w_o, w_up, w_dn, w_pg, w_pp = (
        weight_tiles(inp[n][i]) for n in
        ("w_in", "w_branch_a", "w_branch_b", "w_out", "w_up", "w_down", "w_ple_gate", "w_ple_proj"))
    col = lambda w, m: [w[k, m] for k in range(w.shape[0])]
    q_na, k_na, v_na, q_r, k_r, v_r, g_r, gate = 0, 4, 8, 12, 16, 20, 28, 36
    out = []
    for t in range(4):
        for m in (q_na + t, k_na + t, v_na + t, q_r + t, k_r + t):
            out += col(w_in, m)
        for k in range(KT):
            out += [w_in[k, v_r + 2 * t], w_in[k, v_r + 2 * t + 1]]
        for m in (g_r + 2 * t, g_r + 2 * t + 1, gate + 3 * t, gate + 3 * t + 1, gate + 3 * t + 2):
            out += col(w_in, m)
    for h in range(2):
        for g in range(2):
            out += col(w_in, gate + 12 + 2 * h + g)
        for w in (w_a, w_b):
            for m in range(4):
                out += col(w, 4 * h + m)
    for m in range(KT):
        out += col(w_o, m)
    for w, ms in ((w_pp, range(4)), (w_pg, range(KT)), (w_pp, range(4, KT))):
        for m in ms:
            out += col(w, m)
    for j in range(FT):
        out += col(w_up, j) + col(w_up, FT + j)
    for m in range(KT):
        out += col(w_dn, m)
    return out


def mixer_stream(inp):
    w_in, w_glu, w_o, w_g, w_up, w_dn = (
        weight_tiles(inp[n + "_2"][0]) for n in ("w_in", "w_glu", "w_out", "w_gate", "w_up", "w_down"))
    col = lambda w, m: [w[k, m] for k in range(w.shape[0])]
    out = []
    for m in range(KT):
        out += col(w_in, (m + SP_T) % KT)
    for m in range(SP_T):
        out += col(w_glu, m)
    for m in range(KT):
        out += col(w_o, m)
    for j in range(FT):
        out += col(w_g, j) + col(w_up, j)
    for m in range(KT):
        out += col(w_dn, m)
    return out


def unit_array(tiles):
    import numpy as np
    w = np.stack(tiles)
    return np.ascontiguousarray(w.reshape(-1, UT, P, P).transpose(0, 2, 1, 3)).reshape(-1, P, UT * P)


def feature_major(v):
    import numpy as np
    return np.ascontiguousarray(np.moveaxis(v.reshape(*v.shape[:-1], -1, P), -1, 0))


def layout(inp):
    import numpy as np
    f32 = np.float32
    a = {}
    tiles = []
    for i in range(DEPTH):
        tiles += layer_stream(inp, i)
    tiles += mixer_stream(inp)
    a["w"] = unit_array(tiles)
    a["x"] = np.ascontiguousarray(inp["x"][0].T.reshape(KT, P, T).transpose(1, 0, 2))
    a["p"] = np.ascontiguousarray(inp["p"][:, 0].transpose(0, 2, 1).reshape(DEPTH, PLE_T, P, T).transpose(0, 2, 1, 3))
    a["lnp"] = feature_major(np.stack([inp["ln1_g"], inp["ln1_b"], inp["ln2_g"], inp["ln2_b"]], 1))
    a["convp"] = feature_major(np.concatenate([inp["conv_w"], inp["conv_b"][:, None]], 1))
    rates = np.stack([inp["ret_decay_f"].reshape(-1), inp["ret_decay_b"].reshape(-1)])
    a["decay"] = np.ascontiguousarray(np.broadcast_to(rates[None], (P, 2, DEPTH * RET_H)))
    rows, cols = np.arange(ROWS), np.arange(16)
    dr = rows[None, :] - rows[:, None] + WIN_ROWS - 1
    dc = 16 * np.arange(3)[None, :, None] - 16 + cols[None, None, :] - cols[:, None, None] + WIN_COLS - 1
    table = np.pad(inp["na_rpb"], ((0, 0), (0, 0), (0, 0), (16, 16)))
    spread = table[:, :, dr[:, None, None, :, None], dc[None, :, :, None, :] + 16]
    a["bias"] = np.ascontiguousarray(spread.reshape(DEPTH, 4, 2, P, 3 * P).transpose(0, 1, 3, 2, 4)).reshape(DEPTH * 4, P, 6 * P)
    a["ident"] = np.eye(P, dtype=f32)
    a["pick"] = np.repeat((np.arange(P)[:, None] == 32 * np.arange(4)).astype(f32)[:, :, None], P, 2)
    half = RET_DK // 2
    inv = f32(10000.0) ** (-np.arange(half, dtype=f32) / f32(half))
    ang = np.arange(T, dtype=f32)[None, :] * inv[:, None]
    c, s = np.cos(ang), np.sin(ang)
    a["rope"] = np.ascontiguousarray(np.stack([np.concatenate([c, c]), np.concatenate([-s, s])], 1).astype(f32))
    a["delta"] = (np.arange(7 * P)[None, :] - 3 * P - np.arange(P)[:, None]).astype(f32)
    masks = np.zeros((P, 3, 3, ROWS, 16), f32)
    for m, j in enumerate((0, 1, CB - 1)):
        q = 16 * j + cols
        first = np.clip(q - WIN_COLS // 2, 0, GRID_W - WIN_COLS)
        key = 16 * (j - 1) + 16 * np.arange(3)[:, None] + cols[None, :]
        ok = (key[None] >= first[:, None, None]) & (key[None] < first[:, None, None] + WIN_COLS)
        neg = np.where(ok, 0.0, -1e30).astype(f32)
        masks[:, m] = np.tile(neg, (ROWS, 1, 1))[:, :, None, :]
    a["masks"] = masks.reshape(P, 3, 3 * P)
    two = SG // ST
    by_channel = lambda v: np.repeat(v.reshape(SP_T, P // SCH, SN), SCH, 1).transpose(1, 0, 2).reshape(P, SP_T * SN)
    by_state = lambda v: v.reshape(ST, two * SN).T
    re, im = inp["lam_re_2"][0], inp["lam_im_2"][0]
    a["lam"] = np.stack([np.concatenate([by_channel(v), by_state(v)], 1) for v in (re, im)], 1)
    log_dt = inp["log_dt_2"][0]
    a["log_dt"] = np.concatenate([np.repeat(log_dt.reshape(SP_T, P // SCH).T, SCH, 0),
                                  np.repeat(log_dt.reshape(ST, two).T, SN, 0)], 1)
    b_cs = np.stack([inp["b_re_2"][0], inp["b_im_2"][0]])
    a["w_b"] = b_cs.reshape(2, SP_T, P // SCH, SN, SCH).transpose(2, 4, 0, 1, 3).reshape(P, 2, SP_T, SN)
    apart = np.zeros((two, SN, 2, ST, two, SCH), f32)
    for h in range(two):
        apart[h, :, :, :, h] = b_cs.reshape(2, ST, two, SN, SCH)[:, :, h].transpose(2, 0, 1, 3)
    a["b_st"] = apart.reshape(P, 2, ST, two * SCH)
    c_cs = np.stack([inp["c_re_2"][0], inp["c_im_2"][0]])
    apart = np.zeros((two, SN, 2, ST, two, SCH), f32)
    for h in range(two):
        apart[h, :, :, :, h] = c_cs.reshape(2, ST, two, SCH, SN)[:, :, h].transpose(3, 0, 1, 2)
    a["c_st"] = apart.reshape(P, 2, ST, two * SCH)
    a["w_pool"] = inp["w_pool_2"][0].transpose(1, 0, 2)
    part = np.arange(P)[:, None]
    counts = [np.broadcast_to((f32(1.0) / np.minimum(np.arange(1, 17), w).astype(f32))[None], (P, 16)) for w in WINDOWS]
    cols = [feature_major(v) for v in (inp["norm_mix_2"][0], inp["norm_ffn_2"][0], inp["norm_final_2"], inp["pool_scale_2"][0],
                                       inp["d_skip_2"][0].reshape(-1), inp["b_glu_2"][0])]
    a["mpar"] = np.concatenate(cols + [(part // SCH % 2 == np.arange(2)).astype(f32),
                                       (part // (2 * SCH) == np.arange(4)).astype(f32)] + counts, 1)
    return {n: np.ascontiguousarray(v) for n, v in a.items()}


def kernel(**inputs):
    import numpy as np
    import concourse.bacc as bacc
    from concourse.bass_utils import run_bass_kernel_spmd

    arrays = layout({n: np.asarray(v) for n, v in inputs.items()})
    nc = bacc.Bacc("TRN2", target_bir_lowering=False, num_devices=1)
    dram = {n: nc.dram_tensor(f"in_{n}", v.shape, F32, kind="ExternalInput").ap() for n, v in arrays.items()}
    out = nc.dram_tensor("out_x", (P, KT, T), F32, kind="ExternalOutput").ap()
    build(nc, dram, out)
    r = run_bass_kernel_spmd(nc, [{f"in_{n}": v for n, v in arrays.items()}], core_ids=[0])
    got = r.results[0]["out_x"]
    return np.ascontiguousarray(got.transpose(1, 0, 2).reshape(D, T).T).reshape(1, T, D)
```
